# Optimizing a Trainium2 kernel written in Bass

```python
import math, functools
import jax, jax.numpy as jnp
from jax import lax
import numpy as np

D_MODEL = 2048
BATCH = 1
SEQ = 256
DEPTH = 1
DEC_BATCH = 8
DEC_SEQ = 4
PAST_LEN = 1024
PAGE_SIZE = 128

MIX_W = D_MODEL
ATT_W = MIX_W // 2
POOL_W = MIX_W - ATT_W
ATT_HEAD_DIM = 128
ATT_HEADS = ATT_W // ATT_HEAD_DIM
POOL_WINDOWS = (2, 4, 8, 16)
POOL_GROUP_W = POOL_W // len(POOL_WINDOWS)
POOL_HIST = max(POOL_WINDOWS) - 1
IN_W = 3 * ATT_W + ATT_HEADS + POOL_W
Q_BLOCK = 128
PEER_HEADS = 8
PEER_NKEYS = 128
PEER_EXPERTS = PEER_NKEYS * PEER_NKEYS
PEER_TOPK = 16
PEER_QDIM = 256
PEER_HALF = PEER_QDIM // 2
PEER_BLOCK = 128
NORM_EPS = 1e-6
NEG_INF = -1e30

kernel_name = 'fox_pool_peer_hybrid_step'

def _rmsnorm(x, g):
    xf = x.astype(jnp.float32)
    y = xf * lax.rsqrt(jnp.mean(xf * xf, axis=-1, keepdims=True) + NORM_EPS)
    return y.astype(x.dtype) * g

def _fox_attend(q, f_q, q_pos, k, v, f_k, k_pos):
    s = jnp.einsum('bqhd,bkhd->bhqk', q, k).astype(jnp.float32) * (ATT_HEAD_DIM ** -0.5)
    s = s + jnp.swapaxes(f_q, 1, 2)[..., :, None] - jnp.swapaxes(f_k, 1, 2)[..., None, :]
    s = jnp.where(k_pos[None, :] <= q_pos[:, None], s, NEG_INF)
    pr = jax.nn.softmax(s, axis=-1)
    return jnp.einsum('bhqk,bkhd->bqhd', pr.astype(v.dtype), v)

def _fox_prompt(q, k, v, logf):
    b, t, h, dh = q.shape
    f = jnp.cumsum(logf, axis=1)
    nb = t // Q_BLOCK
    qb = jnp.swapaxes(q.reshape(b, nb, Q_BLOCK, h, dh), 0, 1)
    fb = jnp.swapaxes(f.reshape(b, nb, Q_BLOCK, h), 0, 1)
    pb = jnp.arange(t).reshape(nb, Q_BLOCK)
    k_pos = jnp.arange(t)
    out = lax.map(lambda a: _fox_attend(a[0], a[1], a[2], k, v, f, k_pos), (qb, fb, pb))
    return jnp.swapaxes(out, 0, 1).reshape(b, t, h * dh)

def _pool_mix(p_ext, pos0, w_pool, pool_scale):
    b, le, c = p_ext.shape
    t = le - POOL_HIST
    pf = p_ext.astype(jnp.float32)
    cs = jnp.concatenate([jnp.zeros((b, 1, c), jnp.float32), jnp.cumsum(pf, axis=1)], axis=1)
    pos = pos0 + jnp.arange(t)
    outs = []
    for g, w in enumerate(POOL_WINDOWS):
        sl = slice(g * POOL_GROUP_W, (g + 1) * POOL_GROUP_W)
        ssum = cs[:, POOL_HIST + 1:POOL_HIST + 1 + t, sl] - cs[:, POOL_HIST + 1 - w:POOL_HIST + 1 - w + t, sl]
        cnt = jnp.minimum(pos + 1, w).astype(jnp.float32)
        outs.append(ssum / cnt[None, :, None])
    pooled = jnp.concatenate(outs, axis=-1) - pf[:, POOL_HIST:]
    pooled = pooled.reshape(b, t, len(POOL_WINDOWS), POOL_GROUP_W)
    y = jnp.einsum('btgc,gcd->btgd', pooled.astype(w_pool.dtype), w_pool).reshape(b, t, c)
    return y * pool_scale

def _prompt_mixer(q, k, v, logf, p, w_pool, pool_scale):
    b = q.shape[0]
    att = _fox_prompt(q, k, v, logf)
    p_ext = jnp.concatenate([jnp.zeros((b, POOL_HIST, POOL_W), p.dtype), p], axis=1)
    pool = _pool_mix(p_ext, 0, w_pool, pool_scale)
    return att, pool, (k, v, logf, p_ext[:, -POOL_HIST:])

def _sample_mixer(q, k, v, logf, p, cache_k, cache_v, cache_logf, state_pool, page_table, w_pool, pool_scale):
    b, t, h, dh = q.shape
    past = page_table.shape[1] * PAGE_SIZE
    k_past = cache_k[page_table].reshape(b, past, h, dh).astype(k.dtype)
    v_past = cache_v[page_table].reshape(b, past, h, dh).astype(v.dtype)
    lf_past = cache_logf[page_table].reshape(b, past, h).astype(jnp.float32)
    k_all = jnp.concatenate([k_past, k], axis=1)
    v_all = jnp.concatenate([v_past, v], axis=1)
    f = jnp.cumsum(jnp.concatenate([lf_past, logf], axis=1), axis=1)
    q_pos = past + jnp.arange(t)
    k_pos = jnp.arange(past + t)
    att = _fox_attend(q, f[:, past:], q_pos, k_all, v_all, f, k_pos).reshape(b, t, h * dh)
    p_ext = jnp.concatenate([state_pool.astype(p.dtype), p], axis=1)
    pool = _pool_mix(p_ext, past, w_pool, pool_scale)
    return att, pool, (k, v, logf, p_ext[:, -POOL_HIST:])

def _peer(h, w_q, sub_keys, u_tab, v_tab):
    n, d = h.shape
    nb = -(-n // PEER_BLOCK)
    hp = jnp.pad(h, ((0, nb * PEER_BLOCK - n), (0, 0))).reshape(nb, PEER_BLOCK, d)

    def block(hb):
        q = (hb @ w_q).reshape(PEER_BLOCK, PEER_HEADS, 2, PEER_HALF)
        s = jnp.einsum('thcd,hckd->thck', q, sub_keys).astype(jnp.float32)
        s1, i1 = lax.top_k(s[:, :, 0], PEER_TOPK)
        s2, i2 = lax.top_k(s[:, :, 1], PEER_TOPK)
        n_cand = PEER_TOPK * PEER_TOPK
        cand = (s1[..., :, None] + s2[..., None, :]).reshape(PEER_BLOCK, PEER_HEADS, n_cand)
        cidx = (i1[..., :, None] * PEER_NKEYS + i2[..., None, :]).reshape(PEER_BLOCK, PEER_HEADS, n_cand)
        top, sel = lax.top_k(cand, PEER_TOPK)
        eidx = jnp.take_along_axis(cidx, sel, axis=-1)
        gate = jax.nn.softmax(top, axis=-1)
        act = jax.nn.gelu(jnp.einsum('td,thkd->thk', hb, u_tab[eidx]).astype(jnp.float32), approximate=False)
        wts = (gate * act).astype(hb.dtype)
        return jnp.einsum('thk,thkd->td', wts, v_tab[eidx])

    return lax.map(block, hp).reshape(nb * PEER_BLOCK, d)[:n]

def _layer(x, c, mixer, w_ada, b_ada, g_pre_mix, g_post_mix, g_pre_ffn, g_post_ffn,
           w_in, b_f, w_out, w_peer_q, peer_subkeys, peer_u, peer_v):
    b, t, d = x.shape
    ada = (jax.nn.silu(c) @ w_ada + b_ada)[:, None, :]
    sh1, sc1, gt1, sh2, sc2, gt2 = jnp.split(ada, 6, axis=-1)
    h = _rmsnorm(x, g_pre_mix) * (1 + sc1) + sh1
    u = h @ w_in
    q = u[..., :ATT_W].reshape(b, t, ATT_HEADS, ATT_HEAD_DIM)
    k = u[..., ATT_W:2 * ATT_W].reshape(b, t, ATT_HEADS, ATT_HEAD_DIM)
    v = u[..., 2 * ATT_W:3 * ATT_W].reshape(b, t, ATT_HEADS, ATT_HEAD_DIM)
    logf = jax.nn.log_sigmoid((u[..., 3 * ATT_W:3 * ATT_W + ATT_HEADS] + b_f).astype(jnp.float32))
    p = u[..., 3 * ATT_W + ATT_HEADS:]
    att, pool, state = mixer(q, k, v, logf, p)
    m = jnp.concatenate([att.astype(x.dtype), pool.astype(x.dtype)], axis=-1) @ w_out
    x = x + gt1 * _rmsnorm(m, g_post_mix)
    h2 = _rmsnorm(x, g_pre_ffn) * (1 + sc2) + sh2
    f = _peer(h2.reshape(b * t, d), w_peer_q, peer_subkeys, peer_u, peer_v).reshape(b, t, d)
    x = x + gt2 * _rmsnorm(f, g_post_ffn)
    return x, state

def setup_inputs(seed: int = 0) -> dict:
    key = jax.random.key(seed)
    ks = jax.random.split(key, 28)
    f32 = jnp.float32
    d = D_MODEL
    n_pages = PAST_LEN // PAGE_SIZE
    n_used = DEC_BATCH * n_pages
    n_pool = n_used + n_used // 4

    def nrm(k, shape, scale=1.0):
        return scale * jax.random.normal(k, shape, f32)

    x_prompt = nrm(ks[0], (BATCH, SEQ, d))
    x_sample = nrm(ks[1], (DEC_BATCH, DEC_SEQ, d))
    c_prompt = nrm(ks[2], (BATCH, d))
    c_sample = nrm(ks[3], (DEC_BATCH, d))
    cache_k = nrm(ks[4], (DEPTH, n_pool, PAGE_SIZE, ATT_HEADS, ATT_HEAD_DIM))
    cache_v = nrm(ks[5], (DEPTH, n_pool, PAGE_SIZE, ATT_HEADS, ATT_HEAD_DIM))
    cache_logf = jax.nn.log_sigmoid(4.0 + nrm(ks[6], (DEPTH, n_pool, PAGE_SIZE, ATT_HEADS)))
    state_pool = nrm(ks[7], (DEPTH, DEC_BATCH, POOL_HIST, POOL_W))
    page_table = jax.random.permutation(ks[8], n_pool)[:n_used].reshape(DEC_BATCH, n_pages).astype(jnp.int32)
    w_ada = nrm(ks[9], (DEPTH, d, 6 * d), 0.5 * d ** -0.5)
    b_ada = nrm(ks[10], (DEPTH, 6 * d), 0.02)
    g_pre_mix = 1.0 + nrm(ks[11], (DEPTH, d), 0.05)
    g_post_mix = 1.0 + nrm(ks[12], (DEPTH, d), 0.05)
    g_pre_ffn = 1.0 + nrm(ks[13], (DEPTH, d), 0.05)
    g_post_ffn = 1.0 + nrm(ks[14], (DEPTH, d), 0.05)
    w_qkv = nrm(ks[15], (DEPTH, d, 3 * ATT_W), d ** -0.5)
    w_fg = nrm(ks[16], (DEPTH, d, ATT_HEADS), 0.5 * d ** -0.5)
    w_pin = nrm(ks[17], (DEPTH, d, POOL_W), d ** -0.5)
    w_in = jnp.concatenate([w_qkv, w_fg, w_pin], axis=-1)
    b_f = jnp.linspace(1.0, 6.0, ATT_HEADS, dtype=f32) + nrm(ks[18], (DEPTH, ATT_HEADS), 0.1)
    w_pool = nrm(ks[19], (DEPTH, len(POOL_WINDOWS), POOL_GROUP_W, POOL_GROUP_W), POOL_GROUP_W ** -0.5)
    pool_scale = 1.0 + nrm(ks[20], (DEPTH, POOL_W), 0.1)
    w_out = nrm(ks[21], (DEPTH, MIX_W, d), MIX_W ** -0.5)
    w_peer_q = nrm(ks[22], (DEPTH, d, PEER_HEADS * PEER_QDIM), d ** -0.5)
    peer_subkeys = nrm(ks[23], (DEPTH, PEER_HEADS, 2, PEER_NKEYS, PEER_HALF), PEER_HALF ** -0.5)
    peer_u = nrm(ks[24], (DEPTH, PEER_EXPERTS, d), d ** -0.5)
    peer_v = nrm(ks[25], (DEPTH, PEER_EXPERTS, d), 1.0)
    return {'x_prompt': x_prompt, 'x_sample': x_sample, 'c_prompt': c_prompt, 'c_sample': c_sample,
            'cache_k': cache_k, 'cache_v': cache_v, 'cache_logf': cache_logf, 'state_pool': state_pool,
            'page_table': page_table, 'w_ada': w_ada, 'b_ada': b_ada,
            'g_pre_mix': g_pre_mix, 'g_post_mix': g_post_mix, 'g_pre_ffn': g_pre_ffn, 'g_post_ffn': g_post_ffn,
            'w_in': w_in, 'b_f': b_f, 'w_pool': w_pool, 'pool_scale': pool_scale, 'w_out': w_out,
            'w_peer_q': w_peer_q, 'peer_subkeys': peer_subkeys, 'peer_u': peer_u, 'peer_v': peer_v}

def reference(x_prompt, x_sample, c_prompt, c_sample, cache_k, cache_v, cache_logf, state_pool,
              page_table, w_ada, b_ada, g_pre_mix, g_post_mix, g_pre_ffn, g_post_ffn,
              w_in, b_f, w_pool, pool_scale, w_out, w_peer_q, peer_subkeys, peer_u, peer_v):
    yp = x_prompt
    ys = x_sample
    kp, vp, lp, pp = [], [], [], []
    ks_, vs_, ls_, ps_ = [], [], [], []
    for l in range(DEPTH):
        shared = (w_ada[l], b_ada[l], g_pre_mix[l], g_post_mix[l], g_pre_ffn[l], g_post_ffn[l],
                  w_in[l], b_f[l], w_out[l], w_peer_q[l], peer_subkeys[l], peer_u[l], peer_v[l])
        pmix = functools.partial(_prompt_mixer, w_pool=w_pool[l], pool_scale=pool_scale[l])
        yp, st_p = _layer(yp, c_prompt, pmix, *shared)
        smix = functools.partial(_sample_mixer, cache_k=cache_k[l], cache_v=cache_v[l],
                                 cache_logf=cache_logf[l], state_pool=state_pool[l],
                                 page_table=page_table, w_pool=w_pool[l], pool_scale=pool_scale[l])
        ys, st_s = _layer(ys, c_sample, smix, *shared)
        kp.append(st_p[0]); vp.append(st_p[1]); lp.append(st_p[2]); pp.append(st_p[3])
        ks_.append(st_s[0]); vs_.append(st_s[1]); ls_.append(st_s[2]); ps_.append(st_s[3])
    k_prompt = jnp.stack(kp)
    v_prompt = jnp.stack(vp)
    logf_prompt = jnp.stack(lp)
    pool_prompt = jnp.stack(pp)
    k_sample = jnp.stack(ks_)
    v_sample = jnp.stack(vs_)
    logf_sample = jnp.stack(ls_)
    pool_sample = jnp.stack(ps_)
    return (yp, ys, k_prompt, v_prompt, logf_prompt, pool_prompt, k_sample, v_sample, logf_sample, pool_sample)


_drawn_inputs = setup_inputs


def setup_inputs(seed=0):
    import zlib

    import numpy as np

    out = dict(_drawn_inputs(seed))
    spreads = {}
    factors = {'g_post_ffn': 3.925}
    for name, (base, spread) in spreads.items():
        noise = np.random.default_rng([zlib.crc32(name.encode()), seed]).standard_normal(out[name].shape)
        drawn = base * np.exp(spread * noise) if base else spread * noise
        out[name] = __import__('jax').numpy.asarray(drawn.astype(out[name].dtype))
    for name, factor in factors.items():
        out[name] = (out[name] * factor).astype(out[name].dtype)
    return out
```

```python
import numpy as np

import concourse.bass as bass
from concourse import mybir

F32 = mybir.dt.float32
U32 = mybir.dt.uint32
I32 = mybir.dt.int32
ALU = mybir.AluOpType
ACT = mybir.ActivationFunctionType
AX_X = mybir.AxisListType.X

P = 128
D = 2048
KC = D // P
NP_TOK, NB, NQ = 256, 8, 4
NS_TOK = NB * NQ
NT = NP_TOK + NS_TOK
NROW = 1 + NB
HEADS, HD = 8, 128
PAGES = 8
POOL_PAGES = 80
HIST = 15
WINDOWS = (2, 4, 8, 16)
SK = 128
TOPK = 16
SLOTS = 8
EPS = 1e-6
NEG = -1e30
LOWEST = -3.0e38

C_ID, C_ONE, C_NTRI, C_NONE, C_MASK, C_SUF = 0, 128, 256, 384, 512, 768
C_NT32, C_MNEW, C_IOTA, C_RC, C_PART, C_END = 896, 928, 960, 976, 1040, 1041
R_C, R_BADA, R_G, R_PS, R_BF, R_WF, R_END = 0, 144, 240, 304, 312, 320, 448

PHASES = [("ada", 12, 16), ("in", 4, 16), ("k", 4, 32), ("v", 4, 32), ("out", 2, 16), ("pq", 2, 16),
          ("u0", 16, 16), ("v0", 16, 16), ("u1", 16, 16), ("v1", 16, 16), ("u2", 4, 16), ("v2", 4, 16)]


def ring_plan():
    plan, used, landed = {}, 0, {True: 0, False: 0}
    for name, rounds, inc in PHASES:
        gather = name[0] in "kuv"
        plan[name] = (used, landed[gather], inc, rounds)
        used += rounds
        landed[gather] += rounds * inc
    return plan


PLAN = ring_plan()


class Order:

    def __init__(self, eng, sem):
        self.eng, self.sem, self.base, self.k = eng, sem, 0, 0

    def __call__(self, ins):
        self.k += 1
        ins.then_inc(self.sem, 1)
        self.eng.wait_ge(self.sem, self.base + self.k)

    def enter(self, i, per):
        self.start, self.per = self.base + self.k, per
        self.base, self.k = self.start + i * per, 0

    def leave(self, count):
        assert self.k == self.per, (self.k, self.per)
        self.base, self.k = self.start + count * self.per, 0


def build(nc, x_t, cst_in, prm_in, w_ada, w_in, w_out, w_pq, cache_k, cache_v, cache_f, pages_bc, pages_col,
          hist_in, sk_in, wpool_in, peer_u, peer_v, y_out, kv_out, lf_out, pool_out):
    sb = nc.alloc_sbuf_tensor
    ring = sb("ring", [P, SLOTS, D], F32)
    xT = sb("xT", [P, KC, NT], F32)
    hT = sb("hT", [P, KC, NT], F32)
    uT = sb("uT", [P, 2 * KC, NT], F32)
    mixT = sb("mixT", [P, KC, NT], F32)
    work = sb("work", [P, 6784], F32)
    vnat = sb("vnat", [P, 3, HEADS * HD], F32)
    cst = sb("cst", [P, C_END], F32)
    prm = sb("prm", [P, R_END], F32)
    adaT = sb("adaT", [P, 6 * KC, NROW], F32)
    mods = sb("mods", [P, 4, KC, NROW], F32)
    rstd = sb("rstd", [P, NT], F32)
    lfs = sb("lfs", [P, 6, 3, 8], F32)
    pg_i = sb("pg_i", [P, 64], I32)
    pg_f = sb("pg_f", [P, 64], F32)
    pg_col = sb("pg_col", [64, 1], I32)
    uidx = sb("uidx", [P, P], U32)
    idxs = sb("idxs", [P, 2 * SLOTS], U32)
    mxs = sb("mxs", [P, 64], F32)
    PS = nc.alloc_psum_tensor("PS", [P, 8, 512], F32)

    ident, ones = cst[:, C_ID:C_ID + P], cst[:, C_ONE:C_ONE + P]
    negtri, mask2 = cst[:, C_NTRI:C_NTRI + P], cst[:, C_MASK:C_MASK + 2 * P]
    suffix = cst[:, C_SUF:C_SUF + P]
    negtri32, masknew = cst[0:32, C_NT32:C_NT32 + 32], cst[0:32, C_MNEW:C_MNEW + 32]
    cT = prm[:, R_C:R_C + KC * NROW].rearrange("p (k n) -> p k n", n=NROW)
    b_ada = prm[:, R_BADA:R_BADA + 6 * KC]
    gains = prm[:, R_G:R_G + 4 * KC].rearrange("p (g k) -> p g k", g=4)
    wf = prm[:, R_WF:R_WF + KC * HEADS].rearrange("p (k h) -> p k h", h=HEADS)
    bf = prm[:, R_BF:R_BF + HEADS]
    A1, G1, A2, G2 = (mods[:, n] for n in range(4))
    SH1, SC1, GT1, SH2, SC2, GT2 = (adaT[:, KC * n:KC * (n + 1)] for n in range(6))

    hF = hT[:, :, :].rearrange("p a b -> p (a b)")
    uF = uT[:, :, :].rearrange("p a b -> p (a b)")
    mF = mixT[:, :, :].rearrange("p a b -> p (a b)")
    NA = 8 * (HIST + NP_TOK)
    NX = NA + 8 * NB * (HIST + NQ)
    assert NX <= 3400

    def ext(flat):
        return (flat[:, 0:NA].rearrange("p (c t) -> p c t", c=8),
                flat[:, NA:NX].rearrange("p (c b t) -> p c b t", c=8, b=NB))

    extA, extB = ext(work[:, :]), ext(hF)
    pT = uT[:, 24:32, :]
    wpool = work[:, 3384:5432].rearrange("p (g c d) -> p g c d", g=4, c=2)
    PT = [work[:, 5432 + 384 * n:5432 + 384 * (n + 1)] for n in range(2)]
    Rsuf = work[:, 6200:6712]
    S_sb = [hF[:, 3400 + 256 * n:3656 + 256 * n] for n in range(2)]
    lfg = mF[0:64, 0:1024]
    lfp = mF[:, 1024:1536].rearrange("p (g h) -> p g h", h=HEADS)
    lfsuf = mF[:, 1536:2048].rearrange("p (g h) -> p g h", h=HEADS)
    pool_st = mF[:, 2048:3128]
    hist = mF[:, 3136:4096].rearrange("p (c b t) -> p c b t", c=8, b=NB)
    Sall = work[:, 0:2048].rearrange("p (b g m) -> p b g m", b=NB, g=PAGES)
    Mx, Snew, Lsum, Rd, newO, Cneg = (hF[:, 256 * n:256 * n + (256 if n < 5 else 8)] for n in range(6))
    diag = hF[:, 1536:1792].rearrange("p (g m) -> p g m", g=2)
    vtmp = hF[:, 1792:1824]
    mT, msq = uF[:, 0:KC * NT], uF[:, KC * NT:2 * KC * NT]
    h2n = uF[:, 0:3 * D].rearrange("p (t n) -> p t n", t=3)
    scr = uF[:, 6144:8192]
    wT, vidx = uF[:, 8192:8192 + NT], uF[:, 8480:8480 + NT].bitcast(U32)
    act, gel, wgt = (uF[:, 8768 + n * P:8896 + n * P] for n in range(3))
    q2T = work[:, 0:KC * NT].rearrange("p (k t) -> p k t", k=KC)
    q2rep = work[:, KC * NT:KC * NT + D].rearrange("p (k t) -> p k t", k=KC)
    skT = vnat[:, :, :].rearrange("p a b -> p (a b)")[:, 0:D].rearrange("p (k n) -> p k n", k=KC)
    fT = mixT
    v16 = hF[:, 0:256].rearrange("p (k n) -> p k n", n=TOPK)
    i16 = hF[:, 256:512].bitcast(U32).rearrange("p (k n) -> p k n", n=TOPK)
    i16f = hF[:, 512:768].rearrange("p (k n) -> p k n", n=TOPK)
    top = hF[:, 768:896].rearrange("p (h n) -> p h n", n=TOPK)
    sel, sela, selb = (hF[:, 896 + n * P:1024 + n * P].bitcast(U32).rearrange("p (h n) -> p h n", n=TOPK)
                       for n in range(3))
    saf, sbf, e1, e2 = (hF[:, 1280 + n * P:1408 + n * P].rearrange("p (h n) -> p h n", n=TOPK) for n in range(4))
    eidx = hF[:, 1792:1920]
    gate = hF[:, 1920:2048].rearrange("p (h n) -> p h n", n=TOPK)
    gsum = hF[:, 2048:2056]
    grec = hF[:, 2056:2064]
    gate2 = hF[:, 2064:2096]

    S = {}

    def sem(name):
        S[name] = nc.alloc_semaphore(name)
        return S[name]

    landed = [sem(f"landed{n}") for n in range(SLOTS)]
    gathered = [sem(f"gathered{n}") for n in range(SLOTS)]
    used = [sem(f"used{n}") for n in range(SLOTS)]
    (x_in, cst_ready, prm_ready, pages_in, hist_ready, wpool_ready, sk_ready, out_done) = map(sem, (
        "x_in", "cst_ready", "prm_ready", "pages_in", "hist_ready", "wpool_ready", "sk_ready", "out_done"))
    dve_own, act_own, pool_own = sem("dve_own"), sem("act_own"), sem("pool_own")
    sq_ready, ssq_ready, var_ready, std_ready = map(sem, ("sq_ready", "ssq_ready", "var_ready", "std_ready"))
    gather_turns = sem("gather_turns")
    silu_ready, ada_done, ada_kept = sem("silu_ready"), sem("ada_done"), sem("ada_kept")
    pgidx_ready, lfg_in, lfpT_done, lfp_kept, suf_done = map(sem, (
        "pgidx_ready", "lfg_in", "lfpT_done", "lfp_kept", "suf_done"))
    h_ready, lf_done, lfabs_ready, lfexp_ready, lfu_ready, lfln_ready, lf_ready = map(sem, (
        "h_ready", "lf_done", "lfabs_ready", "lfexp_ready", "lfu_ready", "lfln_ready", "lf_ready"))
    pmap_done, bank_free = sem("pmap_done"), sem("bank_free")
    kv_sent, pool_sent, pstage_ready = sem("kv_sent"), sem("pool_sent"), sem("pstage_ready")
    q_scaled, vnT_done, vn_kept, pooled_ready = map(sem, ("q_scaled", "vnT_done", "vn_kept", "pooled_ready"))
    s_done, smax_ready, p_exp, p_ready, pT_done, pT_kept, att_done = map(sem, (
        "s_done", "smax_ready", "p_exp", "p_ready", "pT_done", "pT_kept", "att_done"))
    k_free, new_done, mx_ready, mxT_done, diag_ready, mb_done, sub_ready, exp_ready = map(sem, (
        "k_free", "new_done", "mx_ready", "mxT_done", "diag_ready", "mb_done", "sub_ready", "exp_ready"))
    lsum_ready, den_done, newo_done, newo_kept, v_free = map(sem, (
        "lsum_ready", "den_done", "newo_done", "newo_kept", "v_free"))
    x1_ready, h2_ready, h2T_done, h2n_kept = map(sem, ("x1_ready", "h2_ready", "h2T_done", "h2n_kept"))
    sc_done, sc_read, eidx_ready, eT_done, vidx_ready = map(sem, (
        "sc_done", "sc_read", "eidx_ready", "eT_done", "vidx_ready"))
    gsub_ready, gexp_ready = sem("gsub_ready"), sem("gexp_ready")
    uidx_ready, act_ready, gelu_ready, w_ready, wT_done, wT_kept, f_free, y_ready = map(sem, (
        "uidx_ready", "act_ready", "gelu_ready", "w_ready", "wT_done", "wT_kept", "f_free", "y_ready"))

    UNITS = 2 * HEADS
    N_IN, N_ATT, N_POOL, N_OUT, N_PQ, N_END = 0, 32, 40, 48, 64, 80
    TILE_ROWS = (P, P, NS_TOK)
    V_ROUNDS = (16, 16, 4)

    block = nc.Block()
    blk = block.__enter__()

    @blk.sync
    def _(sp):
        sp.dma_start(prm[:, :], prm_in).then_inc(prm_ready, 16)
        sp.dma_start(xT[:, :, :], x_t).then_inc(x_in, 16)
        sp.dma_start(cst[:, :], cst_in).then_inc(cst_ready, 16)

        def stream(phase, src):
            used0, _, _, rounds = PLAN[phase]
            with sp.Fori(0, rounds) as i:
                for r in range(SLOTS):
                    sp.wait_ge(used[r], used0 + i)
                    sp.dma_start(ring[:, r, :], src[i * SLOTS + r]).then_inc(landed[r], 16)

        stream("ada", w_ada)
        sp.dma_start(wpool[:, :, :, :], wpool_in).then_inc(wpool_ready, 16)
        sp.dma_start(hist[:, :, :, :], hist_in).then_inc(hist_ready, 16)
        stream("in", w_in)
        sp.wait_ge(lf_ready, 1)
        sp.dma_start(lf_out[0:2 * P].rearrange("(t p) h -> p t h", p=P), lfs[:, 5, 0:2, :]).then_inc(out_done, 16)
        sp.dma_start(lf_out[2 * P:NT], lfs[0:NS_TOK, 5, 2, :]).then_inc(out_done, 16)
        sp.wait_ge(pstage_ready, 1)
        sp.dma_start(pool_out, pool_st).then_inc(pool_sent, 16)
        sp.wait_ge(bank_free, 4 + 24)
        sp.dma_start(kv_out, uT[:, 8:24, :]).then_inc(kv_sent, 16)
        stream("out", w_out)
        stream("pq", w_pq)
        sp.wait_ge(used[0], PLAN["out"][0] + 1)
        sp.dma_start(skT, sk_in).then_inc(sk_ready, 16)
        sp.wait_ge(y_ready, 1)
        sp.dma_start(y_out, xT[:, :, :]).then_inc(out_done, 16)
        sp.wait_ge(kv_sent, 16)
        sp.wait_ge(pool_sent, 16)
        sp.wait_ge(out_done, 48)

    @blk.gpsimd
    def _(pool):
        own = Order(pool, pool_own)
        pool.dma_start(pg_col[:, :], pages_col).then_inc(pages_in, 16)
        pool.dma_start(pg_i[:, :], pages_bc).then_inc(pages_in, 16)
        pool.wait_ge(pages_in, 32)
        pool.indirect_dma_start(out=lfg, out_offset=None, in_=cache_f,
                                in_offset=bass.IndirectOffsetOnAxis(ap=pg_col[:, 0:1], axis=0)).then_inc(lfg_in, 16)

        def gather_pages(phase, cache):
            used0, _, _, rounds = PLAN[phase]
            with pool.Fori(0, rounds) as i:
                own.enter(i, SLOTS)
                for r in range(SLOTS):
                    pool.wait_ge(used[r], used0 + i)
                    pool.sem_inc(gather_turns, 1)
                    own(nc.gpsimd.tensor_copy(idxs[:, 2 * r:2 * r + 2],
                                              pg_i[:, bass.ds(i * 2 * SLOTS + 2 * r, 2)]))
                    pool.sem_inc(gather_turns, 1)
                    for half in range(2):
                        pool.indirect_dma_start(
                            out=ring[:, r, 1024 * half:1024 * (half + 1)], out_offset=None, in_=cache,
                            in_offset=bass.IndirectOffsetOnAxis(ap=idxs[:, 2 * r + half:2 * r + half + 1], axis=0),
                        ).then_inc(gathered[r], 16)
                own.leave(rounds)

        def gather_experts(phase, index, col0, table):
            used0, _, _, rounds = PLAN[phase]
            with pool.Fori(0, rounds) as i:
                own.enter(i, SLOTS)
                for r in range(SLOTS):
                    pool.wait_ge(used[r], used0 + i)
                    pool.sem_inc(gather_turns, 1)
                    own(nc.gpsimd.tensor_copy(idxs[:, r:r + 1], index[:, bass.ds(i * SLOTS + (col0 + r), 1)]))
                    pool.sem_inc(gather_turns, 1)
                    pool.indirect_dma_start(
                        out=ring[:, r, :], out_offset=None, in_=table,
                        in_offset=bass.IndirectOffsetOnAxis(ap=idxs[:, r:r + 1], axis=0),
                    ).then_inc(gathered[r], 16)
                own.leave(rounds)

        pool.wait_ge(pgidx_ready, 1)
        gather_pages("k", cache_k)
        gather_pages("v", cache_v)
        for t in range(3):
            pool.wait_ge(uidx_ready, t + 1)
            gather_experts(f"u{t}", uidx, 0, peer_u)
            pool.wait_ge(vidx_ready, t + 1)
            gather_experts(f"v{t}", vidx, P * t, peer_v)

    @blk.scalar
    def _(act_eng):
        a = act_eng
        own = Order(a, act_own)
        for _ in range(4):
            a.sem_inc(bank_free, 1)
        a.wait_ge(prm_ready, 16)
        nc.scalar.activation(cT, cT, ACT.Silu).then_inc(silu_ready, 1)
        a.wait_ge(x_in, 16)
        nc.scalar.activation(hT[:, :, :], xT[:, :, :], ACT.Square).then_inc(sq_ready, 1)

        def root(n):
            a.wait_ge(var_ready, n + 1)
            nc.scalar.activation(rstd[:, :], rstd[:, :], ACT.Sqrt).then_inc(std_ready, 1)

        root(0)
        a.wait_ge(lfabs_ready, 1)
        nc.scalar.activation(lfs[:, 1], lfs[:, 1], ACT.Exp).then_inc(lfexp_ready, 1)
        a.wait_ge(lfu_ready, 1)
        nc.scalar.activation(lfs[:, 3], lfs[:, 2], ACT.Ln).then_inc(lfln_ready, 1)

        def evacuate(phase, base, one):
            used0, _, _, rounds = PLAN[phase]
            with a.Fori(0, rounds) as i:
                for r in range(SLOTS):
                    a.wait_ge(used[r], i + (used0 + 1))
                    one(i * SLOTS + r, (base + r) % 4).then_inc(bank_free, 1)

        evacuate("in", N_IN, lambda n, bank: nc.scalar.activation(
            uT[:, bass.ds(n, 1), :], PS[:, bank:bank + 1, 0:NT], ACT.Copy))

        def keep_pT(h):
            a.wait_ge(pT_done, 2 * h + 2)
            if h == 0:
                a.wait_ge(pooled_ready, 1)
            if h >= 2:
                a.wait_ge(att_done, h - 1)
            nc.scalar.activation(PT[h % 2], PS[:, 6 + h % 2, 0:384], ACT.Copy).then_inc(pT_kept, 1)

        def keep_att(h):
            n = N_ATT + h
            a.wait_ge(att_done, h + 1)
            if h == 0:
                a.wait_ge(pool_sent, 16)
            nc.scalar.activation(mixT[:, h, 0:NP_TOK], PS[:, n % 4, 0:NP_TOK], ACT.Copy).then_inc(bank_free, 1)

        for u in range(UNITS + 5):
            if u < UNITS:
                a.wait_ge(smax_ready, u + 1)
                nc.scalar.activation(S_sb[u % 2][:, 0:P * (1 + u % 2)], S_sb[u % 2][:, 0:P * (1 + u % 2)], ACT.Exp,
                                     bias=mxs[:, u:u + 1], accum_out=mxs[:, 16 + u:17 + u]).then_inc(p_exp, 1)
            if u >= 3 and u % 2 and (u - 3) // 2 < HEADS:
                keep_pT((u - 3) // 2)
            if u >= 5 and u % 2 and (u - 5) // 2 < HEADS:
                keep_att((u - 5) // 2)

        for n in range(8):
            a.wait_ge(pmap_done, n + 1)
            nc.scalar.activation(mixT[:, 8 + n, :], PS[:, (N_POOL + n) % 4, 0:NT], ACT.Copy,
                                 scale=prm[:, R_PS + n:R_PS + n + 1]).then_inc(bank_free, 1)

        a.wait_ge(sub_ready, 1)
        nc.scalar.activation(Sall, Sall, ACT.Exp).then_inc(exp_ready, 1)
        nc.scalar.activation(Snew[0:32], Snew[0:32], ACT.Exp).then_inc(exp_ready, 1)

        a.wait_ge(kv_sent, 16)

        def keep_m(n, bank):
            nc.scalar.activation(uT[:, bass.ds(n, 1), :], PS[:, bank:bank + 1, 0:NT], ACT.Copy)
            return nc.scalar.activation(uT[:, bass.ds(n + KC, 1), :], PS[:, bank:bank + 1, 0:NT], ACT.Square)

        evacuate("out", N_OUT, keep_m)
        root(1)
        a.wait_ge(x1_ready, 1)
        nc.scalar.activation(hT[:, :, :], xT[:, :, :], ACT.Square).then_inc(sq_ready, 1)
        root(2)

        def keep_q(n, bank):
            nc.scalar.activation(q2T[:, bass.ds(n, 1), :], PS[:, bank:bank + 1, 0:NT], ACT.Copy)
            return nc.scalar.activation(
                q2rep[:, bass.ds(n, 1), :].rearrange("p o (r t) -> p (o r) t", r=4),
                PS[:, bank:bank + 1, NP_TOK:NT].broadcast_to([P, 4, NS_TOK]), ACT.Copy)

        evacuate("pq", N_PQ, keep_q)

        for _ in range(2):
            a.sem_inc(f_free, 1)
        done = 0
        for t in range(3):
            rows = TILE_ROWS[t]
            a.wait_ge(gsub_ready, t + 1)
            nc.scalar.activation(gate, gate, ACT.Exp).then_inc(gexp_ready, 1)
            a.wait_ge(eT_done, t + 1)
            nc.scalar.activation(vidx[:, P * t:P * t + rows], PS[:, 0, 0:rows], ACT.Copy).then_inc(vidx_ready, 1)
            n = P if t < 2 else NS_TOK
            a.wait_ge(act_ready, t + 1)
            nc.scalar.activation(gel[:, 0:n], act[:, 0:n], ACT.Gelu).then_inc(gelu_ready, 1)
            a.wait_ge(wT_done, t + 1)
            if t < 2:
                nc.scalar.activation(wT[:, P * t:P * t + P], PS[:, 1, 0:P], ACT.Copy).then_inc(wT_kept, 1)
            else:
                for q in range(4):
                    last = nc.scalar.activation(wT[32 * q:32 * q + 32, NP_TOK:NT], PS[0:32, 1, 32 * q:32 * q + 32],
                                                ACT.Copy)
                last.then_inc(wT_kept, 1)
            used0, _, _, rounds = PLAN[f"v{t}"]
            with a.Fori(0, rounds) as i:
                for half in range(2):
                    a.wait_ge(used[4 * half + 3], i + (used0 + 1))
                    nc.scalar.activation(
                        fT[:, :, bass.ds(i * SLOTS + (P * t + 4 * half), 4)].rearrange("p c t -> p t c"),
                        PS[:, 2 + half, 0:4 * KC].rearrange("p (t c) -> p t c", t=4), ACT.Copy).then_inc(f_free, 1)
            done += 2 * rounds
        a.wait_ge(f_free, 2 + done)
        nc.scalar.activation(hT[:, :, :], fT[:, :, :], ACT.Square).then_inc(sq_ready, 1)
        root(3)

    @blk.tensor
    def _(pe):
        mm = nc.tensor.matmul

        def sum_squares(src):
            for k in range(KC):
                last = mm(PS[:, 6, 0:NT], ones, src[:, k, :], start=(k == 0), stop=(k == KC - 1))
            last.then_inc(ssq_ready, 1)

        pe.wait_ge(cst_ready, 16)
        pe.wait_ge(sq_ready, 1)
        sum_squares(hT)

        pe.wait_ge(silu_ready, 1)
        with pe.Fori(0, 6) as i:
            pe.wait_ge(ada_kept, i * 2)
            for n in range(2 * SLOTS):
                r = n % SLOTS
                pe.wait_ge(landed[r], i * 32 + 16 * (n // SLOTS + 1))
                for k in range(KC):
                    last = mm(PS[:, 4 + n // SLOTS, 16 * r:16 * r + NROW], ring[:, r, P * k:P * (k + 1)], cT[:, k, :],
                              start=(k == 0), stop=(k == KC - 1))
                last.then_inc(used[r], 1)

        pe.wait_ge(lfg_in, 16)
        for h in range(HEADS):
            last = nc.tensor.transpose(PS[:, 7, 64 * h:64 * h + 64], lfg[:, P * h:P * h + P], ident[0:64, 0:64])
        last.then_inc(lfpT_done, 1)
        pe.wait_ge(lfp_kept, 1)
        mm(PS[:, 7, :], suffix, lfp, start=True, stop=False)
        mm(PS[:, 7, :], ones, lfsuf, start=False, stop=True).then_inc(suf_done, 1)

        pe.wait_ge(h_ready, 1)
        for t, rows in enumerate(TILE_ROWS):
            for k in range(KC):
                last = mm(PS[0:rows, 6, 8 * t:8 * t + 8], hT[:, k, P * t:P * t + rows], wf[:, k, :],
                          start=(k == 0), stop=(k == KC - 1))
        last.then_inc(lf_done, 1)

        def project(phase, base, src):
            used0, land0, inc, rounds = PLAN[phase]
            with pe.Fori(0, rounds) as i:
                for r in range(SLOTS):
                    pe.wait_ge(bank_free, i * SLOTS + (base + r + 1))
                    pe.wait_ge(landed[r], i * inc + (land0 + inc))
                    for k in range(KC):
                        last = mm(PS[:, (base + r) % 4, 0:NT], ring[:, r, P * k:P * (k + 1)], src[:, k, :],
                                  start=(k == 0), stop=(k == KC - 1))
                    last.then_inc(used[r], 1)

        project("in", N_IN, hT)

        for t, rows in enumerate(TILE_ROWS):
            b0 = (4, 6, 4)[t]
            if t == 0:
                pe.wait_ge(bank_free, 4 + 24)
                pe.wait_ge(q_scaled, 1)
            if t == 2:
                pe.wait_ge(vn_kept, 1)
            for h in range(HEADS):
                last = nc.tensor.transpose(PS[0:rows, b0 + h // 4, P * (h % 4):P * (h % 4) + P],
                                           uT[:, 16 + h, P * t:P * t + rows], ident)
            last.then_inc(vnT_done, 1)

        def scores(u):
            h, qt = u // 2, u % 2
            bank = 4 + u % 2
            mm(PS[:, bank, 0:P * (qt + 1)], uT[:, h, P * qt:P * qt + P], uT[:, 8 + h, 0:P * (qt + 1)],
               start=True, stop=False, skip_group_check=True)
            last = mm(PS[:, bank, 0:P * (qt + 1)], lfs[:, 5, 0, h:h + 1].broadcast_to([P, P]),
                      cst[:, C_NTRI:C_NTRI + P * (qt + 1)], start=False, stop=(qt == 0), skip_group_check=True)
            if qt:
                last = mm(PS[:, bank, P:2 * P], lfs[:, 5, 1, h:h + 1].broadcast_to([P, P]), negtri,
                          start=False, stop=True, skip_group_check=True)
            last.then_inc(s_done, 1)

        def turn_p(u):
            h, qt = u // 2, u % 2
            pe.wait_ge(p_ready, u + 1)
            if qt == 0 and h >= 2:
                pe.wait_ge(pT_kept, h - 1)
            if qt == 0:
                last = nc.tensor.transpose(PS[:, 6 + h % 2, 0:P], S_sb[u % 2][:, 0:P], ident)
            else:
                nc.tensor.transpose(PS[:, 6 + h % 2, P:2 * P], S_sb[u % 2][:, 0:P], ident)
                last = nc.tensor.transpose(PS[:, 6 + h % 2, 2 * P:3 * P], S_sb[u % 2][:, P:2 * P], ident)
            last.then_inc(pT_done, 1)

        def attend(h):
            n = N_ATT + h
            pe.wait_ge(bank_free, n + 1)
            pe.wait_ge(pT_kept, h + 1)
            mm(PS[:, n % 4, 0:2 * P], vnat[:, 0, P * h:P * h + P], PT[h % 2][:, 0:2 * P],
               start=True, stop=False, skip_group_check=True)
            mm(PS[:, n % 4, P:2 * P], vnat[:, 1, P * h:P * h + P], PT[h % 2][:, 2 * P:3 * P],
               start=False, stop=True, skip_group_check=True).then_inc(att_done, 1)

        pe.wait_ge(lf_ready, 1)
        pe.wait_ge(q_scaled, 1)
        pe.wait_ge(vn_kept, 3)
        scores(0)
        scores(1)
        for u in range(UNITS):
            turn_p(u)
            if u + 2 < UNITS:
                scores(u + 2)
            if u % 2 and u >= 3:
                attend((u - 3) // 2)
        attend(HEADS - 1)

        pe.wait_ge(pooled_ready, 1)
        pe.wait_ge(wpool_ready, 16)
        for n in range(8):
            g, dc = n // 2, n % 2
            pe.wait_ge(bank_free, N_POOL + n + 1)
            for c in range(2):
                last = mm(PS[:, (N_POOL + n) % 4, 0:NT], wpool[:, g, c, P * dc:P * dc + P], pT[:, 2 * g + c, :],
                          start=(c == 0), stop=(c == 1))
            last.then_inc(pmap_done, 1)

        used0, land0, inc, rounds = PLAN["k"]
        pe.wait_ge(pT_kept, HEADS)
        with pe.Fori(0, rounds) as i:
            for bb in range(2):
                pe.wait_ge(k_free, i * 2 + (bb + 1))
                for s in range(4):
                    r = 4 * bb + s
                    pe.wait_ge(gathered[r], i * inc + (land0 + inc))
                    for half in range(2):
                        for h in range(HEADS):
                            col = 32 * (2 * s + half) + NQ * h
                            last = mm(PS[:, 6 + bb, col:col + NQ],
                                      ring[:, r, 1024 * half + P * h:1024 * half + P * h + P],
                                      uT[:, h, bass.ds(i * 2 * NQ + (NP_TOK + NQ * bb), NQ)],
                                      start=True, stop=True, skip_group_check=True)
                    last.then_inc(used[r], 1)
        for h in range(HEADS):
            mm(PS[0:32, 4, 0:256].rearrange("p (b h q) -> p b h q", b=NB, q=NQ)[:, :, h, :],
               uT[:, 8 + h, NP_TOK:NT], uT[:, h, NP_TOK:NT], start=True, stop=True, skip_group_check=True)
        mm(PS[0:32, 5, 0:HEADS], negtri32, lfs[0:32, 5, 2, :], start=True, stop=True).then_inc(new_done, 1)
        pe.wait_ge(mx_ready, 1)
        for g in range(2):
            last = nc.tensor.transpose(PS[:, 5, P * g:P * g + P], Mx[:, P * g:P * g + P], ident)
        last.then_inc(mxT_done, 1)
        pe.wait_ge(diag_ready, 1)
        mm(PS[:, 4, 0:256], ones, hF[:, 1536:1792], start=True, stop=True).then_inc(mb_done, 1)
        pe.wait_ge(lsum_ready, 1)
        mm(PS[:, 5, 0:256], ones, Lsum, start=True, stop=True).then_inc(den_done, 1)
        for h in range(HEADS):
            last = mm(PS[:, 4, 0:256].rearrange("p (b h q) -> p b h q", b=NB, q=NQ)[:, :, h, :],
                      vnat[0:32, 2, P * h:P * h + P],
                      Snew[0:32].rearrange("p (b h q) -> p b h q", b=NB, q=NQ)[:, :, h, :],
                      start=True, stop=True, skip_group_check=True)
        last.then_inc(newo_done, 1)
        used0, land0, inc, rounds = PLAN["v"]
        with pe.Fori(0, rounds) as i:
            for bb in range(2):
                pe.wait_ge(v_free, i * 2 + (bb + 1))
                for s in range(4):
                    r = 4 * bb + s
                    pe.wait_ge(gathered[r], i * inc + (land0 + inc))
                    for half in range(2):
                        for h in range(HEADS):
                            last = mm(PS[:, 6 + bb, NQ * h:NQ * h + NQ],
                                      ring[:, r, 1024 * half + P * h:1024 * half + P * h + P],
                                      work[:, bass.ds(i * 512 + (256 * bb + 32 * (2 * s + half) + NQ * h), NQ)],
                                      start=(s == 0 and half == 0 and h == 0),
                                      stop=(s == 3 and half == 1), skip_group_check=True)
                    last.then_inc(used[r], 1)

        pe.wait_ge(bank_free, 4 + N_OUT)
        pe.wait_ge(v_free, 2 + NB)
        project("out", N_OUT, mixT)
        pe.wait_ge(bank_free, 4 + N_PQ)
        sum_squares(uT[:, KC:2 * KC, :])
        pe.wait_ge(sq_ready, 2)
        sum_squares(hT)

        pe.wait_ge(h2_ready, 1)
        for t, rows in enumerate(TILE_ROWS):
            if t:
                pe.wait_ge(h2n_kept, t)
            for k in range(KC):
                last = nc.tensor.transpose(PS[0:rows, 4 + k // 4, P * (k % 4):P * (k % 4) + P],
                                           hT[:, k, P * t:P * t + rows], ident)
            last.then_inc(h2T_done, 1)
        project("pq", N_PQ, hT)

        def key_scores(t):
            pe.wait_ge(h2n_kept, 3)
            if t == 0:
                pe.wait_ge(bank_free, 4 + N_END)
                pe.wait_ge(sk_ready, 16)
            if t:
                pe.wait_ge(sc_read, t)
            for k in range(KC):
                lhs = q2T[:, k, P * t:P * t + P] if t < 2 else q2rep[:, k, :]
                last = mm(PS[:, 4 + k // 4, P * (k % 4):P * (k % 4) + P], lhs, skT[:, k, :], start=True, stop=True)
            last.then_inc(sc_done, 1)

        def turn_experts(t):
            pe.wait_ge(eidx_ready, t + 1)
            rows = TILE_ROWS[t]
            nc.tensor.transpose(PS[:, 0, 0:rows], eidx[0:rows, :], ident[0:rows, 0:rows]).then_inc(eT_done, 1)

        def turn_weights(t):
            pe.wait_ge(w_ready, t + 1)
            if t < 2:
                nc.tensor.transpose(PS[:, 1, 0:P], wgt, ident).then_inc(wT_done, 1)
            else:
                nc.tensor.transpose(PS[0:32, 1, 0:P], wgt[:, 0:32], ident).then_inc(wT_done, 1)

        def weigh(t, before):
            used0, land0, inc, rounds = PLAN[f"v{t}"]
            pe.wait_ge(wT_kept, t + 1)
            with pe.Fori(0, rounds) as i:
                for r in range(SLOTS):
                    if r % 4 == 0:
                        pe.wait_ge(f_free, i * 2 + (before + r // 4 + 1))
                    pe.wait_ge(gathered[r], i * inc + (land0 + inc))
                    for c in range(KC):
                        col = KC * (r % 4) + c
                        last = mm(PS[:, 2 + r // 4, col:col + 1], ring[:, r, P * c:P * c + P],
                                  wT[:, bass.ds(i * SLOTS + (P * t + r), 1)],
                                  start=True, stop=True, skip_group_check=True)
                    last.then_inc(used[r], 1)

        key_scores(0)
        turn_experts(0)
        key_scores(1)
        turn_weights(0)
        weigh(0, 0)
        turn_experts(1)
        key_scores(2)
        turn_weights(1)
        weigh(1, 32)
        turn_experts(2)
        turn_weights(2)
        weigh(2, 64)
        pe.wait_ge(sq_ready, 3)
        sum_squares(hT)

    @blk.vector
    def _(dve):
        own = Order(dve, dve_own)
        v = nc.vector

        def norm(n):
            dve.wait_ge(ssq_ready, n + 1)
            v.tensor_scalar(rstd[:, :], PS[:, 6, 0:NT], 1.0 / D, EPS, ALU.mult, ALU.add).then_inc(var_ready, 1)
            dve.wait_ge(std_ready, n + 1)
            own(v.reciprocal(rstd[:, :], rstd[:, :]))

        def modulate(A, shift):
            for k in range(KC):
                v.tensor_scalar(hT[:, k, 0:NP_TOK], hT[:, k, 0:NP_TOK], A[:, k, 0:1], shift[:, k, 0:1],
                                ALU.mult, ALU.add)
            sample = hT[:, :, NP_TOK:NT].rearrange("p k (b i) -> p k b i", i=NQ)
            own(v.tensor_tensor(sample, sample, A[:, :, 1:NROW].unsqueeze(3).broadcast_to([P, KC, NB, NQ]), ALU.mult))
            return v.tensor_tensor(sample, sample,
                                   shift[:, :, 1:NROW].unsqueeze(3).broadcast_to([P, KC, NB, NQ]), ALU.add)

        def add_gated(src, G):
            for k in range(KC):
                v.scalar_tensor_tensor(xT[:, k, 0:NP_TOK], src[:, k, 0:NP_TOK], G[:, k, 0:1], xT[:, k, 0:NP_TOK],
                                       ALU.mult, ALU.add)
            sample = src[:, :, NP_TOK:NT].rearrange("p k (b i) -> p k b i", i=NQ)
            own(v.tensor_tensor(sample, sample, G[:, :, 1:NROW].unsqueeze(3).broadcast_to([P, KC, NB, NQ]), ALU.mult))
            return v.tensor_tensor(xT[:, :, NP_TOK:NT], xT[:, :, NP_TOK:NT], src[:, :, NP_TOK:NT], ALU.add)

        def over_tokens(a, n=KC):
            return a[:, :].unsqueeze(1).broadcast_to([P, n, NT])

        for _ in range(2):
            dve.sem_inc(k_free, 1)
        own(v.memset(lfs[:, 0], 0.0))
        dve.wait_ge(pages_in, 32)
        own(v.tensor_copy(pg_f[:, :], pg_i[:, :]))
        dve.wait_ge(cst_ready, 16)
        own(v.tensor_scalar(pg_f[:, :], pg_f[:, :], float(P), cst[:, C_PART:C_PART + 1], ALU.mult, ALU.add))
        v.tensor_copy(pg_i[:, :], pg_f[:, :]).then_inc(pgidx_ready, 1)
        norm(0)
        own(v.tensor_tensor(hT[:, :, :], xT[:, :, :], over_tokens(rstd), ALU.mult))

        dve.wait_ge(prm_ready, 16)
        with dve.Fori(0, 6) as i:
            for half in range(2):
                dve.wait_ge(used[7], i * 2 + (half + 1))
                v.tensor_tensor(adaT[:, bass.ds(i * KC + 8 * half, 8), :],
                                PS[:, 4 + half, 0:P].rearrange("p (r n) -> p r n", n=16)[:, :, 0:NROW],
                                b_ada[:, bass.ds(i * KC + 8 * half, 8)].unsqueeze(2).broadcast_to([P, 8, NROW]),
                                ALU.add).then_inc(ada_kept, 1)
        dve.wait_ge(ada_kept, 12)

        def gain(n):
            return gains[:, n, :].unsqueeze(2).broadcast_to([P, KC, NROW])

        v.scalar_tensor_tensor(A1, SC1, 1.0, gain(0), ALU.add, ALU.mult)
        v.tensor_tensor(G1, GT1, gain(1), ALU.mult)
        v.scalar_tensor_tensor(A2, SC2, 1.0, gain(2), ALU.add, ALU.mult)
        own(v.tensor_tensor(G2, GT2, gain(3), ALU.mult))
        modulate(A1, SH1).then_inc(h_ready, 1)

        dve.wait_ge(lfpT_done, 1)
        own(v.tensor_copy(lfp.rearrange("p g h -> p h g"), PS[:, 7, :].rearrange("p (h g) -> p h g", h=HEADS)))
        pages = lfp.rearrange("p (b g) h -> p b g h", b=NB)
        later = lfsuf.rearrange("p (b g) h -> p b g h", b=NB)
        own(v.memset(later[:, :, PAGES - 1, :], 0.0))
        for g in range(PAGES - 2, -1, -1):
            ins = v.tensor_tensor(later[:, :, g, :], later[:, :, g + 1, :], pages[:, :, g + 1, :], ALU.add)
            if g:
                own(ins)
            else:
                ins.then_inc(lfp_kept, 1)
        dve.wait_ge(suf_done, 1)
        v.tensor_copy(Rsuf, PS[:, 7, :])

        dve.wait_ge(lf_done, 1)
        v.tensor_tensor(lfs[:, 0, 0:2, :], PS[:, 6, 0:16].rearrange("p (t h) -> p t h", t=2),
                        bf.unsqueeze(1).broadcast_to([P, 2, HEADS]), ALU.add)
        own(v.tensor_tensor(lfs[0:32, 0, 2, :], PS[0:32, 6, 16:24], bf[0:32], ALU.add))
        v.scalar_tensor_tensor(lfs[:, 1], lfs[:, 0], -1.0, lfs[:, 0], ALU.mult, ALU.min).then_inc(lfabs_ready, 1)
        dve.wait_ge(lfexp_ready, 1)
        own(v.tensor_scalar(lfs[:, 2], lfs[:, 1], 1.0, None, ALU.add))
        own(v.tensor_scalar(lfs[:, 4], lfs[:, 2], -1.0, None, ALU.add))
        own(v.tensor_tensor(lfs[:, 4], lfs[:, 1], lfs[:, 4], ALU.subtract))
        v.tensor_scalar(lfs[:, 5], lfs[:, 0], 0.0, None, ALU.min).then_inc(lfu_ready, 1)
        own(v.reciprocal(lfs[:, 1], lfs[:, 2]))
        own(v.tensor_tensor(lfs[:, 4], lfs[:, 4], lfs[:, 1], ALU.mult))
        dve.wait_ge(lfln_ready, 1)
        own(v.tensor_tensor(lfs[:, 4], lfs[:, 4], lfs[:, 3], ALU.add))
        v.tensor_tensor(lfs[:, 5], lfs[:, 5], lfs[:, 4], ALU.subtract).then_inc(lf_ready, 1)

        dve.wait_ge(bank_free, 4 + 8)
        v.tensor_scalar(uT[:, 0:8, :], uT[:, 0:8, :], float(HD) ** -0.5, None, ALU.mult).then_inc(q_scaled, 1)
        for t, rows in enumerate(TILE_ROWS):
            b0 = (4, 6, 4)[t]
            dve.wait_ge(vnT_done, t + 1)
            v.tensor_copy(vnat[0:rows, t, :].rearrange("p (a b) -> p a b", a=2),
                          PS[0:rows, b0:b0 + 2, :]).then_inc(vn_kept, 1)

        dve.wait_ge(bank_free, 4 + 32)
        dve.wait_ge(used[7], PLAN["k"][0])
        dve.wait_ge(hist_ready, 16)
        (pa, sa), (pb, sbx) = extA, extB
        v.memset(pa[:, :, 0:HIST], 0.0)
        v.tensor_copy(pa[:, :, HIST:], pT[:, :, 0:NP_TOK])
        v.tensor_copy(sa[:, :, :, 0:HIST], hist)
        own(v.tensor_copy(sa[:, :, :, HIST:], pT[:, :, NP_TOK:NT].rearrange("p c (b i) -> p c b i", i=NQ)))
        v.tensor_copy(pool_st[:, 0:8 * HIST].rearrange("p (c t) -> p c t", c=8), pa[:, :, NP_TOK:NP_TOK + HIST])
        own(v.tensor_copy(pool_st[:, 8 * HIST:].rearrange("p (c b t) -> p c b t", c=8, b=NB), sa[:, :, :, NQ:]))
        dve.sem_inc(pstage_ready, 1)
        bufs = [extA, extB]
        for g, w in enumerate(WINDOWS):
            (p0, s0), (p1, s1) = bufs[g % 2], bufs[(g + 1) % 2]
            lo, sh = 2 * g, w // 2
            v.tensor_tensor(p1[:, lo:, w - 1:], p0[:, lo:, w - 1:], p0[:, lo:, w - 1 - sh:HIST + NP_TOK - sh], ALU.add)
            own(v.tensor_tensor(s1[:, lo:, :, w - 1:], s0[:, lo:, :, w - 1:],
                                s0[:, lo:, :, w - 1 - sh:HIST + NQ - sh], ALU.add))
        for g, w in enumerate(WINDOWS):
            pw, sw = bufs[(g + 1) % 2]
            c = slice(2 * g, 2 * g + 2)
            first = pw[:, c, HIST:HIST + 16]
            own(v.tensor_tensor(first, first, cst[:, C_RC + 16 * g:C_RC + 16 * g + 16].unsqueeze(1)
                                .broadcast_to([P, 2, 16]), ALU.mult))
            v.tensor_tensor(pT[:, c, 0:16], first, pT[:, c, 0:16], ALU.subtract)
            v.scalar_tensor_tensor(pT[:, c, 16:NP_TOK], pw[:, c, HIST + 16:], 1.0 / w, pT[:, c, 16:NP_TOK],
                                   ALU.mult, ALU.subtract)
            for k in range(2):
                new = pT[:, 2 * g + k, NP_TOK:NT].rearrange("p (b i) -> p b i", i=NQ)
                last = v.scalar_tensor_tensor(new, sw[:, 2 * g + k, :, HIST:], 1.0 / w, new, ALU.mult, ALU.subtract)
        last.then_inc(pooled_ready, 1)

        def before_exp(u):
            n = P * (1 + u % 2)
            buf = S_sb[u % 2][:, 0:n]
            dve.wait_ge(s_done, u + 1)
            if u >= 2:
                dve.wait_ge(pT_done, u - 1)
            own(v.tensor_tensor(buf, PS[:, 4 + u % 2, 0:n], mask2[:, 2 * P - n:], ALU.add))
            own(v.tensor_reduce(mxs[:, 32 + u:33 + u], buf, AX_X, ALU.max))
            v.tensor_scalar(mxs[:, u:u + 1], mxs[:, 32 + u:33 + u], -1.0, None, ALU.mult).then_inc(smax_ready, 1)

        def after_exp(u):
            n = P * (1 + u % 2)
            buf = S_sb[u % 2][:, 0:n]
            dve.wait_ge(p_exp, u + 1)
            own(v.reciprocal(mxs[:, 48 + u:49 + u], mxs[:, 16 + u:17 + u]))
            v.tensor_scalar(buf, buf, mxs[:, 48 + u:49 + u], None, ALU.mult).then_inc(p_ready, 1)

        before_exp(0)
        before_exp(1)
        for u in range(UNITS):
            after_exp(u)
            if u + 2 < UNITS:
                before_exp(u + 2)

        used0, _, _, rounds = PLAN["k"]
        with dve.Fori(0, rounds) as i:
            for bb in range(2):
                dve.wait_ge(used[4 * bb + 3], i + (used0 + 1))
                v.tensor_tensor(
                    work[:, bass.ds(i * 512 + 256 * bb, 256)].rearrange("p (m q) -> p m q", q=NQ),
                    PS[:, 6 + bb, 0:256].rearrange("p (m q) -> p m q", q=NQ),
                    work[:, bass.ds(i * 128 + (6200 + 64 * bb), 64)].unsqueeze(2).broadcast_to([P, 64, NQ]),
                    ALU.add).then_inc(k_free, 1)
        dve.wait_ge(new_done, 1)
        own(v.tensor_copy(Cneg[0:32], PS[0:32, 5, 0:HEADS]))
        new4 = Snew[0:32].rearrange("p (b h q) -> p b h q", b=NB, q=NQ)
        own(v.tensor_tensor(new4, PS[0:32, 4, 0:256].rearrange("p (b h q) -> p b h q", b=NB, q=NQ),
                            Cneg[0:32].unsqueeze(1).unsqueeze(3).broadcast_to([32, NB, HEADS, NQ]), ALU.add))
        own(v.tensor_tensor(new4, new4, masknew.rearrange("p (b q) -> p b q", q=NQ).unsqueeze(2)
                            .broadcast_to([32, NB, HEADS, NQ]), ALU.add))
        dve.wait_ge(k_free, 2 + NB)
        for b in range(NB):
            last = v.tensor_reduce(Mx[:, 32 * b:32 * b + 32], Sall[:, b].rearrange("p g m -> p m g"), AX_X, ALU.max)
        own(last)
        v.tensor_tensor(Mx[0:32], Mx[0:32], Snew[0:32], ALU.max).then_inc(mx_ready, 1)
        dve.wait_ge(mxT_done, 1)
        own(v.tensor_reduce(mxs[:, 0:2], PS[:, 5, 0:256].rearrange("p (g m) -> p g m", g=2), AX_X, ALU.max))
        v.tensor_scalar(diag[:, 0], ident, mxs[:, 0:1], None, ALU.mult)
        v.tensor_scalar(diag[:, 1], ident, mxs[:, 1:2], None, ALU.mult).then_inc(diag_ready, 1)
        dve.wait_ge(mb_done, 1)
        v.tensor_tensor(Snew[0:32], Snew[0:32], PS[0:32, 4, 0:256], ALU.subtract)
        v.tensor_tensor(Sall, Sall, PS[:, 4, 0:256].rearrange("p (b m) -> p b m", b=NB).unsqueeze(2)
                        .broadcast_to([P, NB, PAGES, 32]), ALU.subtract).then_inc(sub_ready, 1)
        dve.wait_ge(exp_ready, 2)
        for b in range(NB):
            last = v.tensor_reduce(Lsum[:, 32 * b:32 * b + 32], Sall[:, b].rearrange("p g m -> p m g"), AX_X, ALU.add)
        own(last)
        v.tensor_tensor(Lsum[0:32], Lsum[0:32], Snew[0:32], ALU.add).then_inc(lsum_ready, 1)
        dve.wait_ge(den_done, 1)
        v.reciprocal(Rd, PS[:, 5, 0:256])
        dve.wait_ge(newo_done, 1)
        own(v.tensor_copy(newO, PS[:, 4, 0:256]))
        for _ in range(2):
            dve.sem_inc(v_free, 1)
        used0, _, _, rounds = PLAN["v"]
        with dve.Fori(0, rounds) as i:
            own.enter(i, 2)
            for bb in range(2):
                dve.wait_ge(used[4 * bb + 3], i + (used0 + 1))
                dve.wait_ge(v_free, i * 2 + (2 + bb))
                own(v.tensor_tensor(vtmp, PS[:, 6 + bb, 0:32], hF[:, bass.ds(i * 64 + (1024 + 32 * bb), 32)],
                                    ALU.add))
                v.tensor_tensor(mixT[:, 0:8, bass.ds(i * 8 + (NP_TOK + 4 * bb), 4)],
                                vtmp.rearrange("p (h q) -> p h q", q=NQ),
                                hF[:, bass.ds(i * 64 + (768 + 32 * bb), 32)].rearrange("p (h q) -> p h q", q=NQ),
                                ALU.mult).then_inc(v_free, 1)
            own.leave(rounds)

        norm(1)
        m3 = uT[:, 0:KC, :]
        own(v.tensor_tensor(m3, m3, over_tokens(rstd), ALU.mult))
        add_gated(m3, G1).then_inc(x1_ready, 1)
        dve.wait_ge(x1_ready, 1)
        norm(2)
        own(v.tensor_tensor(hT[:, :, :], xT[:, :, :], over_tokens(rstd), ALU.mult))
        modulate(A2, SH2).then_inc(h2_ready, 1)
        for t, rows in enumerate(TILE_ROWS):
            dve.wait_ge(h2T_done, t + 1)
            for q in range(P // rows):
                last = v.tensor_copy(h2n[rows * q:rows * (q + 1), t, :].rearrange("p (a b) -> p a b", a=4),
                                     PS[0:rows, 4:8, :])
            last.then_inc(h2n_kept, 1)

        def choose(t):
            dve.wait_ge(sc_done, t + 1)
            sc = PS[:, 4:8, :].rearrange("p a (k n) -> p (a k) n", n=SK)
            cut = scr.rearrange("p (k n) -> p k n", n=SK)
            for k in range(KC):
                last = v.max(v16[:, k, 0:8], sc[:, k, :])
            own(last)
            for k in range(KC):
                v.max_index(i16[:, k, 0:8], v16[:, k, 0:8], sc[:, k, :])
                last = v.match_replace(cut[:, k, :], v16[:, k, 0:8], sc[:, k, :], LOWEST)
            own(last)
            dve.sem_inc(sc_read, 1)
            for k in range(KC):
                last = v.max(v16[:, k, 8:16], cut[:, k, :])
            own(last)
            for k in range(KC):
                last = v.max_index(i16[:, k, 8:16], v16[:, k, 8:16], cut[:, k, :])
            own(last)
            v.tensor_copy(i16f, i16)
            cand = scr.rearrange("p (h a b) -> p h a b", h=HEADS, a=TOPK)
            vals = v16.rearrange("p (h c) n -> p h c n", c=2)
            own(v.tensor_tensor(cand, vals[:, :, 0, :].unsqueeze(3).broadcast_to([P, HEADS, TOPK, TOPK]),
                                vals[:, :, 1, :].unsqueeze(2).broadcast_to([P, HEADS, TOPK, TOPK]), ALU.add))
            cnd = scr.rearrange("p (h n) -> p h n", h=HEADS)
            for h in range(HEADS):
                last = v.max(top[:, h, 0:8], cnd[:, h, :])
            own(last)
            for h in range(HEADS):
                last = v.max_index(sel[:, h, 0:8], top[:, h, 0:8], cnd[:, h, :])
            own(last)
            for h in range(HEADS):
                last = v.match_replace(cnd[:, h, :], top[:, h, 0:8], cnd[:, h, :], LOWEST)
            own(last)
            for h in range(HEADS):
                last = v.max(top[:, h, 8:16], cnd[:, h, :])
            own(last)
            for h in range(HEADS):
                last = v.max_index(sel[:, h, 8:16], top[:, h, 8:16], cnd[:, h, :])
            own(last)
            v.tensor_scalar(sela, sel, 4, None, ALU.logical_shift_right)
            own(v.tensor_scalar(selb, sel, 15, None, ALU.bitwise_and))
            v.tensor_copy(saf, sela)
            own(v.tensor_copy(sbf, selb))
            iota = cst[:, C_IOTA:C_IOTA + TOPK].unsqueeze(1).broadcast_to([P, P, TOPK])
            hit = scr.rearrange("p (m j) -> p m j", j=TOPK)
            hit4 = scr.rearrange("p (h m j) -> p h m j", h=HEADS, j=TOPK)
            keys = i16f.rearrange("p (h c) n -> p h c n", c=2)
            for c, (which, dst) in enumerate(((saf, e1), (sbf, e2))):
                own(v.tensor_tensor(hit, which.rearrange("p h n -> p (h n)").unsqueeze(2)
                                    .broadcast_to([P, P, TOPK]), iota, ALU.is_equal))
                own(v.tensor_tensor(hit4, hit4, keys[:, :, c, :].unsqueeze(2)
                                    .broadcast_to([P, HEADS, TOPK, TOPK]), ALU.mult))
                own(v.tensor_reduce(dst.rearrange("p h n -> p (h n)"), hit, AX_X, ALU.add))
            if t:
                dve.wait_ge(eT_done, t)
            own(v.scalar_tensor_tensor(eidx, e1.rearrange("p h n -> p (h n)"), float(SK),
                                       e2.rearrange("p h n -> p (h n)"), ALU.mult, ALU.add))
            dve.sem_inc(eidx_ready, 1)
            if t < 2:
                v.tensor_copy(uidx[:, :], eidx).then_inc(uidx_ready, 1)
            else:
                for q in range(4):
                    rows = slice(32 * q, 32 * q + 32)
                    last = v.tensor_copy(uidx[rows, 0:32], eidx[rows, 32 * q:32 * q + 32])
                last.then_inc(uidx_ready, 1)
            own(v.tensor_tensor(gate, top, top[:, :, 0:1].broadcast_to([P, HEADS, TOPK]), ALU.subtract))

        def gates(t):
            dve.wait_ge(gexp_ready, t + 1)
            own(v.tensor_reduce(gsum, gate, AX_X, ALU.add))
            own(v.reciprocal(grec, gsum))
            own(v.tensor_tensor(gate, gate, grec.unsqueeze(2).broadcast_to([P, HEADS, TOPK]), ALU.mult))
            if t == 2:
                flat = gate.rearrange("p h n -> p (h n)")
                for q in range(4):
                    rows = slice(32 * q, 32 * q + 32)
                    last = v.tensor_copy(gate2[rows, :], flat[rows, 32 * q:32 * q + 32])
                own(last)

        for t in range(3):
            choose(t)
            dve.sem_inc(gsub_ready, 1)
            used0, land0, inc, rounds = PLAN[f"u{t}"]
            with dve.Fori(0, rounds) as i:
                for r in range(SLOTS):
                    dve.wait_ge(gathered[r], i * inc + (land0 + inc))
                    v.scalar_tensor_tensor(ring[:, r, :], ring[:, r, :], 1.0, h2n[:, t, :], ALU.mult, ALU.mult,
                                           accum_out=act[:, bass.ds(i * SLOTS + r, 1)]).then_inc(used[r], 1)
            dve.wait_ge(used[7], used0 + rounds)
            dve.sem_inc(act_ready, 1)
            gates(t)
            dve.wait_ge(gelu_ready, t + 1)
            n = P if t < 2 else NS_TOK
            if t:
                dve.wait_ge(wT_done, t)
            v.tensor_tensor(wgt[:, 0:n], gate.rearrange("p h n -> p (h n)") if t < 2 else gate2, gel[:, 0:n],
                            ALU.mult).then_inc(w_ready, 1)

        norm(3)
        own(v.tensor_tensor(fT[:, :, :], fT[:, :, :], over_tokens(rstd), ALU.mult))
        add_gated(fT, G2).then_inc(y_ready, 1)

    block.__exit__(None, None, None)


def constants():
    c = np.zeros((P, C_END), np.float32)
    i = np.arange(P)
    c[:, C_ID:C_ID + P] = np.eye(P)
    c[:, C_ONE:C_ONE + P] = 1.0
    c[:, C_NTRI:C_NTRI + P] = -(i[:, None] <= i[None, :]).astype(np.float32)
    c[:, C_NONE:C_NONE + P] = -1.0
    c[:, C_MASK + P:C_MASK + 2 * P] = np.where(i[None, :] > i[:, None], NEG, 0.0)
    c[:, C_SUF:C_SUF + P] = i[:, None] > i[None, :]
    j = np.arange(NS_TOK)
    same = (j[:, None] // NQ) == (j[None, :] // NQ)
    c[0:NS_TOK, C_NT32:C_NT32 + NS_TOK] = -(same & (j[:, None] <= j[None, :])).astype(np.float32)
    c[0:NS_TOK, C_MNEW:C_MNEW + NS_TOK] = np.where(same & (j[:, None] <= j[None, :]), 0.0, NEG)
    c[:, C_IOTA:C_IOTA + TOPK] = np.arange(TOPK)
    for g, w in enumerate(WINDOWS):
        c[:, C_RC + 16 * g:C_RC + 16 * g + 16] = 1.0 / np.minimum(np.arange(16) + 1, w)
    c[:, C_PART] = i
    return c


def kernel(x_prompt, x_sample, c_prompt, c_sample, cache_k, cache_v, cache_logf, state_pool, page_table,
           w_ada, b_ada, g_pre_mix, g_post_mix, g_pre_ffn, g_post_ffn, w_in, b_f, w_pool, pool_scale,
           w_out, w_peer_q, peer_subkeys, peer_u, peer_v):
    from concourse import bacc
    from concourse.bass_utils import run_bass_kernel_spmd

    def arr(a):
        return np.ascontiguousarray(np.asarray(a))

    def cols(a):
        return arr(a).reshape(-1, P, a.shape[1]).transpose(1, 0, 2)

    def tiles(w):
        w = arr(w)
        return arr(w.reshape(KC, P, -1, P).transpose(2, 1, 0, 3).reshape(-1, P, D))

    x = np.concatenate([arr(x_prompt)[0], arr(x_sample).reshape(NS_TOK, D)])
    c = np.concatenate([arr(c_prompt), arr(c_sample)])
    w_i = arr(w_in)[0]
    att_w = HEADS * HD
    per_feature = [arr(b_ada)[0].reshape(6 * KC, P).T] + [
        arr(g)[0].reshape(KC, P).T for g in (g_pre_mix, g_post_mix, g_pre_ffn, g_post_ffn)]
    prm = np.concatenate(
        [cols(c.T).reshape(P, -1)] + per_feature + [
            arr(pool_scale)[0].reshape(8, P).T,
            np.broadcast_to(arr(b_f)[0][None, :], (P, HEADS)),
            cols(w_i[:, 3 * att_w:3 * att_w + HEADS]).reshape(P, -1)], axis=1)
    w_main = np.concatenate([w_i[:, :3 * att_w], w_i[:, 3 * att_w + HEADS:]], axis=1)
    pages = arr(page_table).astype(np.int32).reshape(-1)
    arrays = {
        "x_t": arr(cols(x.T)),
        "cst_in": constants(),
        "prm_in": arr(prm),
        "w_ada": tiles(arr(w_ada)[0]),
        "w_in": tiles(w_main),
        "w_out": tiles(arr(w_out)[0]),
        "w_pq": tiles(arr(w_peer_q)[0]),
        "cache_k": arr(arr(cache_k)[0].transpose(0, 3, 2, 1).reshape(POOL_PAGES * P, HEADS * P)),
        "cache_v": arr(cache_v)[0].reshape(POOL_PAGES * P, HEADS * HD),
        "cache_f": arr(arr(cache_logf)[0].transpose(0, 2, 1).reshape(POOL_PAGES, HEADS * P)),
        "pages_bc": arr(np.broadcast_to(pages[None, :], (P, 64))),
        "pages_col": arr(pages[:, None]),
        "hist_in": arr(arr(state_pool)[0].reshape(NB, HIST, 8, P).transpose(3, 2, 0, 1)),
        "sk_in": arr(arr(peer_subkeys)[0].reshape(KC, SK, P).transpose(2, 0, 1)),
        "wpool_in": arr(arr(w_pool)[0].reshape(4, 2, P, 256).transpose(2, 0, 1, 3)),
        "peer_u": arr(peer_u)[0],
        "peer_v": arr(peer_v)[0],
    }
    outs = {"y_out": (P, KC, NT), "kv_out": (P, 16, NT), "lf_out": (NT, HEADS),
            "pool_out": (P, 8 * HIST * (1 + NB))}
    nc = bacc.Bacc("TRN2", target_bir_lowering=False, num_devices=1)
    args = {n: nc.dram_tensor(n, a.shape, mybir.dt.from_np(a.dtype), kind="ExternalInput").ap()
            for n, a in arrays.items()}
    args.update({n: nc.dram_tensor(n, s, F32, kind="ExternalOutput").ap() for n, s in outs.items()})
    build(nc, **args)
    r = run_bass_kernel_spmd(nc, [arrays], core_ids=[0]).results[0]
    y = r["y_out"].transpose(2, 1, 0).reshape(NT, D)
    kv = r["kv_out"].transpose(2, 1, 0)
    k, v = kv[:, 0:HEADS], kv[:, HEADS:]
    pool = r["pool_out"]
    pool_p = pool[:, :8 * HIST].reshape(P, 8, HIST).transpose(2, 1, 0).reshape(1, 1, HIST, 1024)
    pool_s = pool[:, 8 * HIST:].reshape(P, 8, NB, HIST).transpose(2, 3, 1, 0).reshape(1, NB, HIST, 1024)
    lf = r["lf_out"]
    return (y[:NP_TOK].reshape(1, NP_TOK, D), y[NP_TOK:].reshape(NB, NQ, D),
            k[:NP_TOK].reshape(1, 1, NP_TOK, HEADS, HD), v[:NP_TOK].reshape(1, 1, NP_TOK, HEADS, HD),
            lf[:NP_TOK].reshape(1, 1, NP_TOK, HEADS), pool_p,
            k[NP_TOK:].reshape(1, NB, NQ, HEADS, HD), v[NP_TOK:].reshape(1, NB, NQ, HEADS, HD),
            lf[NP_TOK:].reshape(1, NB, NQ, HEADS), pool_s)
```

```python
import numpy as np

import concourse.bass as bass
from concourse import mybir

F32 = mybir.dt.float32
U32 = mybir.dt.uint32
I32 = mybir.dt.int32
ALU = mybir.AluOpType
ACT = mybir.ActivationFunctionType
AX_X = mybir.AxisListType.X

P = 128
D = 2048
KC = D // P
NP_TOK, NB, NQ = 256, 8, 4
NS_TOK = NB * NQ
NT = NP_TOK + NS_TOK
NROW = 1 + NB
HEADS, HD = 8, 128
PAGES = 8
POOL_PAGES = 80
HIST = 15
WINDOWS = (2, 4, 8, 16)
SK = 128
TOPK = 16
SLOTS = 8
EPS = 1e-6
NEG = -1e30
LOWEST = -3.0e38

C_ID, C_ONE, C_NTRI, C_NONE, C_MASK, C_SUF = 0, 128, 256, 384, 512, 768
C_NT32, C_MNEW, C_IOTA, C_RC, C_PART, C_FOLD, C_END = 896, 928, 992, 1008, 1072, 1073, 1105
R_C, R_BADA, R_G, R_PS, R_BF, R_WF, R_END = 0, 144, 240, 304, 312, 320, 448

PHASES = [("ada01", 4, "AAAAAAAA"), ("q", 2, "WAWAWAWA"), ("kv0", 4, "WKKWKKWA"), ("kv1", 4, "WKKWKKWA"),
          ("ada4", 2, "AAAAAAAA"), ("v", 4, "VVVVVVVV"), ("out", 4, "OAOAOAOA"), ("pq", 2, "QQQQQQQQ"),
          ("ada5", 2, "AAAAAAAA"), ("u0", 16, "UUUUUUUU"), ("x0", 16, "XXXXXXXX"), ("u1", 16, "UUUUUUUU"),
          ("x1", 16, "XXXXXXXX"), ("u2", 4, "UUUUUUUU"), ("x2", 4, "XXXXXXXX")]


class Phase:

    def __init__(self, rounds, kinds, used0, loads, gathers):
        self.rounds, self.kinds, self.used0 = rounds, kinds, used0
        self.gathers = [k in "KVUX" for k in kinds]
        self.inc = [32 if k in "KV" else 16 for k in kinds]
        self.base = [(gathers if g else loads)[r] for r, g in enumerate(self.gathers)]


def ring_plan():
    plan, used, loads, gathers = {}, 1, [0] * SLOTS, [0] * SLOTS
    for name, rounds, kinds in PHASES:
        ph = plan[name] = Phase(rounds, kinds, used, loads, gathers)
        for r in range(SLOTS):
            (gathers if ph.gathers[r] else loads)[r] += rounds * ph.inc[r]
        used += rounds
    return plan


PLAN = ring_plan()


class Order:

    def __init__(self, eng, sem):
        self.eng, self.sem, self.base, self.k = eng, sem, 0, 0

    def __call__(self, ins):
        self.k += 1
        ins.then_inc(self.sem, 1)
        self.eng.wait_ge(self.sem, self.base + self.k)

    def enter(self, i, per):
        self.start, self.per = self.base + self.k, per
        self.base, self.k = self.start + i * per, 0

    def leave(self, count):
        assert self.k == self.per, (self.k, self.per)
        self.base, self.k = self.start + count * self.per, 0


def build(nc, x_t, cst_in, prm_in, w_ada, w_in, w_out, w_pq, cache_k, cache_v, cache_f, pages_bc, pages_col,
          hist_in, sk_in, wpool_in, peer_u, peer_v, y_out, kv_out, lf_out, pool_out):
    sb = nc.alloc_sbuf_tensor
    ring = sb("ring", [P, SLOTS, D], F32)
    xT = sb("xT", [P, KC, NT], F32)
    hT = sb("hT", [P, KC, NT], F32)
    uT = sb("uT", [P, 2 * KC, NT], F32)
    mixT = sb("mixT", [P, KC, NT], F32)
    work = sb("work", [P, 6656], F32)
    vnat = sb("vnat", [P, 3, HEADS * HD], F32)
    cst = sb("cst", [P, C_END], F32)
    prm = sb("prm", [P, R_END], F32)
    adaT = sb("adaT", [P, 6 * KC, NROW], F32)
    ada_nat = sb("ada_nat", [P, 512], F32)
    rstd = sb("rstd", [P, NT], F32)
    lfs = sb("lfs", [P, 6, 3, 8], F32)
    pg_i = sb("pg_i", [P, 64], I32)
    pg_col = sb("pg_col", [64, 1], I32)
    uidx = sb("uidx", [P, 2, P], U32)
    idxs = sb("idxs", [P, 2 * SLOTS], U32)
    mxs = sb("mxs", [P, 80], F32)
    cstage = sb("cstage", [P, 4, NROW], F32)
    PS = nc.alloc_psum_tensor("PS", [P, 8, 512], F32)
    psum_flat = PS[:, :, :].rearrange("p a b -> p (a b)")

    ident, ones = cst[:, C_ID:C_ID + P], cst[:, C_ONE:C_ONE + P]
    negtri, mask2 = cst[:, C_NTRI:C_NTRI + P], cst[:, C_MASK:C_MASK + 2 * P]
    suffix, fold = cst[:, C_SUF:C_SUF + P], cst[:, C_FOLD:C_FOLD + NS_TOK]
    negtri32 = cst[0:NS_TOK, C_NT32:C_NT32 + NS_TOK]
    masknew = cst[:, C_MNEW:C_MNEW + 64].rearrange("p (g j) -> p g j", g=2)
    cT = prm[:, R_C:R_C + KC * NROW].rearrange("p (k n) -> p k n", n=NROW)
    b_ada = prm[:, R_BADA:R_BADA + 6 * KC]
    gains = prm[:, R_G:R_G + 4 * KC].rearrange("p (g k) -> p g k", g=4)
    wf = prm[:, R_WF:R_WF + KC * HEADS].rearrange("p (k h) -> p k h", h=HEADS)
    bf = prm[:, R_BF:R_BF + HEADS]
    SH1, A1, G1, SH2, A2, G2 = (adaT[:, KC * n:KC * (n + 1)] for n in range(6))

    hF = hT[:, :, :].rearrange("p a b -> p (a b)")
    uF = uT[:, :, :].rearrange("p a b -> p (a b)")
    mF = mixT[:, :, :].rearrange("p a b -> p (a b)")
    vF = vnat[:, :, :].rearrange("p a b -> p (a b)")
    NA = 8 * (HIST + NP_TOK)
    NX = NA + 8 * NB * (HIST + NQ)
    assert NX <= 3384

    def ext(flat):
        return (flat[:, 0:NA].rearrange("p (c t) -> p c t", c=8),
                flat[:, NA:NX].rearrange("p (c b t) -> p c b t", c=8, b=NB))

    extA, extB = ext(work[:, :]), ext(hF)
    pT = uT[:, 24:32, :]
    lfg = mF[0:64, 0:1024]
    lfp = mF[:, 1024:1536].rearrange("p (g h) -> p g h", h=HEADS)
    lfsuf = mF[:, 1536:2048].rearrange("p (g h) -> p g h", h=HEADS)
    bias = mF[:, 0:2048].rearrange("p (g n m) -> p g n m", g=2, n=PAGES)
    pool_st = mF[:, 2304:3384]
    hist = mF[:, 3384:4344].rearrange("p (c b t) -> p c b t", c=8, b=NB)
    S_sb = [hF[:, 3400 + 256 * n:3656 + 256 * n] for n in range(2)]
    PT = [work[:, 5432 + 384 * n:5432 + 384 * (n + 1)] for n in range(2)]
    qz = work[:, 0:2048].rearrange("p (h b m) -> p h b m", b=NB, h=HEADS)
    Pnat = work[:, 3384:5432].rearrange("p (g n) -> p g n", g=2)
    Snew = work[:, 6200:6264].rearrange("p (g j) -> p g j", g=2)
    PnT = work[0:32, 6264:6520].rearrange("p (g m) -> p g m", g=2)
    lfrows = work[0:NS_TOK, 6520:6648]
    PTs = uF[:, 0:2048].rearrange("p (g n m) -> p g n m", g=2, n=PAGES)
    Og = uF[:, 2304:4352].rearrange("p (g n) -> p g n", g=2)
    wpool = uF[:, 4608:6656].rearrange("p (g c d) -> p g c d", g=4, c=2)
    h2n = uF[:, 0:3 * D].rearrange("p (t n) -> p t n", t=3)
    scr = uF[:, 6144:8192]
    act, gel, wgt = (uF[:, 8192 + n * P:8320 + n * P] for n in range(3))
    q2T = work[:, 0:KC * NT].rearrange("p (k t) -> p k t", k=KC)
    q2rep = work[:, KC * NT:KC * NT + D].rearrange("p (k t) -> p k t", k=KC)
    skT = vF[:, 0:D].rearrange("p (k n) -> p k n", k=KC)
    fT = mixT
    v16 = hF[:, 0:256].rearrange("p (k n) -> p k n", n=TOPK)
    i16 = hF[:, 256:512].bitcast(U32).rearrange("p (k n) -> p k n", n=TOPK)
    i16f = hF[:, 512:768].rearrange("p (k n) -> p k n", n=TOPK)
    top = hF[:, 768:896].rearrange("p (h n) -> p h n", n=TOPK)
    sel, sela, selb = (hF[:, 896 + n * P:1024 + n * P].bitcast(U32).rearrange("p (h n) -> p h n", n=TOPK)
                       for n in range(3))
    saf, sbf, e1, e2 = (hF[:, 1280 + n * P:1408 + n * P].rearrange("p (h n) -> p h n", n=TOPK) for n in range(4))
    eidx = hF[:, 1792:1920]
    gate = hF[:, 1920:2048].rearrange("p (h n) -> p h n", n=TOPK)
    gsum = hF[:, 2048:2056]
    grec = hF[:, 2056:2064]
    gate2 = hF[:, 2064:2096]
    fsq = hF[:, 2304:4352]

    def sem(name):
        return nc.alloc_semaphore(name)

    landed = [sem(f"landed{n}") for n in range(SLOTS)]
    gathered = [sem(f"gathered{n}") for n in range(SLOTS)]
    used = [sem(f"used{n}") for n in range(SLOTS)]
    emptied = [sem(f"emptied{n}") for n in range(7)]
    (x_in, cst_ready, prm_ready, pages_in, hist_ready, wpool_ready, sk_ready, out_done) = map(sem, (
        "x_in", "cst_ready", "prm_ready", "pages_in", "hist_ready", "wpool_ready", "sk_ready", "out_done"))
    dve_own, pool_own, gather_turns = sem("dve_own"), sem("pool_own"), sem("gather_turns")
    sq_ready, ssq_done, var_ready, std_ready = map(sem, ("sq_ready", "ssq_done", "var_ready", "std_ready"))
    biasT_done, bias_kept, k_kept = sem("biasT_done"), sem("bias_kept"), sem("k_kept")
    ada_summed, cstage_ready = sem("ada_summed"), sem("cstage_ready")
    silu_ready, adanat_kept, adaT_done, ada_kept = map(sem, ("silu_ready", "adanat_kept", "adaT_done", "ada_kept"))
    pgidx_ready, lfg_in, lfpT_done, lfp_kept, suf_done, suf_kept = map(sem, (
        "pgidx_ready", "lfg_in", "lfpT_done", "lfp_kept", "suf_done", "suf_kept"))
    h_ready, lf_done, lfabs_ready, lfexp_ready, lfu_ready, lfln_ready, lf_ready = map(sem, (
        "h_ready", "lf_done", "lfabs_ready", "lfexp_ready", "lfu_ready", "lfln_ready", "lf_ready"))
    kv_sent, pool_sent, pstage_ready = sem("kv_sent"), sem("pool_sent"), sem("pstage_ready")
    qz_ready, new_done, newmax_ready, negmax_ready, exp_ready = map(sem, (
        "qz_ready", "new_done", "newmax_ready", "negmax_ready", "exp_ready"))
    vnT_done, vn_kept, pooled_ready, pmap_done = map(sem, ("vnT_done", "vn_kept", "pooled_ready", "pmap_done"))
    s_done, smax_ready, p_exp, p_ready, pT_done, pT_kept, att_done, att_kept = map(sem, (
        "s_done", "smax_ready", "p_exp", "p_ready", "pT_done", "pT_kept", "att_done", "att_kept"))
    psT_done, psT_kept, den_ready, og_kept, oT_done, oT_kept = map(sem, (
        "psT_done", "psT_kept", "den_ready", "og_kept", "oT_done", "oT_kept"))
    x1_ready, h2_ready, h2T_done, h2n_kept = map(sem, ("x1_ready", "h2_ready", "h2T_done", "h2n_kept"))
    sc_done, sc_read, gsub_ready, gexp_ready = map(sem, ("sc_done", "sc_read", "gsub_ready", "gexp_ready"))
    uidx_ready, act_ready, gelu_ready, f_ready, fT_done, fT_kept, y_ready = map(sem, (
        "uidx_ready", "act_ready", "gelu_ready", "f_ready", "fT_done", "fT_kept", "y_ready"))

    UNITS = 2 * HEADS
    TILE_ROWS = (P, P, NS_TOK)
    TILE_COLS = [(0, P), (P, 2 * P), (2 * P, NT)]

    def arrived(eng, ph, r, i):
        eng.wait_ge((gathered if ph.gathers[r] else landed)[r], i * ph.inc[r] + (ph.base[r] + ph.inc[r]))

    block = nc.Block()
    blk = block.__enter__()

    @blk.sync
    def _(sp):
        for r in range(SLOTS):
            sp.sem_inc(used[r], 1)
        sp.dma_start(prm[:, :], prm_in).then_inc(prm_ready, 16)
        sp.dma_start(xT[:, :, :], x_t).then_inc(x_in, 16)
        sp.dma_start(cst[:, :], cst_in).then_inc(cst_ready, 16)

        def stream(phase, tile_of):
            ph = PLAN[phase]
            with sp.Fori(0, ph.rounds) as i:
                for r in range(SLOTS):
                    if not ph.gathers[r]:
                        kind = ph.kinds[r]
                        sp.wait_ge(used[r], i + ph.used0)
                        sp.dma_start(ring[:, r, :], tile_of(kind, ph.kinds[:r].count(kind), i)).then_inc(landed[r], 16)

        stream("ada01", lambda kind, n, i: w_ada[i * SLOTS + n])
        sp.dma_start(hist[:, :, :, :], hist_in).then_inc(hist_ready, 16)
        stream("q", lambda kind, n, i: w_in[i * 4 + n] if kind == "W" else w_ada[i * 4 + (2 * KC + n)])
        sp.wait_ge(lf_ready, 1)
        sp.dma_start(lf_out[0:2 * P].rearrange("(t p) h -> p t h", p=P), lfs[:, 5, 0:2, :]).then_inc(out_done, 16)
        sp.dma_start(lf_out[2 * P:NT], lfs[0:NS_TOK, 5, 2, :]).then_inc(out_done, 16)
        for g in range(2):
            stream(f"kv{g}", lambda kind, n, i: w_in[i * 3 + (8 + 12 * g + n)] if kind == "W"
                   else w_ada[i + (2 * KC + 8 + 4 * g)])
        stream("ada4", lambda kind, n, i: w_ada[i * SLOTS + (4 * KC + n)])
        for b in range(3):
            sp.wait_ge(emptied[b], 1 + 2 + 8)
        sp.dma_start(kv_out, uT[:, 8:24, :]).then_inc(kv_sent, 16)
        sp.wait_ge(vnT_done, 3)
        sp.wait_ge(kv_sent, 16)
        sp.dma_start(wpool[:, :, :, :], wpool_in).then_inc(wpool_ready, 16)
        sp.wait_ge(pstage_ready, 1)
        sp.dma_start(pool_out, pool_st).then_inc(pool_sent, 16)
        stream("out", lambda kind, n, i: w_out[i * 4 + n] if kind == "O" else w_ada[i * 4 + (3 * KC + n)])
        sp.wait_ge(used[0], PLAN["out"].used0 + 1)
        sp.dma_start(skT, sk_in).then_inc(sk_ready, 16)
        stream("pq", lambda kind, n, i: w_pq[i * SLOTS + n])
        stream("ada5", lambda kind, n, i: w_ada[i * SLOTS + (5 * KC + n)])
        for t, (c0, c1) in enumerate(TILE_COLS):
            sp.wait_ge(y_ready, t + 1)
            sp.dma_start(y_out[:, :, c0:c1], xT[:, :, c0:c1]).then_inc(out_done, 16)
        sp.wait_ge(kv_sent, 16)
        sp.wait_ge(pool_sent, 16)
        sp.wait_ge(out_done, 5 * 16)

    @blk.gpsimd
    def _(pool):
        own = Order(pool, pool_own)
        pool.dma_start(pg_col[:, :], pages_col).then_inc(pages_in, 16)
        pool.dma_start(pg_i[:, :], pages_bc).then_inc(pages_in, 16)
        pool.wait_ge(pages_in, 32)
        pool.indirect_dma_start(out=lfg, out_offset=None, in_=cache_f,
                                in_offset=bass.IndirectOffsetOnAxis(ap=pg_col[:, 0:1], axis=0)).then_inc(lfg_in, 16)

        def gather(phase, index, col0, table, per):
            ph = PLAN[phase]
            mine = [r for r in range(SLOTS) if ph.gathers[r]]
            width = D // per
            with pool.Fori(0, ph.rounds) as i:
                own.enter(i, len(mine))
                for n, r in enumerate(mine):
                    pool.wait_ge(used[r], i + ph.used0)
                    pool.sem_inc(gather_turns, 1)
                    own(nc.gpsimd.tensor_copy(idxs[:, per * r:per * (r + 1)],
                                              index[:, bass.ds(i * (per * len(mine)) + (col0 + per * n), per)]))
                    pool.sem_inc(gather_turns, 1)
                    for m in range(per):
                        pool.indirect_dma_start(
                            out=ring[:, r, width * m:width * (m + 1)], out_offset=None, in_=table,
                            in_offset=bass.IndirectOffsetOnAxis(ap=idxs[:, per * r + m:per * r + m + 1], axis=0),
                        ).then_inc(gathered[r], 16)
                own.leave(ph.rounds)

        pool.wait_ge(pgidx_ready, 1)
        gather("kv0", pg_i, 0, cache_k, 2)
        gather("kv1", pg_i, 32, cache_k, 2)
        gather("v", pg_i, 0, cache_v, 2)
        for t in range(3):
            pool.wait_ge(uidx_ready, t + 1)
            gather(f"u{t}", uidx[:, t % 2, :], 0, peer_u, 1)
            gather(f"x{t}", uidx[:, t % 2, :], 0, peer_v, 1)

    @blk.scalar
    def _(a):
        fn = nc.scalar.activation
        for b in range(7):
            a.sem_inc(emptied[b], 1)
        a.wait_ge(prm_ready, 16)
        fn(cT, cT, ACT.Silu).then_inc(silu_ready, 1)
        a.wait_ge(x_in, 16)
        fn(hT[:, :, :], xT[:, :, :], ACT.Square).then_inc(sq_ready, 1)

        def root(n, c0=0, c1=NT):
            a.wait_ge(var_ready, n + 1)
            fn(rstd[:, c0:c1], rstd[:, c0:c1], ACT.Sqrt).then_inc(std_ready, 1)

        def keep_adanat(count, bank=7):
            a.wait_ge(ada_summed, count)
            fn(ada_nat[:, :], PS[:, bank, :], ACT.Copy).then_inc(adanat_kept, 1)

        root(0)
        with a.Fori(0, 2) as i:
            keep_adanat(i + 1)
        a.wait_ge(lfabs_ready, 1)
        fn(lfs[:, 1], lfs[:, 1], ACT.Exp).then_inc(lfexp_ready, 1)
        a.wait_ge(lfu_ready, 1)
        fn(lfs[:, 3], lfs[:, 2], ACT.Ln).then_inc(lfln_ready, 1)

        def evacuate(phase, kind, chunk0, banks, one):
            ph = PLAN[phase]
            slots = [r for r in range(SLOTS) if ph.kinds[r] == kind]
            with a.Fori(0, ph.rounds) as i:
                for n, r in enumerate(slots):
                    a.wait_ge(used[r], i + (ph.used0 + 1))
                    bank = n % banks
                    one(i * len(slots) + (chunk0 + n), bank).then_inc(emptied[bank], 1)

        def keep_u(n, bank):
            return fn(uT[:, bass.ds(n, 1), :], PS[:, bank:bank + 1, 0:NT], ACT.Copy)

        evacuate("q", "W", 0, 4, keep_u)
        for g in range(2):
            evacuate(f"kv{g}", "W", 8 + 12 * g, 3, keep_u)
            a.wait_ge(negmax_ready, g + 1)
            fn(Pnat[:, g, :], Pnat[:, g, :], ACT.Exp, bias=mxs[:, 64 + g:65 + g],
               accum_out=mxs[:, 66 + g:67 + g]).then_inc(exp_ready, 1)
            fn(Snew[:, g, :], Snew[:, g, :], ACT.Exp, bias=mxs[:, 64 + g:65 + g],
               accum_out=mxs[:, 68 + g:69 + g]).then_inc(exp_ready, 1)
        keep_adanat(3)
        a.wait_ge(vnT_done, 2)
        fn(vnat[:, 1, :].rearrange("p (a b) -> p a b", a=2), PS[:, 0:2, :], ACT.Copy).then_inc(vn_kept, 1)

        def keep_pT(h):
            a.wait_ge(pT_done, 2 * h + 2)
            if h >= 2:
                a.wait_ge(att_done, h - 1)
            fn(PT[h % 2], PS[:, 2 + h % 2, 0:384], ACT.Copy).then_inc(pT_kept, 1)

        def keep_att(h):
            a.wait_ge(att_done, h + 1)
            fn(mixT[:, h, 0:NP_TOK], PS[:, 4 + h % 2, 0:NP_TOK], ACT.Copy).then_inc(att_kept, 1)

        for u in range(UNITS + 5):
            if u < UNITS:
                a.wait_ge(smax_ready, u + 1)
                fn(S_sb[u % 2][:, 0:P * (1 + u % 2)], S_sb[u % 2][:, 0:P * (1 + u % 2)], ACT.Exp,
                   bias=mxs[:, u:u + 1], accum_out=mxs[:, 16 + u:17 + u]).then_inc(p_exp, 1)
            if u >= 3 and u % 2 and (u - 3) // 2 < HEADS:
                keep_pT((u - 3) // 2)
            if u >= 5 and u % 2 and (u - 5) // 2 < HEADS:
                keep_att((u - 5) // 2)
        keep_adanat(4)

        for g in range(2):
            a.wait_ge(psT_done, g + 1)
            b0 = (4, 2)[g]
            fn(PTs[:, g].rearrange("p (a b) m -> p a (b m)", a=2), PS[:, b0:b0 + 2, :], ACT.Copy)
            fn(PnT[:, g, :], PS[0:32, g, 0:P], ACT.Copy).then_inc(psT_kept, 1)

        a.wait_ge(pool_sent, 16)
        for n in range(8):
            a.wait_ge(pmap_done, n + 1)
            fn(mixT[:, 8 + n, :], PS[:, 4 + n % 3, 0:NT], ACT.Copy,
               scale=prm[:, R_PS + n:R_PS + n + 1]).then_inc(emptied[4 + n % 3], 1)
        a.wait_ge(den_ready, 1)
        for g in range(2):
            a.wait_ge(used[7], PLAN["v"].used0 + 2 * (g + 1))
            fn(Og[:, g, :].rearrange("p (a b) -> p a b", a=2), PS[:, 2 * g:2 * g + 2, :], ACT.Copy,
               scale=mxs[:, 72 + g:73 + g]).then_inc(og_kept, 1)

        def keep_m(n, bank):
            keep_u(n, bank)
            return fn(uT[:, bass.ds(n + KC, 1), :], PS[:, bank:bank + 1, 0:NT], ACT.Square)

        evacuate("out", "O", 0, 4, keep_m)
        keep_adanat(5)
        root(1)
        a.wait_ge(x1_ready, 1)
        fn(hT[:, :, :], xT[:, :, :], ACT.Square).then_inc(sq_ready, 1)
        root(2)

        def keep_q(n, bank):
            fn(q2T[:, bass.ds(n, 1), :], PS[:, bank:bank + 1, 0:NT], ACT.Copy)
            return fn(q2rep[:, bass.ds(n, 1), :].rearrange("p o (r t) -> p (o r) t", r=4),
                      PS[:, bank:bank + 1, NP_TOK:NT].broadcast_to([P, 4, NS_TOK]), ACT.Copy)

        evacuate("pq", "Q", 0, 4, keep_q)
        keep_adanat(6, bank=3)

        def exp_gates(t):
            a.wait_ge(gsub_ready, t + 1)
            fn(gate, gate, ACT.Exp).then_inc(gexp_ready, 1)

        exp_gates(0)
        for t, (c0, c1) in enumerate(TILE_COLS):
            n = P if t < 2 else NS_TOK
            a.wait_ge(act_ready, t + 1)
            fn(gel[:, 0:n], act[:, 0:n], ACT.Gelu).then_inc(gelu_ready, 1)
            if t < 2:
                exp_gates(t + 1)
            n = c1 - c0
            src = psum_flat[:, 0:KC * n].rearrange("p (k m) -> p k m", k=KC)
            a.wait_ge(fT_done, t + 1)
            fn(fT[:, :, c0:c1], src, ACT.Copy)
            if t:
                a.wait_ge(ssq_done, 3 + t)
            fn(fsq[:, 0:KC * n].rearrange("p (k m) -> p k m", k=KC), src, ACT.Square).then_inc(fT_kept, 1)
            root(3 + t, c0, c1)

    @blk.tensor
    def _(pe):
        mm = nc.tensor.matmul
        fills = [0] * 7

        def sum_squares(src, n=NT, bank=6):
            for k in range(KC):
                last = mm(PS[:, bank, 0:n], ones, src(k), start=(k == 0), stop=(k == KC - 1))
            last.then_inc(ssq_done, 1)

        def ada_edge(opening, bank=7):
            for j in range(4):
                last = mm(PS[32 * j:32 * j + NROW, bank, :], mask2[:, 0:NROW], cst[:, 0:512],
                          start=opening, stop=not opening, skip_group_check=True)
            if not opening:
                last.then_inc(ada_summed, 1)

        def ada_tile(ph, r, i, c_rows, bank=7):
            arrived(pe, ph, r, i)
            for j in range(4):
                last = mm(PS[32 * j:32 * j + NROW, bank, :], c_rows, ring[:, r, 512 * j:512 * (j + 1)],
                          start=False, stop=False, skip_group_check=True)
            last.then_inc(used[r], 1)

        def turn_ada(count, bank=7):
            pe.wait_ge(adanat_kept, count)
            for c in range(4):
                last = nc.tensor.transpose(PS[:, bank, P * c:P * c + P], ada_nat[:, P * c:P * c + P], ident)
            last.then_inc(adaT_done, 1)

        pe.wait_ge(cst_ready, 16)
        pe.wait_ge(sq_ready, 1)
        sum_squares(lambda k: hT[:, k, :])

        pe.wait_ge(lfg_in, 16)
        for h in range(HEADS):
            last = nc.tensor.transpose(PS[:, 5, 64 * h:64 * h + 64], lfg[:, P * h:P * h + P], ident[0:64, 0:64])
        last.then_inc(lfpT_done, 1)
        pe.wait_ge(lfp_kept, 1)
        mm(PS[:, 5, :], suffix, lfp, start=True, stop=False)
        mm(PS[:, 5, :], ones, lfsuf, start=False, stop=True).then_inc(suf_done, 1)
        pe.wait_ge(suf_kept, 1)
        for g in range(2):
            for n in range(PAGES):
                last = nc.tensor.transpose(PS[:, (0, 2)[g] + n // 4, P * (n % 4):P * (n % 4) + P],
                                           bias[:, g, n, :], ident)
        last.then_inc(biasT_done, 1)

        pe.wait_ge(silu_ready, 1)
        pe.wait_ge(bias_kept, 1)
        ph = PLAN["ada01"]
        with pe.Fori(0, 2) as i:
            pe.wait_ge(ada_kept, i + 1)
            ada_edge(True)
            for k in range(KC):
                ada_tile(ph, k % SLOTS, i * 2 + k // SLOTS, cT[:, k, :])
            ada_edge(False)
            turn_ada(i + 1)

        pe.wait_ge(h_ready, 1)
        for t, rows in enumerate(TILE_ROWS):
            for k in range(KC):
                last = mm(PS[0:rows, 6, 8 * t:8 * t + 8], hT[:, k, P * t:P * t + rows], wf[:, k, :],
                          start=(k == 0), stop=(k == KC - 1))
        last.then_inc(lf_done, 1)

        def chunk(ph, r, i, bank, fill, src):
            pe.wait_ge(emptied[bank], fill)
            arrived(pe, ph, r, i)
            for k in range(KC):
                last = mm(PS[:, bank, 0:NT], ring[:, r, P * k:P * (k + 1)], src[:, k, :],
                          start=(k == 0), stop=(k == KC - 1))
            last.then_inc(used[r], 1)

        def four_and_four(phase, src, staged):
            ph = PLAN[phase]
            with pe.Fori(0, ph.rounds) as i:
                pe.wait_ge(cstage_ready, i + (staged + 1))
                for r in range(SLOTS):
                    if r % 2 == 0:
                        chunk(ph, r, i, r // 2, i + (fills[r // 2] + 1), src)
                    else:
                        ada_tile(ph, r, i, cstage[:, r // 2, :])
            for b in range(4):
                fills[b] += ph.rounds

        def k_slots(ph, g, i, pair, r):
            for m in (r, r + 1):
                arrived(pe, ph, m, i)
            for h in range(HEADS):
                for b in range(4):
                    at = P * h + 1024 * (b % 2)
                    last = mm(PS[32 * b:32 * b + 32, 4 + pair, 0:P], qz[:, h, 4 * g + b, :],
                              ring[:, r + b // 2, at:at + P],
                              start=(h == 0), stop=(h == HEADS - 1), skip_group_check=True)
                    if h == HEADS - 1 and b % 2:
                        last.then_inc(used[r + b // 2], 1)

        pe.wait_ge(ada_kept, 3)
        ada_edge(True)
        four_and_four("q", hT, 0)
        pe.wait_ge(qz_ready, 1)

        for g in range(2):
            ph = PLAN[f"kv{g}"]
            with pe.Fori(0, ph.rounds) as i:
                pe.wait_ge(cstage_ready, i + (2 + 4 * g + 1))
                pe.wait_ge(k_kept, i + (4 * g + 1))
                chunk(ph, 0, i, 0, i + (fills[0] + 1), hT)
                k_slots(ph, g, i, 0, 1)
                chunk(ph, 3, i, 1, i + (fills[1] + 1), hT)
                k_slots(ph, g, i, 1, 4)
                chunk(ph, 6, i, 2, i + (fills[2] + 1), hT)
                ada_tile(ph, 7, i, cstage[:, 0, :])
            for b in range(3):
                fills[b] += ph.rounds
            if g == 0:
                for b in range(3):
                    pe.wait_ge(emptied[b], fills[b] + 1)
                for gg in range(2):
                    for h in range(HEADS):
                        mm(PS[:, 3, 448 + 32 * gg:480 + 32 * gg], qz[:, h, 4 * gg:4 * gg + 4, :].rearrange("p b m -> p (b m)"),
                           uT[:, 8 + h, NP_TOK:NT], start=(h == 0), stop=False, skip_group_check=True)
                    last = mm(PS[:, 3, 448 + 32 * gg:480 + 32 * gg], lfrows, negtri32, start=False, stop=True, skip_group_check=True)
                last.then_inc(new_done, 1)
        ada_edge(False)
        turn_ada(3)

        for b in range(3):
            pe.wait_ge(emptied[b], fills[b] + 1)
        pe.wait_ge(k_kept, 9)
        pe.wait_ge(newmax_ready, 1)
        for t, rows in enumerate(TILE_ROWS):
            b0 = (4, 0, 2)[t]
            for h in range(HEADS):
                last = nc.tensor.transpose(PS[0:rows, b0 + h // 4, P * (h % 4):P * (h % 4) + P],
                                           uT[:, 16 + h, P * t:P * t + rows], ident)
            last.then_inc(vnT_done, 1)

        def scores(u):
            h, qt = u // 2, u % 2
            mm(PS[:, qt, 0:P * (qt + 1)], uT[:, h, P * qt:P * qt + P], uT[:, 8 + h, 0:P * (qt + 1)],
               start=True, stop=False, skip_group_check=True)
            last = mm(PS[:, qt, 0:P * (qt + 1)], lfs[:, 5, 0, h:h + 1].broadcast_to([P, P]),
                      cst[:, C_NTRI:C_NTRI + P * (qt + 1)], start=False, stop=(qt == 0), skip_group_check=True)
            if qt:
                last = mm(PS[:, qt, P:2 * P], lfs[:, 5, 1, h:h + 1].broadcast_to([P, P]), negtri,
                          start=False, stop=True, skip_group_check=True)
            last.then_inc(s_done, 1)

        def turn_p(u):
            h, qt = u // 2, u % 2
            pe.wait_ge(p_ready, u + 1)
            if qt == 0 and h >= 2:
                pe.wait_ge(pT_kept, h - 1)
            if qt == 0:
                last = nc.tensor.transpose(PS[:, 2 + h % 2, 0:P], S_sb[0][:, 0:P], ident)
            else:
                nc.tensor.transpose(PS[:, 2 + h % 2, P:2 * P], S_sb[1][:, 0:P], ident)
                last = nc.tensor.transpose(PS[:, 2 + h % 2, 2 * P:3 * P], S_sb[1][:, P:2 * P], ident)
            last.then_inc(pT_done, 1)

        def attend(h):
            pe.wait_ge(pT_kept, h + 1)
            if h >= 2:
                pe.wait_ge(att_kept, h - 1)
            bank = 4 + h % 2
            mm(PS[:, bank, 0:2 * P], vnat[:, 0, P * h:P * h + P], PT[h % 2][:, 0:2 * P],
               start=True, stop=False, skip_group_check=True)
            mm(PS[:, bank, P:2 * P], vnat[:, 1, P * h:P * h + P], PT[h % 2][:, 2 * P:3 * P],
               start=False, stop=True, skip_group_check=True).then_inc(att_done, 1)

        ph = PLAN["ada4"]
        pe.wait_ge(ada_kept, 4)
        ada_edge(True)
        pe.wait_ge(vn_kept, 3)
        scores(0)
        scores(1)
        for u in range(UNITS):
            ada_tile(ph, u % SLOTS, u // SLOTS, cT[:, u, :])
            turn_p(u)
            if u + 2 < UNITS:
                scores(u + 2)
            if u % 2 and u >= 3:
                attend((u - 3) // 2)
        ada_edge(False)
        attend(HEADS - 1)
        turn_ada(4)

        for g in range(2):
            b0 = (4, 2)[g]
            if g == 0:
                pe.wait_ge(att_kept, HEADS)
            for n in range(PAGES):
                nc.tensor.transpose(PS[:, b0 + n // 4, P * (n % 4):P * (n % 4) + P], Pnat[:, g, P * n:P * n + P], ident)
            nc.tensor.transpose(PS[0:32, g, 0:P], Snew[:, g, :], ident).then_inc(psT_done, 1)

        ph = PLAN["v"]
        pe.wait_ge(psT_kept, 2)
        for g in range(2):
            for b in range(4):
                for n in range(2):
                    mm(PS[32 * b:32 * b + 32, 2 * g + n, :], PnT[:, g, 32 * b:32 * b + 32],
                       vnat[0:32, 2, 512 * n:512 * (n + 1)], start=True, stop=False, skip_group_check=True)
            for page in range(PAGES):
                i, r = 2 * g + page // 4, 2 * (page % 4)
                for m in (r, r + 1):
                    arrived(pe, ph, m, i)
                for n in range(2):
                    for b in range(4):
                        at = 1024 * (b % 2) + 512 * n
                        last = mm(PS[32 * b:32 * b + 32, 2 * g + n, :], PTs[:, g, page, 32 * b:32 * b + 32],
                                  ring[:, r + b // 2, at:at + 512], start=False, stop=(page == PAGES - 1),
                                  skip_group_check=True)
                        if n and b % 2:
                            last.then_inc(used[r + b // 2], 1)
            if g == 0:
                pe.wait_ge(pooled_ready, 1)
                pe.wait_ge(wpool_ready, 16)
                pe.wait_ge(att_kept, HEADS)
                for n in range(8):
                    w, dc, bank = n // 2, n % 2, 4 + n % 3
                    pe.wait_ge(emptied[bank], fills[bank] + 1)
                    fills[bank] += 1
                    for c in range(2):
                        last = mm(PS[:, bank, 0:NT], wpool[:, w, c, P * dc:P * dc + P], pT[:, 2 * w + c, :],
                                  start=(c == 0), stop=(c == 1))
                    last.then_inc(pmap_done, 1)
        for b in (4, 5, 6):
            pe.wait_ge(emptied[b], fills[b] + 1)
        pe.wait_ge(og_kept, 2)
        for h in range(HEADS):
            bank = (4, 5, 6, 0)[h // 2]
            for g in range(2):
                c0 = 256 * (h % 2) + P * g
                last = nc.tensor.transpose(PS[:, bank, c0:c0 + P], Og[:, g, P * h:P * h + P], ident)
        last.then_inc(oT_done, 1)

        pe.wait_ge(oT_kept, 1)
        pe.wait_ge(ada_kept, 5)
        ada_edge(True)
        four_and_four("out", mixT, 10)
        ada_edge(False)
        for b in range(4):
            pe.wait_ge(emptied[b], fills[b] + 1)
        sum_squares(lambda k: uT[:, KC + k, :])
        turn_ada(5)
        pe.wait_ge(sq_ready, 2)
        sum_squares(lambda k: hT[:, k, :])

        pe.wait_ge(h2_ready, 1)
        for t, rows in enumerate(TILE_ROWS):
            if t:
                pe.wait_ge(h2n_kept, t)
            for k in range(KC):
                last = nc.tensor.transpose(PS[0:rows, 4 + k // 4, P * (k % 4):P * (k % 4) + P],
                                           hT[:, k, P * t:P * t + rows], ident)
            last.then_inc(h2T_done, 1)
        ph = PLAN["pq"]
        with pe.Fori(0, ph.rounds) as i:
            for r in range(SLOTS):
                chunk(ph, r, i, r % 4, i * 2 + (fills[r % 4] + r // 4 + 1), hT)
        for b in range(4):
            fills[b] += 2 * ph.rounds

        def key_scores(t):
            if t == 0:
                pe.wait_ge(h2n_kept, 3)
                for b in range(4):
                    pe.wait_ge(emptied[b], fills[b] + 1)
                pe.wait_ge(sk_ready, 16)
            else:
                pe.wait_ge(sc_read, t)
            for k in range(KC):
                lhs = q2T[:, k, P * t:P * t + P] if t < 2 else q2rep[:, k, :]
                last = mm(PS[:, 4 + k // 4, P * (k % 4):P * (k % 4) + P], lhs, skT[:, k, :], start=True, stop=True)
            last.then_inc(sc_done, 1)

        key_scores(0)
        ph = PLAN["ada5"]
        ada_edge(True, bank=3)
        for k in range(KC):
            ada_tile(ph, k % SLOTS, k // SLOTS, cT[:, k, :], bank=3)
        ada_edge(False, bank=3)
        turn_ada(6, bank=3)
        key_scores(1)
        for t, rows in enumerate(TILE_ROWS):
            pe.wait_ge(f_ready, t + 1)
            if t == 0:
                pe.wait_ge(ada_kept, 7)
            for k in range(KC):
                out = psum_flat[:, rows * k:rows * (k + 1)]
                if t < 2:
                    last = nc.tensor.transpose(out, h2n[:, t, P * k:P * (k + 1)], ident)
                else:
                    last = mm(out, h2n[:, t, P * k:P * (k + 1)], fold, start=True, stop=True, skip_group_check=True)
            last.then_inc(fT_done, 1)
            pe.wait_ge(fT_kept, t + 1)
            sum_squares(lambda k: fsq[:, rows * k:rows * (k + 1)], n=rows, bank=0)
            if t == 0:
                key_scores(2)

    @blk.vector
    def _(dve):
        own = Order(dve, dve_own)
        v = nc.vector

        def norm(n, c0=0, c1=NT, bank=6):
            dve.wait_ge(ssq_done, n + 1)
            v.tensor_scalar(rstd[:, c0:c1], PS[:, bank, 0:c1 - c0], 1.0 / D, EPS, ALU.mult,
                            ALU.add).then_inc(var_ready, 1)
            dve.wait_ge(std_ready, n + 1)
            own(v.reciprocal(rstd[:, c0:c1], rstd[:, c0:c1]))

        def rows9(a, n=NQ):
            return a[:, :, 1:NROW].unsqueeze(3).broadcast_to([P, KC, NB, n])

        def by_batch(a):
            return a.rearrange("p k (b i) -> p k b i", i=NQ)

        def modulate(A, shift):
            for k in range(KC):
                v.tensor_scalar(hT[:, k, 0:NP_TOK], hT[:, k, 0:NP_TOK], A[:, k, 0:1], shift[:, k, 0:1],
                                ALU.mult, ALU.add)
            sample = by_batch(hT[:, :, NP_TOK:NT])
            own(v.tensor_tensor(sample, sample, rows9(A), ALU.mult))
            return v.tensor_tensor(sample, sample, rows9(shift), ALU.add)

        def add_gated(src, G, c0=0, c1=NT):
            c = min(c1, NP_TOK)
            if c > c0:
                for k in range(KC):
                    last = v.scalar_tensor_tensor(xT[:, k, c0:c], src[:, k, c0:c], G[:, k, 0:1], xT[:, k, c0:c],
                                                  ALU.mult, ALU.add)
            if c1 == NT:
                new = src[:, :, NP_TOK:NT]
                own(v.tensor_tensor(by_batch(new), by_batch(new), rows9(G), ALU.mult))
                last = v.tensor_tensor(xT[:, :, NP_TOK:NT], xT[:, :, NP_TOK:NT], new, ALU.add)
            return last

        def over_tokens(c0=0, c1=NT):
            return rstd[:, c0:c1].unsqueeze(1).broadcast_to([P, KC, c1 - c0])

        def keep_ada(count, n, bank=7):
            dve.wait_ge(adaT_done, count)
            return v.tensor_tensor(
                adaT[:, bass.ds(n * KC, KC), :].rearrange("p (j c) n -> p c j n", c=4),
                PS[:, bank, :].rearrange("p (c j n) -> p c j n", c=4, j=4)[:, :, :, 0:NROW],
                b_ada[:, bass.ds(n * KC, KC)].rearrange("p (j c) -> p c j", c=4).unsqueeze(3)
                .broadcast_to([P, 4, 4, NROW]), ALU.add).then_inc(ada_kept, 1)

        def gain(n):
            return gains[:, n, :].unsqueeze(2).broadcast_to([P, KC, NROW])

        def stage_c(phase, k0, n):
            ph = PLAN[phase]
            with dve.Fori(0, ph.rounds) as i:
                dve.wait_ge(used[7], i + ph.used0)
                v.tensor_copy(cstage[:, 0:n, :], cT[:, bass.ds(i * n + k0, n), :]).then_inc(cstage_ready, 1)

        v.memset(PS[:, 7, :], 0.0).then_inc(ada_kept, 1)
        dve.sem_inc(k_kept, 1)
        own(v.memset(lfs[:, 0], 0.0))
        dve.wait_ge(pages_in, 32)
        own(v.tensor_copy(mxs[:, 0:64], pg_i[:, :]))
        dve.wait_ge(cst_ready, 16)
        own(v.tensor_scalar(mxs[:, 0:64], mxs[:, 0:64], float(P), cst[:, C_PART:C_PART + 1], ALU.mult, ALU.add))
        v.tensor_copy(pg_i[:, :], mxs[:, 0:64]).then_inc(pgidx_ready, 1)
        norm(0)
        own(v.tensor_tensor(hT[:, :, :], xT[:, :, :], over_tokens(), ALU.mult))

        dve.wait_ge(lfpT_done, 1)
        own(v.tensor_copy(lfp.rearrange("p g h -> p h g"), PS[:, 5, :].rearrange("p (h g) -> p h g", h=HEADS)))
        pages = lfp.rearrange("p (b g) h -> p b g h", b=NB)
        later = lfsuf.rearrange("p (b g) h -> p b g h", b=NB)
        own(v.memset(later[:, :, PAGES - 1, :], 0.0))
        for g in range(PAGES - 2, -1, -1):
            ins = v.tensor_tensor(later[:, :, g, :], later[:, :, g + 1, :], pages[:, :, g + 1, :], ALU.add)
            if g:
                own(ins)
            else:
                ins.then_inc(lfp_kept, 1)
        dve.wait_ge(suf_done, 1)
        for b in range(NB):
            last = v.tensor_copy(
                bias[:, b // 4, :, 32 * (b % 4):32 * (b % 4) + 32].rearrange("p n (h q) -> p n h q", q=NQ),
                PS[:, 5, 64 * b:64 * b + 64].rearrange("p (n h) -> p n h", h=HEADS).unsqueeze(3)
                .broadcast_to([P, PAGES, HEADS, NQ]))
        last.then_inc(suf_kept, 1)
        dve.wait_ge(biasT_done, 1)
        v.tensor_copy(Pnat.rearrange("p g (a b) -> p (g a) b", a=2), PS[:, 0:4, :]).then_inc(bias_kept, 1)

        dve.wait_ge(prm_ready, 16)
        with dve.Fori(0, 2) as i:
            keep_ada(i + 1, i)
        dve.wait_ge(ada_kept, 3)
        own(v.scalar_tensor_tensor(A1, A1, 1.0, gain(0), ALU.add, ALU.mult))
        modulate(A1, SH1).then_inc(h_ready, 1)

        dve.wait_ge(lf_done, 1)
        v.tensor_tensor(lfs[:, 0, 0:2, :], PS[:, 6, 0:16].rearrange("p (t h) -> p t h", t=2),
                        bf.unsqueeze(1).broadcast_to([P, 2, HEADS]), ALU.add)
        own(v.tensor_tensor(lfs[0:32, 0, 2, :], PS[0:32, 6, 16:24], bf[0:32], ALU.add))
        v.scalar_tensor_tensor(lfs[:, 1], lfs[:, 0], -1.0, lfs[:, 0], ALU.mult, ALU.min).then_inc(lfabs_ready, 1)
        dve.wait_ge(lfexp_ready, 1)
        own(v.tensor_scalar(lfs[:, 2], lfs[:, 1], 1.0, None, ALU.add))
        own(v.tensor_scalar(lfs[:, 4], lfs[:, 2], -1.0, None, ALU.add))
        own(v.tensor_tensor(lfs[:, 4], lfs[:, 1], lfs[:, 4], ALU.subtract))
        v.tensor_scalar(lfs[:, 5], lfs[:, 0], 0.0, None, ALU.min).then_inc(lfu_ready, 1)
        own(v.reciprocal(lfs[:, 1], lfs[:, 2]))
        own(v.tensor_tensor(lfs[:, 4], lfs[:, 4], lfs[:, 1], ALU.mult))
        dve.wait_ge(lfln_ready, 1)
        own(v.tensor_tensor(lfs[:, 4], lfs[:, 4], lfs[:, 3], ALU.add))
        v.tensor_tensor(lfs[:, 5], lfs[:, 5], lfs[:, 4], ALU.subtract).then_inc(lf_ready, 1)

        dve.wait_ge(lf_ready, 1)
        v.tensor_copy(lfrows.rearrange("p (b h q) -> p b h q", b=4, q=NQ),
                      lfs[0:NS_TOK, 5, 2, :].unsqueeze(1).unsqueeze(3).broadcast_to([NS_TOK, 4, HEADS, NQ]))
        v.memset(work[:, 0:2048], 0.0)
        stage_c("q", 0, 4)
        for b in range(4):
            dve.wait_ge(emptied[b], 1 + 2)
        own(v.tensor_scalar(uT[:, 0:8, :], uT[:, 0:8, :], float(HD) ** -0.5, None, ALU.mult))
        for h in range(HEADS):
            last = v.tensor_copy(qz[:, h, :, NQ * h:NQ * h + NQ],
                                 uT[:, h, NP_TOK:NT].rearrange("p (b i) -> p b i", i=NQ))
        last.then_inc(qz_ready, 1)

        for g in range(2):
            ph = PLAN[f"kv{g}"]
            with dve.Fori(0, ph.rounds) as i:
                dve.wait_ge(used[7], i + ph.used0)
                v.tensor_copy(cstage[:, 0:1, :], cT[:, bass.ds(i + (8 + 4 * g), 1), :]).then_inc(cstage_ready, 1)
                dve.wait_ge(used[5], i + (ph.used0 + 1))
                at = work[:, bass.ds(i * 256 + (3384 + 1024 * g), 256)].rearrange("p (a b) -> p a b", a=2)
                v.tensor_tensor(at, PS[:, 4:6, 0:P], at, ALU.add).then_inc(k_kept, 1)
            if g == 0:
                dve.wait_ge(new_done, 1)
                v.tensor_tensor(Snew[:, :, :], PS[:, 3, 448:512].rearrange("p (g j) -> p g j", g=2), masknew,
                                ALU.add).then_inc(newmax_ready, 1)
                dve.wait_ge(newmax_ready, 1)
            dve.wait_ge(k_kept, 1 + 4 * (g + 1))
            v.tensor_reduce(mxs[:, 70:71], Pnat[:, g, :], AX_X, ALU.max)
            own(v.tensor_reduce(mxs[:, 71:72], Snew[:, g, :], AX_X, ALU.max))
            own(v.tensor_tensor(mxs[:, 70:71], mxs[:, 70:71], mxs[:, 71:72], ALU.max))
            v.tensor_scalar(mxs[:, 64 + g:65 + g], mxs[:, 70:71], -1.0, None, ALU.mult).then_inc(negmax_ready, 1)
            dve.wait_ge(negmax_ready, g + 1)
        keep_ada(3, 2)
        dve.wait_ge(exp_ready, 4)
        own(v.tensor_tensor(mxs[:, 72:74], mxs[:, 66:68], mxs[:, 68:70], ALU.add))
        v.reciprocal(mxs[:, 72:74], mxs[:, 72:74]).then_inc(den_ready, 1)
        for t, b0 in ((0, 4), (2, 2)):
            rows = TILE_ROWS[t]
            dve.wait_ge(vnT_done, t + 1)
            v.tensor_copy(vnat[0:rows, t, :].rearrange("p (a b) -> p a b", a=2),
                          PS[0:rows, b0:b0 + 2, :]).then_inc(vn_kept, 1)
        dve.wait_ge(ada_kept, 4)
        own(v.tensor_tensor(G1, G1, gain(1), ALU.mult))

        def before_exp(u):
            n = P * (1 + u % 2)
            buf = S_sb[u % 2][:, 0:n]
            dve.wait_ge(s_done, u + 1)
            if u >= 2:
                dve.wait_ge(pT_done, u - 1)
            own(v.tensor_tensor(buf, PS[:, u % 2, 0:n], mask2[:, 2 * P - n:], ALU.add))
            own(v.tensor_reduce(mxs[:, 32 + u:33 + u], buf, AX_X, ALU.max))
            v.tensor_scalar(mxs[:, u:u + 1], mxs[:, 32 + u:33 + u], -1.0, None, ALU.mult).then_inc(smax_ready, 1)

        def after_exp(u):
            n = P * (1 + u % 2)
            buf = S_sb[u % 2][:, 0:n]
            dve.wait_ge(p_exp, u + 1)
            own(v.reciprocal(mxs[:, 48 + u:49 + u], mxs[:, 16 + u:17 + u]))
            v.tensor_scalar(buf, buf, mxs[:, 48 + u:49 + u], None, ALU.mult).then_inc(p_ready, 1)

        before_exp(0)
        before_exp(1)
        for u in range(UNITS):
            after_exp(u)
            if u + 2 < UNITS:
                before_exp(u + 2)

        dve.wait_ge(hist_ready, 16)
        (pa, sa) = extA
        v.memset(pa[:, :, 0:HIST], 0.0)
        v.tensor_copy(pa[:, :, HIST:], pT[:, :, 0:NP_TOK])
        v.tensor_copy(sa[:, :, :, 0:HIST], hist)
        own(v.tensor_copy(sa[:, :, :, HIST:], pT[:, :, NP_TOK:NT].rearrange("p c (b i) -> p c b i", i=NQ)))
        v.tensor_copy(pool_st[:, 0:8 * HIST].rearrange("p (c t) -> p c t", c=8), pa[:, :, NP_TOK:NP_TOK + HIST])
        own(v.tensor_copy(pool_st[:, 8 * HIST:].rearrange("p (c b t) -> p c b t", c=8, b=NB), sa[:, :, :, NQ:]))
        dve.sem_inc(pstage_ready, 1)
        bufs = [extA, extB]
        for g, w in enumerate(WINDOWS):
            (p0, s0), (p1, s1) = bufs[g % 2], bufs[(g + 1) % 2]
            lo, sh = 2 * g, w // 2
            v.tensor_tensor(p1[:, lo:, w - 1:], p0[:, lo:, w - 1:], p0[:, lo:, w - 1 - sh:HIST + NP_TOK - sh], ALU.add)
            own(v.tensor_tensor(s1[:, lo:, :, w - 1:], s0[:, lo:, :, w - 1:],
                                s0[:, lo:, :, w - 1 - sh:HIST + NQ - sh], ALU.add))
        for g, w in enumerate(WINDOWS):
            pw, sw = bufs[(g + 1) % 2]
            c = slice(2 * g, 2 * g + 2)
            first = pw[:, c, HIST:HIST + 16]
            own(v.tensor_tensor(first, first, cst[:, C_RC + 16 * g:C_RC + 16 * g + 16].unsqueeze(1)
                                .broadcast_to([P, 2, 16]), ALU.mult))
            v.tensor_tensor(pT[:, c, 0:16], first, pT[:, c, 0:16], ALU.subtract)
            v.scalar_tensor_tensor(pT[:, c, 16:NP_TOK], pw[:, c, HIST + 16:], 1.0 / w, pT[:, c, 16:NP_TOK],
                                   ALU.mult, ALU.subtract)
            for k in range(2):
                new = pT[:, 2 * g + k, NP_TOK:NT].rearrange("p (b i) -> p b i", i=NQ)
                last = v.scalar_tensor_tensor(new, sw[:, 2 * g + k, :, HIST:], 1.0 / w, new, ALU.mult, ALU.subtract)
        last.then_inc(pooled_ready, 1)
        keep_ada(4, 4)
        dve.wait_ge(ada_kept, 5)
        own(v.scalar_tensor_tensor(A2, A2, 1.0, gain(2), ALU.add, ALU.mult))

        dve.wait_ge(oT_done, 1)
        for h in range(HEADS):
            bank, c0 = (4, 5, 6, 0)[h // 2], 256 * (h % 2)
            last = v.tensor_copy(
                mixT[:, h, NP_TOK:NT].rearrange("p (b i) -> p b i", i=NQ),
                PS[:, bank, c0:c0 + 256].rearrange("p (b m) -> p b m", b=NB)[:, :, NQ * h:NQ * h + NQ])
        last.then_inc(oT_kept, 1)
        stage_c("out", 0, 4)

        norm(1)
        m3 = uT[:, 0:KC, :]
        own(v.tensor_tensor(m3, m3, over_tokens(), ALU.mult))
        add_gated(m3, G1).then_inc(x1_ready, 1)
        keep_ada(5, 3)
        norm(2)
        own(v.tensor_tensor(hT[:, :, :], xT[:, :, :], over_tokens(), ALU.mult))
        modulate(A2, SH2).then_inc(h2_ready, 1)
        for t, rows in enumerate(TILE_ROWS):
            dve.wait_ge(h2T_done, t + 1)
            for q in range(P // rows):
                last = v.tensor_copy(h2n[rows * q:rows * (q + 1), t, :].rearrange("p (a b) -> p a b", a=4),
                                     PS[0:rows, 4:8, :])
            last.then_inc(h2n_kept, 1)

        def choose(t):
            dve.wait_ge(sc_done, t + 1)
            sc = PS[:, 4:8, :].rearrange("p a (k n) -> p (a k) n", n=SK)
            cut = scr.rearrange("p (k n) -> p k n", n=SK)
            for k in range(KC):
                last = v.max(v16[:, k, 0:8], sc[:, k, :])
            own(last)
            for k in range(KC):
                v.max_index(i16[:, k, 0:8], v16[:, k, 0:8], sc[:, k, :])
                last = v.match_replace(cut[:, k, :], v16[:, k, 0:8], sc[:, k, :], LOWEST)
            own(last)
            dve.sem_inc(sc_read, 1)
            yield
            for k in range(KC):
                last = v.max(v16[:, k, 8:16], cut[:, k, :])
            own(last)
            for k in range(KC):
                last = v.max_index(i16[:, k, 8:16], v16[:, k, 8:16], cut[:, k, :])
            own(last)
            v.tensor_copy(i16f, i16)
            cand = scr.rearrange("p (h a b) -> p h a b", h=HEADS, a=TOPK)
            vals = v16.rearrange("p (h c) n -> p h c n", c=2)
            own(v.tensor_tensor(cand, vals[:, :, 0, :].unsqueeze(3).broadcast_to([P, HEADS, TOPK, TOPK]),
                                vals[:, :, 1, :].unsqueeze(2).broadcast_to([P, HEADS, TOPK, TOPK]), ALU.add))
            yield
            cnd = scr.rearrange("p (h n) -> p h n", h=HEADS)
            for h in range(HEADS):
                last = v.max(top[:, h, 0:8], cnd[:, h, :])
            own(last)
            for h in range(HEADS):
                last = v.max_index(sel[:, h, 0:8], top[:, h, 0:8], cnd[:, h, :])
            own(last)
            for h in range(HEADS):
                last = v.match_replace(cnd[:, h, :], top[:, h, 0:8], cnd[:, h, :], LOWEST)
            own(last)
            for h in range(HEADS):
                last = v.max(top[:, h, 8:16], cnd[:, h, :])
            own(last)
            for h in range(HEADS):
                last = v.max_index(sel[:, h, 8:16], top[:, h, 8:16], cnd[:, h, :])
            own(last)
            yield
            v.tensor_scalar(sela, sel, 4, None, ALU.logical_shift_right)
            own(v.tensor_scalar(selb, sel, 15, None, ALU.bitwise_and))
            v.tensor_copy(saf, sela)
            own(v.tensor_copy(sbf, selb))
            iota = cst[:, C_IOTA:C_IOTA + TOPK].unsqueeze(1).broadcast_to([P, P, TOPK])
            hit = scr.rearrange("p (m j) -> p m j", j=TOPK)
            hit4 = scr.rearrange("p (h m j) -> p h m j", h=HEADS, j=TOPK)
            keys = i16f.rearrange("p (h c) n -> p h c n", c=2)
            for c, (which, dst) in enumerate(((saf, e1), (sbf, e2))):
                own(v.tensor_tensor(hit, which.rearrange("p h n -> p (h n)").unsqueeze(2)
                                    .broadcast_to([P, P, TOPK]), iota, ALU.is_equal))
                own(v.tensor_tensor(hit4, hit4, keys[:, :, c, :].unsqueeze(2)
                                    .broadcast_to([P, HEADS, TOPK, TOPK]), ALU.mult))
                own(v.tensor_reduce(dst.rearrange("p h n -> p (h n)"), hit, AX_X, ALU.add))
            own(v.scalar_tensor_tensor(eidx, e1.rearrange("p h n -> p (h n)"), float(SK),
                                       e2.rearrange("p h n -> p (h n)"), ALU.mult, ALU.add))
            if t < 2:
                v.tensor_copy(uidx[:, t, :], eidx).then_inc(uidx_ready, 1)
            else:
                for q in range(4):
                    rows = slice(32 * q, 32 * q + 32)
                    last = v.tensor_copy(uidx[rows, 0, 0:32], eidx[rows, 32 * q:32 * q + 32])
                last.then_inc(uidx_ready, 1)
            own(v.tensor_tensor(gate, top, top[:, :, 0:1].broadcast_to([P, HEADS, TOPK]), ALU.subtract))
            dve.sem_inc(gsub_ready, 1)
            yield

        def gates(t):
            dve.wait_ge(gexp_ready, t + 1)
            own(v.tensor_reduce(gsum, gate, AX_X, ALU.add))
            own(v.reciprocal(grec, gsum))
            own(v.tensor_tensor(gate, gate, grec.unsqueeze(2).broadcast_to([P, HEADS, TOPK]), ALU.mult))
            if t == 2:
                flat = gate.rearrange("p h n -> p (h n)")
                for q in range(4):
                    rows = slice(32 * q, 32 * q + 32)
                    last = v.tensor_copy(gate2[rows, :], flat[rows, 32 * q:32 * q + 32])
                own(last)

        def finish(t):
            c0, c1 = TILE_COLS[t]
            norm(3 + t, c0, c1, bank=0)
            own(v.tensor_tensor(fT[:, :, c0:c1], fT[:, :, c0:c1], over_tokens(c0, c1), ALU.mult))
            add_gated(fT, G2, c0, c1).then_inc(y_ready, 1)
            yield

        def expert_products(t, i0, i1):
            ph = PLAN[f"u{t}"]
            with dve.Fori(i0, i1) as i:
                for r in range(SLOTS):
                    arrived(dve, ph, r, i)
                    v.scalar_tensor_tensor(ring[:, r, :], ring[:, r, :], 1.0, h2n[:, t, :], ALU.mult, ALU.mult,
                                           accum_out=act[:, bass.ds(i * SLOTS + r, 1)]).then_inc(used[r], 1)

        def expert_sums(t, i0, i1):
            ph = PLAN[f"x{t}"]
            with dve.Fori(i0, i1) as i:
                for r in range(SLOTS):
                    arrived(dve, ph, r, i)
                    dve.wait_ge(used[(r - 1) % SLOTS], i + (ph.used0 + (1 if r else 0)))
                    v.scalar_tensor_tensor(h2n[:, t, :], ring[:, r, :], wgt[:, bass.ds(i * SLOTS + r, 1)],
                                           h2n[:, t, :], ALU.mult, ALU.add).then_inc(used[r], 1)

        def spread(step, t, parts):
            rounds = PLAN[f"u{t}"].rounds
            n = len(parts) + 1
            at = 0
            for m in range(n):
                to = rounds * (m + 1) // n
                step(t, at, to)
                at = to
                if m < n - 1:
                    next(parts[m])

        for _ in choose(0):
            pass
        keep_ada(6, 5, bank=3)
        dve.wait_ge(ada_kept, 7)
        own(v.tensor_tensor(G2, G2, gain(3), ALU.mult))
        for t in range(3):
            spread(expert_products, t, [finish(t - 1)] if t else [])
            ph = PLAN[f"u{t}"]
            dve.wait_ge(used[7], ph.used0 + ph.rounds)
            dve.sem_inc(act_ready, 1)
            gates(t)
            own(v.memset(h2n[:, t, :], 0.0))
            dve.wait_ge(gelu_ready, t + 1)
            n = P if t < 2 else NS_TOK
            own(v.tensor_tensor(wgt[:, 0:n], gate.rearrange("p h n -> p (h n)") if t < 2 else gate2, gel[:, 0:n],
                                ALU.mult))
            spread(expert_sums, t, [choose(t + 1)] * 4 if t < 2 else [])
            dve.wait_ge(used[7], PLAN[f"x{t}"].used0 + PLAN[f"x{t}"].rounds)
            dve.sem_inc(f_ready, 1)
        for _ in finish(2):
            pass

    block.__exit__(None, None, None)


def constants():
    c = np.zeros((P, C_END), np.float32)
    i = np.arange(P)
    c[:, C_ID:C_ID + P] = np.eye(P)
    c[:, C_ONE:C_ONE + P] = 1.0
    c[:, C_NTRI:C_NTRI + P] = -(i[:, None] <= i[None, :]).astype(np.float32)
    c[:, C_NONE:C_NONE + P] = -1.0
    c[:, C_MASK + P:C_MASK + 2 * P] = np.where(i[None, :] > i[:, None], NEG, 0.0)
    c[:, C_SUF:C_SUF + P] = i[:, None] > i[None, :]
    j = np.arange(NS_TOK)
    same = (j[:, None] // NQ) == (j[None, :] // NQ)
    c[0:NS_TOK, C_NT32:C_NT32 + NS_TOK] = -(same & (j[:, None] <= j[None, :])).astype(np.float32)
    row_b, row_q = i // (HEADS * NQ), i % NQ
    for g in range(2):
        seen = (j[None, :] // NQ == 4 * g + row_b[:, None]) & (j[None, :] % NQ <= row_q[:, None])
        c[:, C_MNEW + NS_TOK * g:C_MNEW + NS_TOK * (g + 1)] = np.where(seen, 0.0, NEG)
    c[:, C_FOLD:C_FOLD + NS_TOK] = (i[:, None] % NS_TOK) == j[None, :]
    c[:, C_IOTA:C_IOTA + TOPK] = np.arange(TOPK)
    for g, w in enumerate(WINDOWS):
        c[:, C_RC + 16 * g:C_RC + 16 * g + 16] = 1.0 / np.minimum(np.arange(16) + 1, w)
    c[:, C_PART] = i
    return c


def kernel(x_prompt, x_sample, c_prompt, c_sample, cache_k, cache_v, cache_logf, state_pool, page_table,
           w_ada, b_ada, g_pre_mix, g_post_mix, g_pre_ffn, g_post_ffn, w_in, b_f, w_pool, pool_scale,
           w_out, w_peer_q, peer_subkeys, peer_u, peer_v):
    from concourse import bacc
    from concourse.bass_utils import run_bass_kernel_spmd

    def arr(a):
        return np.ascontiguousarray(np.asarray(a))

    def cols(a):
        return arr(a).reshape(-1, P, a.shape[1]).transpose(1, 0, 2)

    def tiles(w):
        w = arr(w)
        return arr(w.reshape(KC, P, -1, P).transpose(2, 1, 0, 3).reshape(-1, P, D))

    x = np.concatenate([arr(x_prompt)[0], arr(x_sample).reshape(NS_TOK, D)])
    c = np.concatenate([arr(c_prompt), arr(c_sample)])
    w_i = arr(w_in)[0]
    att_w = HEADS * HD
    per_feature = [arr(b_ada)[0].reshape(6 * KC, P).T] + [
        arr(g)[0].reshape(KC, P).T for g in (g_pre_mix, g_post_mix, g_pre_ffn, g_post_ffn)]
    prm = np.concatenate(
        [cols(c.T).reshape(P, -1)] + per_feature + [
            arr(pool_scale)[0].reshape(8, P).T,
            np.broadcast_to(arr(b_f)[0][None, :], (P, HEADS)),
            cols(w_i[:, 3 * att_w:3 * att_w + HEADS]).reshape(P, -1)], axis=1)
    w_main = np.concatenate([w_i[:, :3 * att_w], w_i[:, 3 * att_w + HEADS:]], axis=1)
    pages = arr(page_table).astype(np.int32).reshape(-1)
    arrays = {
        "x_t": arr(cols(x.T)),
        "cst_in": constants(),
        "prm_in": arr(prm),
        "w_ada": arr(arr(w_ada)[0].reshape(KC, P, 6, D).transpose(2, 0, 1, 3).reshape(6 * KC, P, D)),
        "w_in": tiles(w_main),
        "w_out": tiles(arr(w_out)[0]),
        "w_pq": tiles(arr(w_peer_q)[0]),
        "cache_k": arr(arr(cache_k)[0].transpose(0, 3, 2, 1).reshape(POOL_PAGES * P, HEADS * P)),
        "cache_v": arr(cache_v)[0].reshape(POOL_PAGES * P, HEADS * HD),
        "cache_f": arr(arr(cache_logf)[0].transpose(0, 2, 1).reshape(POOL_PAGES, HEADS * P)),
        "pages_bc": arr(np.broadcast_to(pages.reshape(2, 4, PAGES).transpose(0, 2, 1).reshape(1, -1), (P, 64))),
        "pages_col": arr(pages[:, None]),
        "hist_in": arr(arr(state_pool)[0].reshape(NB, HIST, 8, P).transpose(3, 2, 0, 1)),
        "sk_in": arr(arr(peer_subkeys)[0].reshape(KC, SK, P).transpose(2, 0, 1)),
        "wpool_in": arr(arr(w_pool)[0].reshape(4, 2, P, 256).transpose(2, 0, 1, 3)),
        "peer_u": arr(peer_u)[0],
        "peer_v": arr(peer_v)[0],
    }
    outs = {"y_out": (P, KC, NT), "kv_out": (P, 16, NT), "lf_out": (NT, HEADS),
            "pool_out": (P, 8 * HIST * (1 + NB))}
    nc = bacc.Bacc("TRN2", target_bir_lowering=False, num_devices=1)
    args = {n: nc.dram_tensor(n, a.shape, mybir.dt.from_np(a.dtype), kind="ExternalInput").ap()
            for n, a in arrays.items()}
    args.update({n: nc.dram_tensor(n, s, F32, kind="ExternalOutput").ap() for n, s in outs.items()})
    build(nc, **args)
    r = run_bass_kernel_spmd(nc, [arrays], core_ids=[0]).results[0]
    y = r["y_out"].transpose(2, 1, 0).reshape(NT, D)
    kv = r["kv_out"].transpose(2, 1, 0)
    k, v = kv[:, 0:HEADS], kv[:, HEADS:]
    pool = r["pool_out"]
    pool_p = pool[:, :8 * HIST].reshape(P, 8, HIST).transpose(2, 1, 0).reshape(1, 1, HIST, 1024)
    pool_s = pool[:, 8 * HIST:].reshape(P, 8, NB, HIST).transpose(2, 3, 1, 0).reshape(1, NB, HIST, 1024)
    lf = r["lf_out"]
    return (y[:NP_TOK].reshape(1, NP_TOK, D), y[NP_TOK:].reshape(NB, NQ, D),
            k[:NP_TOK].reshape(1, 1, NP_TOK, HEADS, HD), v[:NP_TOK].reshape(1, 1, NP_TOK, HEADS, HD),
            lf[:NP_TOK].reshape(1, 1, NP_TOK, HEADS), pool_p,
            k[NP_TOK:].reshape(1, NB, NQ, HEADS, HD), v[NP_TOK:].reshape(1, NB, NQ, HEADS, HD),
            lf[NP_TOK:].reshape(1, NB, NQ, HEADS), pool_s)
```

```python
import numpy as np

import concourse.bass as bass
from concourse import mybir

F32 = mybir.dt.float32
U32 = mybir.dt.uint32
I32 = mybir.dt.int32
ALU = mybir.AluOpType
ACT = mybir.ActivationFunctionType
AX_X = mybir.AxisListType.X

P = 128
D = 2048
KC = D // P
NP_TOK, NB, NQ = 256, 8, 4
NS_TOK = NB * NQ
NT = NP_TOK + NS_TOK
NROW = 1 + NB
HEADS, HD = 8, 128
PAGES = 8
POOL_PAGES = 80
HIST = 15
WINDOWS = (2, 4, 8, 16)
SK = 128
TOPK = 16
SLOTS = 8
EPS = 1e-6
NEG = -1e30
LOWEST = -3.0e38

C_ID, C_ONE, C_NTRI, C_NONE, C_MASK, C_SUF = 0, 128, 256, 384, 512, 768
C_NT32, C_MNEW, C_IOTA, C_RC, C_PART, C_FOLD, C_END = 896, 928, 992, 1008, 1072, 1073, 1105
R_C, R_BADA, R_G, R_PS, R_BF, R_WF, R_END = 0, 144, 240, 304, 312, 320, 448

PHASES = [("ada01", 4, "AAAAAAAA"), ("p", 2, "WAWAWAWA"), ("q", 2, "WAWAWAWA"), ("kv0", 4, "WKKWKKAA"),
          ("kv1", 4, "WKKWKKAA"), ("v", 4, "VVVVVVVV"), ("out", 4, "OAOAOAOA"), ("ada5", 2, "AAAAAAAA"),
          ("pq0", 1, "QQQQQQQQ"), ("pq1", 4, "QUUUQUUU"), ("u0a", 5, "UUUUUUUU"), ("u0b", 8, "UUUUUUUU"), ("x0", 16, "XXXXXXXX"), ("u1", 16, "UUUUUUUU"),
          ("x1", 16, "XXXXXXXX"), ("u2", 4, "UUUUUUUU"), ("x2", 4, "XXXXXXXX")]


class Phase:

    def __init__(self, rounds, kinds, used0, loads, gathers):
        self.rounds, self.kinds, self.used0 = rounds, kinds, used0
        self.gathers = [k in "KVUX" for k in kinds]
        self.inc = [32 if k in "KV" else 16 for k in kinds]
        self.base = [(gathers if g else loads)[r] for r, g in enumerate(self.gathers)]


def ring_plan():
    plan, used, loads, gathers = {}, 1, [0] * SLOTS, [0] * SLOTS
    for name, rounds, kinds in PHASES:
        ph = plan[name] = Phase(rounds, kinds, used, loads, gathers)
        for r in range(SLOTS):
            (gathers if ph.gathers[r] else loads)[r] += rounds * ph.inc[r]
        used += rounds
    return plan


PLAN = ring_plan()


class Order:

    def __init__(self, eng, sem):
        self.eng, self.sem, self.base, self.k = eng, sem, 0, 0

    def __call__(self, ins):
        self.k += 1
        ins.then_inc(self.sem, 1)
        self.eng.wait_ge(self.sem, self.base + self.k)

    def enter(self, i, per):
        self.start, self.per = self.base + self.k, per
        self.base, self.k = self.start + i * per, 0

    def leave(self, count):
        assert self.k == self.per, (self.k, self.per)
        self.base, self.k = self.start + count * self.per, 0


def build(nc, x_t, cst_in, prm_in, w_ada, w_in, w_out, w_pq, cache_k, cache_v, cache_f, pages_bc, pages_col,
          hist_in, sk_in, wpool_in, peer_u, peer_v, y_out, kv_out, lf_out, pool_out):
    sb = nc.alloc_sbuf_tensor
    ring = sb("ring", [P, SLOTS, D], F32)
    xT = sb("xT", [P, KC, NT], F32)
    hT = sb("hT", [P, KC, NT], F32)
    uT = sb("uT", [P, 2 * KC, NT], F32)
    mixT = sb("mixT", [P, KC, NT], F32)
    work = sb("work", [P, 6656], F32)
    vnat = sb("vnat", [P, 3, HEADS * HD], F32)
    cst = sb("cst", [P, C_END], F32)
    prm = sb("prm", [P, R_END], F32)
    adaT = sb("adaT", [P, 6 * KC, NROW], F32)
    ada_nat = sb("ada_nat", [P, 512], F32)
    rstd = sb("rstd", [P, NT], F32)
    lfs = sb("lfs", [P, 6, 3, 8], F32)
    pg_i = sb("pg_i", [P, 64], I32)
    pg_col = sb("pg_col", [64, 1], I32)
    uidx = sb("uidx", [P, 2, P], U32)
    idxs = sb("idxs", [P, 2 * SLOTS], U32)
    mxs = sb("mxs", [P, 80], F32)
    cstage = sb("cstage", [P, 4, NROW], F32)
    PS = nc.alloc_psum_tensor("PS", [P, 8, 512], F32)
    psum_flat = PS[:, :, :].rearrange("p a b -> p (a b)")

    ident, ones = cst[:, C_ID:C_ID + P], cst[:, C_ONE:C_ONE + P]
    negtri, mask2 = cst[:, C_NTRI:C_NTRI + P], cst[:, C_MASK:C_MASK + 2 * P]
    suffix, fold = cst[:, C_SUF:C_SUF + P], cst[:, C_FOLD:C_FOLD + NS_TOK]
    negtri32 = cst[0:NS_TOK, C_NT32:C_NT32 + NS_TOK]
    masknew = cst[:, C_MNEW:C_MNEW + 64].rearrange("p (g j) -> p g j", g=2)
    cT = prm[:, R_C:R_C + KC * NROW].rearrange("p (k n) -> p k n", n=NROW)
    b_ada = prm[:, R_BADA:R_BADA + 6 * KC]
    gains = prm[:, R_G:R_G + 4 * KC].rearrange("p (g k) -> p g k", g=4)
    wf = prm[:, R_WF:R_WF + KC * HEADS].rearrange("p (k h) -> p k h", h=HEADS)
    bf = prm[:, R_BF:R_BF + HEADS]
    SH1, A1, G1, SH2, A2, G2 = (adaT[:, KC * n:KC * (n + 1)] for n in range(6))

    hF = hT[:, :, :].rearrange("p a b -> p (a b)")
    uF = uT[:, :, :].rearrange("p a b -> p (a b)")
    mF = mixT[:, :, :].rearrange("p a b -> p (a b)")
    vF = vnat[:, :, :].rearrange("p a b -> p (a b)")
    NA = 8 * (HIST + NP_TOK)
    NX = NA + 8 * NB * (HIST + NQ)

    def ext(prompt, sample):
        return (prompt.rearrange("p (c t) -> p c t", c=8), sample.rearrange("p (c b t) -> p c b t", c=8, b=NB))

    extA, extB = (ext(mF[:, n * NA:(n + 1) * NA], vF[:, n * (NX - NA):(n + 1) * (NX - NA)]) for n in range(2))
    pT = uT[:, 24:32, :]
    lfg = mF[0:64, 0:1024]
    lfp = mF[:, 1024:1536].rearrange("p (g h) -> p g h", h=HEADS)
    lfsuf = mF[:, 1536:2048].rearrange("p (g h) -> p g h", h=HEADS)
    bias = mF[:, 0:2048].rearrange("p (g n m) -> p g n m", g=2, n=PAGES)
    hist = uF[:, 4608:5568].rearrange("p (c b t) -> p c b t", c=8, b=NB)
    pool_st = uF[:, 5568:6648]
    wpool = vF[:, 0:2048].rearrange("p (g c d) -> p g c d", g=4, c=2)
    sqsum = hF[:, 0:NT]
    S_sb = [hF[:, 3400 + 256 * n:3656 + 256 * n] for n in range(4)]
    PT = [work[:, 5432 + 384 * n:5432 + 384 * (n + 1)] for n in range(2)]
    qz = work[:, 0:2048].rearrange("p (h b m) -> p h b m", b=NB, h=HEADS)
    Pnat = work[:, 3384:5432].rearrange("p (g n) -> p g n", g=2)
    Snew = work[:, 6200:6264].rearrange("p (g j) -> p g j", g=2)
    PnT = work[0:32, 6264:6520].rearrange("p (g m) -> p g m", g=2)
    lfrows = work[0:NS_TOK, 6520:6648]
    PTs = hF[:, 0:2048].rearrange("p (g n m) -> p g n m", g=2, n=PAGES)
    Og = work[:, 0:2048].rearrange("p (g n) -> p g n", g=2)
    h2n = uF[:, 0:3 * D].rearrange("p (t n) -> p t n", t=3)
    scr = uF[:, 6144:8192]
    act, gel, wgt = (uF[:, 8192 + n * P:8320 + n * P] for n in range(3))
    q2T = work[:, 0:KC * NT].rearrange("p (k t) -> p k t", k=KC)
    q2rep = work[:, KC * NT:KC * NT + D].rearrange("p (k t) -> p k t", k=KC)
    skT = vF[:, 0:D].rearrange("p (k n) -> p k n", k=KC)
    fT = hT
    v16 = mF[:, 0:256].rearrange("p (k n) -> p k n", n=TOPK)
    i16 = mF[:, 256:512].bitcast(U32).rearrange("p (k n) -> p k n", n=TOPK)
    i16f = mF[:, 512:768].rearrange("p (k n) -> p k n", n=TOPK)
    top = mF[:, 768:896].rearrange("p (h n) -> p h n", n=TOPK)
    sel, sela, selb = (mF[:, 896 + n * P:1024 + n * P].bitcast(U32).rearrange("p (h n) -> p h n", n=TOPK)
                       for n in range(3))
    saf, sbf, e1, e2 = (mF[:, 1280 + n * P:1408 + n * P].rearrange("p (h n) -> p h n", n=TOPK) for n in range(4))
    eidx = mF[:, 1792:1920]
    gate = mF[:, 1920:2048].rearrange("p (h n) -> p h n", n=TOPK)
    gsum = mF[:, 2048:2056]
    grec = mF[:, 2056:2064]
    gate2 = mF[:, 2064:2096]
    fsum = mF[:, 2096:2224]
    fsq = mF[:, 2304:4352]

    def sem(name):
        return nc.alloc_semaphore(name)

    landed = [sem(f"landed{n}") for n in range(SLOTS)]
    gathered = [sem(f"gathered{n}") for n in range(SLOTS)]
    used = [sem(f"used{n}") for n in range(SLOTS)]
    emptied = [sem(f"emptied{n}") for n in range(7)]
    (x_in, cst_ready, prm_ready, pages_in, hist_ready, wpool_ready, sk_ready, out_done) = map(sem, (
        "x_in", "cst_ready", "prm_ready", "pages_in", "hist_ready", "wpool_ready", "sk_ready", "out_done"))
    dve_own, pool_own, gather_turns = sem("dve_own"), sem("pool_own"), sem("gather_turns")
    sq_ready, ssq_done, var_ready, std_ready = map(sem, ("sq_ready", "ssq_done", "var_ready", "std_ready"))
    sqsum_ready, h2mul_ready, fsum_ready = sem("sqsum_ready"), sem("h2mul_ready"), sem("fsum_ready")
    biasT_done, bias_kept, k_kept = sem("biasT_done"), sem("bias_kept"), sem("k_kept")
    ada_summed, cstage_ready = sem("ada_summed"), sem("cstage_ready")
    silu_ready, adanat_kept, adaT_done, ada_kept = map(sem, ("silu_ready", "adanat_kept", "adaT_done", "ada_kept"))
    pgidx_ready, lfg_in, lfpT_done, lfp_kept, suf_done, suf_kept = map(sem, (
        "pgidx_ready", "lfg_in", "lfpT_done", "lfp_kept", "suf_done", "suf_kept"))
    h_ready, lf_done, lfabs_ready, lfexp_ready, lfu_ready, lfln_ready, lf_ready = map(sem, (
        "h_ready", "lf_done", "lfabs_ready", "lfexp_ready", "lfu_ready", "lfln_ready", "lf_ready"))
    kv_sent, pool_sent, pstage_ready = sem("kv_sent"), sem("pool_sent"), sem("pstage_ready")
    qz_ready, new_done, newmax_ready, negmax_ready, exp_ready = map(sem, (
        "qz_ready", "new_done", "newmax_ready", "negmax_ready", "exp_ready"))
    vnT_done, vn_kept, pooled_ready, pmap_done = map(sem, ("vnT_done", "vn_kept", "pooled_ready", "pmap_done"))
    vn1_kept, a1_ready, hact_ready, zT_done, z_kept = map(sem, ("vn1_kept", "a1_ready", "hact_ready", "zT_done", "z_kept"))
    s_done, smax_ready, p_exp, p_ready, pT_done, pT_kept, att_done, att_kept = map(sem, (
        "s_done", "smax_ready", "p_exp", "p_ready", "pT_done", "pT_kept", "att_done", "att_kept"))
    psT_done, psT_kept, den_ready, og_kept, oT_done, oT_kept = map(sem, (
        "psT_done", "psT_kept", "den_ready", "og_kept", "oT_done", "oT_kept"))
    x1_ready, h2_ready, h2T_done, h2n_kept = map(sem, ("x1_ready", "h2_ready", "h2T_done", "h2n_kept"))
    sc_done, sc_read, gsub_ready, gexp_ready = map(sem, ("sc_done", "sc_read", "gsub_ready", "gexp_ready"))
    uidx_ready, act_ready, gelu_ready, f_ready, fT_done, fT_kept, y_ready = map(sem, (
        "uidx_ready", "act_ready", "gelu_ready", "f_ready", "fT_done", "fT_kept", "y_ready"))

    UNITS = 2 * HEADS
    OUT_FILLS = (15, 15, 6, 4)
    TILE_ROWS = (P, P, NS_TOK)
    TILE_COLS = [(0, P), (P, 2 * P), (2 * P, NT)]

    def arrived(eng, ph, r, i):
        eng.wait_ge((gathered if ph.gathers[r] else landed)[r], i * ph.inc[r] + (ph.base[r] + ph.inc[r]))

    block = nc.Block()
    blk = block.__enter__()

    @blk.sync
    def _(sp):
        for r in range(SLOTS):
            sp.sem_inc(used[r], 1)
        sp.dma_start(prm[:, :], prm_in).then_inc(prm_ready, 16)
        sp.dma_start(cst[:, :], cst_in).then_inc(cst_ready, 16)

        def stream(phase, tile_of, start=0, end=None):
            ph = PLAN[phase]
            with sp.Fori(start, end or ph.rounds) as i:
                for r in range(SLOTS):
                    if not ph.gathers[r]:
                        kind = ph.kinds[r]
                        sp.wait_ge(used[r], i + ph.used0)
                        sp.dma_start(ring[:, r, :], tile_of(kind, ph.kinds[:r].count(kind), i)).then_inc(landed[r], 16)

        stream("ada01", lambda kind, n, i: w_ada[i * SLOTS + n], 0, 1)
        sp.dma_start(xT[:, :, :], x_t).then_inc(x_in, 16)
        stream("ada01", lambda kind, n, i: w_ada[i * SLOTS + n], 1)
        sp.dma_start(hist[:, :, :, :], hist_in).then_inc(hist_ready, 16)
        stream("p", lambda kind, n, i: w_in[i * 4 + (24 + n)] if kind == "W" else w_ada[i * 4 + (2 * KC + n)])
        sp.wait_ge(lf_ready, 1)
        sp.dma_start(lf_out[0:2 * P].rearrange("(t p) h -> p t h", p=P), lfs[:, 5, 0:2, :]).then_inc(out_done, 16)
        sp.dma_start(lf_out[2 * P:NT], lfs[0:NS_TOK, 5, 2, :]).then_inc(out_done, 16)
        stream("q", lambda kind, n, i: w_in[i * 4 + n] if kind == "W" else w_ada[i * 4 + (2 * KC + 8 + n)])
        sp.wait_ge(pstage_ready, 1)
        sp.dma_start(pool_out, pool_st).then_inc(pool_sent, 16)
        stream("kv0", lambda kind, n, i: w_in[i * 2 + (8 + n)] if kind == "W" else w_ada[i * 2 + (4 * KC + n)])
        sp.wait_ge(pooled_ready, 1)
        sp.dma_start(wpool[:, :, :, :], wpool_in).then_inc(wpool_ready, 16)
        stream("kv1", lambda kind, n, i: w_in[i * 2 + (16 + n)] if kind == "W" else w_ada[i * 2 + (4 * KC + 8 + n)])
        for b in range(2):
            sp.wait_ge(emptied[b], 1 + OUT_FILLS[b])
        sp.dma_start(kv_out, uT[:, 8:24, :]).then_inc(kv_sent, 16)
        stream("out", lambda kind, n, i: w_out[i * 4 + n] if kind == "O" else w_ada[i * 4 + (3 * KC + n)])
        sp.wait_ge(used[0], PLAN["out"].used0 + 1)
        sp.dma_start(skT, sk_in).then_inc(sk_ready, 16)
        stream("ada5", lambda kind, n, i: w_ada[i * SLOTS + (5 * KC + n)])
        stream("pq0", lambda kind, n, i: w_pq[n])
        stream("pq1", lambda kind, n, i: w_pq[i * 2 + (8 + n)])
        for t, (c0, c1) in enumerate(TILE_COLS):
            sp.wait_ge(y_ready, t + 1)
            sp.dma_start(y_out[:, :, c0:c1], xT[:, :, c0:c1]).then_inc(out_done, 16)
        sp.wait_ge(kv_sent, 16)
        sp.wait_ge(pool_sent, 16)
        sp.wait_ge(out_done, 5 * 16)

    @blk.gpsimd
    def _(pool):
        own = Order(pool, pool_own)
        pool.dma_start(pg_col[:, :], pages_col).then_inc(pages_in, 16)
        pool.dma_start(pg_i[:, :], pages_bc).then_inc(pages_in, 16)
        pool.wait_ge(pages_in, 32)
        pool.indirect_dma_start(out=lfg, out_offset=None, in_=cache_f,
                                in_offset=bass.IndirectOffsetOnAxis(ap=pg_col[:, 0:1], axis=0)).then_inc(lfg_in, 16)

        def gather(phase, index, col0, table, per):
            ph = PLAN[phase]
            mine = [r for r in range(SLOTS) if ph.gathers[r]]
            width = D // per
            with pool.Fori(0, ph.rounds) as i:
                own.enter(i, len(mine))
                for n, r in enumerate(mine):
                    pool.wait_ge(used[r], i + ph.used0)
                    pool.sem_inc(gather_turns, 1)
                    own(nc.gpsimd.tensor_copy(idxs[:, per * r:per * (r + 1)],
                                              index[:, bass.ds(i * (per * len(mine)) + (col0 + per * n), per)]))
                    pool.sem_inc(gather_turns, 1)
                    for m in range(per):
                        pool.indirect_dma_start(
                            out=ring[:, r, width * m:width * (m + 1)], out_offset=None, in_=table,
                            in_offset=bass.IndirectOffsetOnAxis(ap=idxs[:, per * r + m:per * r + m + 1], axis=0),
                        ).then_inc(gathered[r], 16)
                own.leave(ph.rounds)

        pool.wait_ge(silu_ready, 1)
        ph = PLAN["q"]
        with pool.Fori(0, ph.rounds) as i:
            pool.wait_ge(used[7], i + ph.used0)
            pool.sem_inc(gather_turns, 1)
            nc.gpsimd.tensor_copy(cstage[:, :, :], cT[:, bass.ds(i * 4 + 8, 4), :]).then_inc(cstage_ready, 1)
        pool.wait_ge(pgidx_ready, 1)
        gather("kv0", pg_i, 0, cache_k, 2)
        gather("kv1", pg_i, 32, cache_k, 2)
        gather("v", pg_i, 0, cache_v, 2)
        pool.wait_ge(uidx_ready, 1)
        gather("pq1", uidx[:, 0, :], 0, peer_u, 1)
        pool.wait_ge(uidx_ready, 2)
        gather("u0a", uidx[:, 0, :], 24, peer_u, 1)
        pool.wait_ge(uidx_ready, 3)
        gather("u0b", uidx[:, 0, :], 64, peer_u, 1)
        gather("x0", uidx[:, 0, :], 0, peer_v, 1)
        for t in (1, 2):
            pool.wait_ge(uidx_ready, t + 3)
            gather(f"u{t}", uidx[:, t % 2, :], 0, peer_u, 1)
            gather(f"x{t}", uidx[:, t % 2, :], 0, peer_v, 1)

    @blk.scalar
    def _(a):
        fn = nc.scalar.activation
        for b in range(7):
            a.sem_inc(emptied[b], 1)
        a.wait_ge(prm_ready, 16)
        fn(cT, cT, ACT.Silu).then_inc(silu_ready, 1)
        a.wait_ge(x_in, 16)
        fn(hT[:, :, :], xT[:, :, :], ACT.Square).then_inc(sq_ready, 1)

        def root(n, c0=0, c1=NT):
            a.wait_ge(var_ready, n + 1)
            fn(rstd[:, c0:c1], rstd[:, c0:c1], ACT.Sqrt).then_inc(std_ready, 1)

        def keep_adanat(count, bank=7):
            a.wait_ge(ada_summed, count)
            fn(ada_nat[:, :], PS[:, bank, :], ACT.Copy).then_inc(adanat_kept, 1)

        keep_adanat(1)
        root(0)
        keep_adanat(2)
        a.wait_ge(a1_ready, 1)
        for k in range(8, KC):
            last = fn(hT[:, k, 0:NP_TOK], hT[:, k, 0:NP_TOK], ACT.Identity, bias=SH1[:, k, 0:1], scale=A1[:, k, 0:1])
        last.then_inc(hact_ready, 1)
        a.wait_ge(zT_done, 1)
        fn(rstd[0:HEADS, :], PS[0:HEADS, 6, 0:NT], ACT.Copy).then_inc(z_kept, 1)
        a.wait_ge(lfabs_ready, 1)
        fn(lfs[:, 1], lfs[:, 1], ACT.Exp).then_inc(lfexp_ready, 1)
        a.wait_ge(lfu_ready, 1)
        fn(lfs[:, 3], lfs[:, 2], ACT.Ln).then_inc(lfln_ready, 1)

        def evacuate(phase, kind, chunk0, banks, one):
            ph = PLAN[phase]
            slots = [r for r in range(SLOTS) if ph.kinds[r] == kind]
            with a.Fori(0, ph.rounds) as i:
                for n, r in enumerate(slots):
                    a.wait_ge(used[r], i + (ph.used0 + 1))
                    bank = n % banks
                    one(i * len(slots) + (chunk0 + n), bank).then_inc(emptied[bank], 1)

        def keep_u(n, bank):
            return fn(uT[:, bass.ds(n, 1), :], PS[:, bank:bank + 1, 0:NT], ACT.Copy)

        def sampled_exp(g):
            a.wait_ge(negmax_ready, g + 1)
            fn(Pnat[:, g, :], Pnat[:, g, :], ACT.Exp, bias=mxs[:, 64 + g:65 + g],
               accum_out=mxs[:, 66 + g:67 + g]).then_inc(exp_ready, 1)
            fn(Snew[:, g, :], Snew[:, g, :], ACT.Exp, bias=mxs[:, 64 + g:65 + g],
               accum_out=mxs[:, 68 + g:69 + g]).then_inc(exp_ready, 1)

        def keep_psT(g):
            a.wait_ge(psT_done, g + 1)
            fn(PTs[:, g].rearrange("p (a b) m -> p a (b m)", a=2), PS[:, 2:4, :], ACT.Copy)
            fn(PnT[:, g, :], PS[0:32, 6, P * g:P * (g + 1)], ACT.Copy).then_inc(psT_kept, 1)

        evacuate("p", "W", 24, 4, keep_u)
        evacuate("q", "W", 0, 4, keep_u)
        keep_adanat(3)
        evacuate("kv0", "W", 8, 2, keep_u)
        for n in range(8):
            a.wait_ge(pmap_done, n + 1)
            fn(mixT[:, 8 + n, :], PS[:, n % 3, 0:NT], ACT.Copy,
               scale=prm[:, R_PS + n:R_PS + n + 1]).then_inc(emptied[n % 3], 1)
        sampled_exp(0)
        a.wait_ge(pool_sent, 16)
        evacuate("kv1", "W", 16, 2, keep_u)
        keep_adanat(4)
        keep_psT(0)
        sampled_exp(1)
        a.wait_ge(vnT_done, 2)
        fn(vnat[:, 1, :].rearrange("p (a b) -> p a b", a=2), PS[:, 4:6, :], ACT.Copy).then_inc(vn1_kept, 1)

        def keep_og(g):
            a.wait_ge(used[7], PLAN["v"].used0 + 2 * (g + 1))
            fn(Og[:, g, :].rearrange("p (a b) -> p a b", a=2), PS[:, 6:8, :], ACT.Copy,
               scale=mxs[:, 72 + g:73 + g]).then_inc(og_kept, 1)

        def keep_pT(h):
            a.wait_ge(pT_done, 2 * h + 2)
            if h >= 2:
                a.wait_ge(att_done, h - 1)
            fn(PT[h % 2], PS[:, 2 + h % 2, 0:384], ACT.Copy).then_inc(pT_kept, 1)

        def keep_att(h):
            a.wait_ge(att_done, h + 1)
            fn(mixT[:, h, 0:NP_TOK], PS[:, 4 + h % 2, 0:NP_TOK], ACT.Copy).then_inc(att_kept, 1)

        for u in range(UNITS + 5):
            if u < UNITS:
                a.wait_ge(smax_ready, u + 1)
                if u >= 4:
                    a.wait_ge(pT_done, u - 3)
                n = P * (1 + u % 2)
                fn(S_sb[u % 4][:, 0:n], PS[:, u % 2, 0:n], ACT.Exp,
                   bias=mxs[:, u:u + 1], accum_out=mxs[:, 16 + u:17 + u]).then_inc(p_exp, 1)
            if u == 1:
                keep_psT(1)
            if u >= 3 and u % 2 and (u - 3) // 2 < HEADS:
                keep_pT((u - 3) // 2)
            if u >= 5 and u % 2 and (u - 5) // 2 < HEADS:
                keep_att((u - 5) // 2)
            if u == 8:
                a.wait_ge(den_ready, 1)
                keep_og(0)
        keep_og(1)
        a.wait_ge(kv_sent, 16)

        def keep_m(n, bank):
            keep_u(n, bank)
            return fn(uT[:, bass.ds(n + KC, 1), :], PS[:, bank:bank + 1, 0:NT], ACT.Square)

        evacuate("out", "O", 0, 4, keep_m)
        keep_adanat(5)
        root(1)
        for g in range(4):
            a.wait_ge(x1_ready, g + 1)
            fn(hT[:, 4 * g:4 * g + 4, :], xT[:, 4 * g:4 * g + 4, :], ACT.Square).then_inc(sq_ready, 1)
        root(2)
        for g in range(4):
            a.wait_ge(h2mul_ready, g + 1)
            for k in range(4 * g, 4 * g + 4):
                last = fn(hT[:, k, 0:NP_TOK], hT[:, k, 0:NP_TOK], ACT.Identity, bias=SH2[:, k, 0:1])
            last.then_inc(h2_ready, 1)

        def keep_q(n, bank):
            fn(q2T[:, bass.ds(n, 1), :], PS[:, bank:bank + 1, 0:NT], ACT.Copy)
            return fn(q2rep[:, bass.ds(n, 1), :].rearrange("p o (r t) -> p (o r) t", r=4),
                      PS[:, bank:bank + 1, NP_TOK:NT].broadcast_to([P, 4, NS_TOK]), ACT.Copy)

        def keep_h2n(t):
            a.wait_ge(h2T_done, t + 1)
            rows = TILE_ROWS[t]
            for q in range(P // rows):
                last = fn(h2n[rows * q:rows * (q + 1), t, :].rearrange("p (a b) -> p a b", a=4),
                          PS[0:rows, 0:4, :], ACT.Copy)
            last.then_inc(h2n_kept, 1)

        for n in range(SLOTS):
            bank = n if n < 4 else 5 + n % 2
            a.wait_ge(used[n], PLAN["pq0"].used0 + 1)
            keep_q(n, bank).then_inc(emptied[bank], 1)
            if n == 3:
                keep_adanat(6)
                keep_h2n(0)
        evacuate("pq1", "Q", 8, 2, keep_q)
        keep_h2n(1)
        keep_h2n(2)

        def exp_gates(t):
            a.wait_ge(gsub_ready, t + 1)
            fn(gate, gate, ACT.Exp).then_inc(gexp_ready, 1)

        exp_gates(0)
        for t, (c0, c1) in enumerate(TILE_COLS):
            n = P if t < 2 else NS_TOK
            a.wait_ge(act_ready, t + 1)
            fn(gel[:, 0:n], act[:, 0:n], ACT.Gelu).then_inc(gelu_ready, 1)
            if t < 2:
                exp_gates(t + 1)
            n = c1 - c0
            src = psum_flat[:, 0:KC * n].rearrange("p (k m) -> p k m", k=KC)
            a.wait_ge(fT_done, t + 1)
            fn(fT[:, :, c0:c1], src, ACT.Copy)
            if t:
                a.wait_ge(fsum_ready, t)
            fn(fsq[:, 0:KC * n].rearrange("p (k m) -> p k m", k=KC), src, ACT.Square).then_inc(fT_kept, 1)
            root(3 + t, c0, c1)

    @blk.tensor
    def _(pe):
        mm = nc.tensor.matmul
        fills = [0] * 7

        def sum_squares(src, n=NT, bank=6):
            for k in range(KC):
                last = mm(PS[:, bank, 0:n], ones, src(k), start=(k == 0), stop=(k == KC - 1))
            last.then_inc(ssq_done, 1)

        def ada_edge(opening, bank=7):
            for j in range(4):
                last = mm(PS[32 * j:32 * j + NROW, bank, :], mask2[:, 0:NROW], cst[:, 0:512],
                          start=opening, stop=not opening, skip_group_check=True)
            if not opening:
                last.then_inc(ada_summed, 1)

        def ada_tile(ph, r, i, c_rows, bank=7):
            arrived(pe, ph, r, i)
            for j in range(4):
                last = mm(PS[32 * j:32 * j + NROW, bank, :], c_rows, ring[:, r, 512 * j:512 * (j + 1)],
                          start=False, stop=False, skip_group_check=True)
            last.then_inc(used[r], 1)

        def turn_ada(count, bank=7):
            pe.wait_ge(adanat_kept, count)
            for c in range(4):
                last = nc.tensor.transpose(PS[:, bank, P * c:P * c + P], ada_nat[:, P * c:P * c + P], ident)
            last.then_inc(adaT_done, 1)

        def log_forget_turn():
            pe.wait_ge(lfg_in, 16)
            for h in range(HEADS):
                last = nc.tensor.transpose(PS[:, 5, 64 * h:64 * h + 64], lfg[:, P * h:P * h + P], ident[0:64, 0:64])
            last.then_inc(lfpT_done, 1)

        def log_forget_sums():
            pe.wait_ge(lfp_kept, 1)
            mm(PS[:, 5, :], suffix, lfp, start=True, stop=False)
            mm(PS[:, 5, :], ones, lfsuf, start=False, stop=True).then_inc(suf_done, 1)

        def log_forget_rows():
            pe.wait_ge(suf_kept, 1)
            for g in range(2):
                for n in range(PAGES):
                    last = nc.tensor.transpose(PS[:, (0, 2)[g] + n // 4, P * (n % 4):P * (n % 4) + P],
                                               bias[:, g, n, :], ident)
            last.then_inc(biasT_done, 1)

        pe.wait_ge(cst_ready, 16)
        pe.wait_ge(silu_ready, 1)
        between = {(1, 2): log_forget_turn, (1, 6): log_forget_sums, (1, 10): log_forget_rows}
        ph = PLAN["ada01"]
        for piece in range(2):
            pe.wait_ge(ada_kept, piece + 1)
            ada_edge(True)
            for k in range(KC):
                ada_tile(ph, k % SLOTS, piece * 2 + k // SLOTS, cT[:, k, :])
                if (piece, k) in between:
                    between[piece, k]()
            ada_edge(False)
            turn_ada(piece + 1)
            if piece == 0:
                pe.wait_ge(sq_ready, 1)
                sum_squares(lambda k: hT[:, k, :])

        pe.wait_ge(h_ready, 1)
        pe.wait_ge(hact_ready, 1)
        for k in range(KC):
            last = mm(PS[0:HEADS, 6, 0:NT], wf[:, k, :], hT[:, k, :], start=(k == 0), stop=(k == KC - 1))
        last.then_inc(zT_done, 1)
        pe.wait_ge(z_kept, 1)
        for t, rows in enumerate(TILE_ROWS):
            last = nc.tensor.transpose(PS[0:rows, 5, 8 * t:8 * t + 8], rstd[0:HEADS, P * t:P * t + rows],
                                       ident[0:HEADS, 0:HEADS])
        last.then_inc(lf_done, 1)

        def chunk(ph, r, i, bank, fill, src, groups_ready=None):
            pe.wait_ge(emptied[bank], fill)
            arrived(pe, ph, r, i)
            for k in range(KC):
                if groups_ready is not None and k % 4 == 0:
                    pe.wait_ge(groups_ready, k // 4 + 1)
                last = mm(PS[:, bank, 0:NT], ring[:, r, P * k:P * (k + 1)], src[:, k, :],
                          start=(k == 0), stop=(k == KC - 1))
            last.then_inc(used[r], 1)

        def four_and_four(phase, src, staged):
            ph = PLAN[phase]
            with pe.Fori(0, ph.rounds) as i:
                for r in range(SLOTS):
                    if r % 2 == 0:
                        chunk(ph, r, i, r // 2, i + (fills[r // 2] + 1), src)
                    else:
                        if r == 1:
                            pe.wait_ge(cstage_ready, i + (staged + 1))
                        ada_tile(ph, r, i, cstage[:, r // 2, :])
            for b in range(4):
                fills[b] += ph.rounds

        def k_slots(ph, g, i, pair, r):
            for m in (r, r + 1):
                arrived(pe, ph, m, i)
            for h in range(HEADS):
                for b in range(4):
                    at = P * h + 1024 * (b % 2)
                    last = mm(PS[32 * b:32 * b + 32, 4 + pair, 0:P], qz[:, h, 4 * g + b, :],
                              ring[:, r + b // 2, at:at + P],
                              start=(h == 0), stop=(h == HEADS - 1), skip_group_check=True)
                    if h == HEADS - 1 and b % 2:
                        last.then_inc(used[r + b // 2], 1)

        pe.wait_ge(bias_kept, 1)
        pe.wait_ge(ada_kept, 3)
        ada_edge(True)
        four_and_four("p", hT, 0)
        four_and_four("q", hT, 2)
        ada_edge(False)
        turn_ada(3)
        pe.wait_ge(ada_kept, 4)
        ada_edge(True)
        pe.wait_ge(qz_ready, 1)

        for g in range(2):
            ph = PLAN[f"kv{g}"]
            with pe.Fori(0, ph.rounds) as i:
                chunk(ph, 0, i, 0, i + (fills[0] + 1), hT)
                pe.wait_ge(k_kept, i + (4 * g + 1))
                k_slots(ph, g, i, 0, 1)
                chunk(ph, 3, i, 1, i + (fills[1] + 1), hT)
                k_slots(ph, g, i, 1, 4)
                pe.wait_ge(cstage_ready, i + (4 + 4 * g + 1))
                for r in (6, 7):
                    ada_tile(ph, r, i, cstage[:, r - 6, :])
            for b in range(2):
                fills[b] += ph.rounds
            if g == 0:
                for b in range(2):
                    pe.wait_ge(emptied[b], fills[b] + 1)
                for gg in range(2):
                    for h in range(HEADS):
                        mm(PS[:, 3, 448 + 32 * gg:480 + 32 * gg], qz[:, h, 4 * gg:4 * gg + 4, :].rearrange("p b m -> p (b m)"),
                           uT[:, 8 + h, NP_TOK:NT], start=(h == 0), stop=False, skip_group_check=True)
                    last = mm(PS[:, 3, 448 + 32 * gg:480 + 32 * gg], lfrows, negtri32, start=False, stop=True, skip_group_check=True)
                last.then_inc(new_done, 1)
                pe.wait_ge(pooled_ready, 1)
                pe.wait_ge(wpool_ready, 16)
                for n in range(8):
                    w, dc, bank = n // 2, n % 2, n % 3
                    pe.wait_ge(emptied[bank], fills[bank] + 1)
                    fills[bank] += 1
                    for c in range(2):
                        last = mm(PS[:, bank, 0:NT], wpool[:, w, c, P * dc:P * dc + P], pT[:, 2 * w + c, :],
                                  start=(c == 0), stop=(c == 1))
                    last.then_inc(pmap_done, 1)
        ada_edge(False)
        turn_ada(4)

        def turn_sampled_p(g):
            for n in range(PAGES):
                nc.tensor.transpose(PS[:, 2 + n // 4, P * (n % 4):P * (n % 4) + P], Pnat[:, g, P * n:P * n + P], ident)
            nc.tensor.transpose(PS[0:32, 6, P * g:P * (g + 1)], Snew[:, g, :], ident).then_inc(psT_done, 1)

        pe.wait_ge(newmax_ready, 1)
        pe.wait_ge(exp_ready, 2)
        pe.wait_ge(emptied[2], fills[2] + 1)
        turn_sampled_p(0)
        for b in range(2):
            pe.wait_ge(emptied[b], fills[b] + 1)
        pe.wait_ge(k_kept, 9)
        for t, rows in enumerate(TILE_ROWS):
            b0 = (0, 4, 2)[t]
            if t == 2:
                pe.wait_ge(psT_kept, 1)
            for h in range(HEADS):
                last = nc.tensor.transpose(PS[0:rows, b0 + h // 4, P * (h % 4):P * (h % 4) + P],
                                           uT[:, 16 + h, P * t:P * t + rows], ident)
            last.then_inc(vnT_done, 1)

        def scores(u):
            h, qt = u // 2, u % 2
            mm(PS[:, qt, 0:P * (qt + 1)], uT[:, h, P * qt:P * qt + P], uT[:, 8 + h, 0:P * (qt + 1)],
               start=True, stop=False, skip_group_check=True)
            mm(PS[:, qt, 0:P * (qt + 1)], lfs[:, 5, 0, h:h + 1].broadcast_to([P, P]),
               cst[:, C_NTRI:C_NTRI + P * (qt + 1)], start=False, stop=False, skip_group_check=True)
            if qt:
                mm(PS[:, qt, P:2 * P], lfs[:, 5, 1, h:h + 1].broadcast_to([P, P]), negtri,
                   start=False, stop=False, skip_group_check=True)
            mm(PS[:, qt, P * qt:P * (qt + 1)], ident, mask2[:, P:2 * P],
               start=False, stop=True, skip_group_check=True).then_inc(s_done, 1)

        def turn_p(u):
            h, qt = u // 2, u % 2
            pe.wait_ge(p_ready, u + 1)
            if qt == 0 and h >= 2:
                pe.wait_ge(pT_kept, h - 1)
            if qt == 0:
                last = nc.tensor.transpose(PS[:, 2 + h % 2, 0:P], S_sb[u % 4][:, 0:P], ident)
            else:
                nc.tensor.transpose(PS[:, 2 + h % 2, P:2 * P], S_sb[u % 4][:, 0:P], ident)
                last = nc.tensor.transpose(PS[:, 2 + h % 2, 2 * P:3 * P], S_sb[u % 4][:, P:2 * P], ident)
            last.then_inc(pT_done, 1)

        def attend(h):
            pe.wait_ge(pT_kept, h + 1)
            if h >= 2:
                pe.wait_ge(att_kept, h - 1)
            bank = 4 + h % 2
            mm(PS[:, bank, 0:2 * P], vnat[:, 0, P * h:P * h + P], PT[h % 2][:, 0:2 * P],
               start=True, stop=False, skip_group_check=True)
            mm(PS[:, bank, P:2 * P], vnat[:, 1, P * h:P * h + P], PT[h % 2][:, 2 * P:3 * P],
               start=False, stop=True, skip_group_check=True).then_inc(att_done, 1)

        def sampled_page(n):
            g, page = divmod(n, PAGES)
            i, r = n // 4, 2 * (n % 4)
            if page == 0:
                for b in range(4):
                    for c in range(2):
                        mm(PS[32 * b:32 * b + 32, 6 + c, :], PnT[:, g, 32 * b:32 * b + 32],
                           vnat[0:32, 2, 512 * c:512 * (c + 1)], start=True, stop=False, skip_group_check=True)
            for m in (r, r + 1):
                arrived(pe, PLAN["v"], m, i)
            for c in range(2):
                for b in range(4):
                    at = 1024 * (b % 2) + 512 * c
                    last = mm(PS[32 * b:32 * b + 32, 6 + c, :], PTs[:, g, page, 32 * b:32 * b + 32],
                              ring[:, r + b // 2, at:at + 512], start=False, stop=(page == PAGES - 1),
                              skip_group_check=True)
                    if c and b % 2:
                        last.then_inc(used[r + b // 2], 1)

        pe.wait_ge(vn_kept, 1)
        scores(0)
        scores(1)
        pe.wait_ge(vn_kept, 2)
        pe.wait_ge(vn1_kept, 1)
        pe.wait_ge(exp_ready, 4)
        turn_sampled_p(1)
        pe.wait_ge(psT_kept, 2)
        pe.wait_ge(ada_kept, 5)
        for u in range(UNITS):
            turn_p(u)
            if u + 2 < UNITS:
                scores(u + 2)
            if u % 2 and u >= 3:
                attend((u - 3) // 2)
            if u == 8:
                pe.wait_ge(og_kept, 1)
            sampled_page(u)
        attend(HEADS - 1)

        pe.wait_ge(att_kept, HEADS)
        pe.wait_ge(og_kept, 2)
        for h in range(HEADS):
            for g in range(2):
                c0 = 256 * (h % 2) + P * g
                last = nc.tensor.transpose(PS[:, h // 2, c0:c0 + P], Og[:, g, P * h:P * h + P], ident)
        last.then_inc(oT_done, 1)

        pe.wait_ge(oT_kept, 1)
        ada_edge(True)
        assert tuple(fills[0:4]) == OUT_FILLS
        four_and_four("out", mixT, 12)
        ada_edge(False)
        pe.wait_ge(sqsum_ready, 1)
        mm(PS[:, 6, 0:NT], ones, sqsum, start=True, stop=True).then_inc(ssq_done, 1)
        turn_ada(5)
        ph = PLAN["ada5"]
        pe.wait_ge(ada_kept, 6)
        ada_edge(True)
        for k in range(KC):
            ada_tile(ph, k % SLOTS, k // SLOTS, cT[:, k, :])
            if 3 <= k < 7:
                pe.wait_ge(sq_ready, k - 1)
                for m in range(4 * (k - 3), 4 * (k - 2)):
                    last = mm(PS[:, 6, 0:NT], ones, hT[:, m, :], start=(m == 0), stop=(m == KC - 1))
                if k == 6:
                    last.then_inc(ssq_done, 1)
        ada_edge(False)

        def key_scores(t, h0=0, h1=HEADS):
            for k in range(2 * h0, 2 * h1):
                lhs = q2T[:, k, P * t:P * t + P] if t < 2 else q2rep[:, k, :]
                last = mm(PS[:, 4 + k // 4, P * (k % 4):P * (k % 4) + P], lhs, skT[:, k, :], start=True, stop=True)
            last.then_inc(sc_done, 1)

        def turn_h2(t):
            rows = TILE_ROWS[t]
            for k in range(KC):
                last = nc.tensor.transpose(PS[0:rows, k // 4, P * (k % 4):P * (k % 4) + P],
                                           hT[:, k, P * t:P * t + rows], ident)
            last.then_inc(h2T_done, 1)

        ph = PLAN["pq0"]
        for n in range(4):
            chunk(ph, n, 0, n, fills[n] + 1, hT, h2_ready if n == 0 else None)
            fills[n] += 1
        turn_ada(6)
        for b in range(4):
            pe.wait_ge(emptied[b], fills[b] + 1)
        pe.wait_ge(sk_ready, 16)
        key_scores(0, 0, 2)
        turn_h2(0)
        for n in range(4, SLOTS):
            bank = 5 + n % 2
            chunk(ph, n, 0, bank, fills[bank] + 1, hT)
            fills[bank] += 1
        for b in (5, 6):
            pe.wait_ge(emptied[b], fills[b] + 1)
        key_scores(0, 2, 4)
        pe.wait_ge(h2n_kept, 1)
        ph = PLAN["pq1"]
        with pe.Fori(0, ph.rounds) as i:
            for n in range(2):
                chunk(ph, 4 * n, i, n, i + (fills[n] + 1), hT)
        for b in range(2):
            fills[b] += ph.rounds
            pe.wait_ge(emptied[b], fills[b] + 1)
        pe.wait_ge(ada_kept, 7)
        key_scores(0, 4, 8)
        turn_h2(1)
        pe.wait_ge(h2n_kept, 2)
        turn_h2(2)
        pe.wait_ge(sc_read, 3)
        key_scores(1)
        for t, rows in enumerate(TILE_ROWS):
            pe.wait_ge(f_ready, t + 1)
            if t == 0:
                pe.wait_ge(h2n_kept, 3)
            for k in range(KC):
                out = psum_flat[:, rows * k:rows * (k + 1)]
                if t < 2:
                    last = nc.tensor.transpose(out, h2n[:, t, P * k:P * (k + 1)], ident)
                else:
                    last = mm(out, h2n[:, t, P * k:P * (k + 1)], fold, start=True, stop=True, skip_group_check=True)
            last.then_inc(fT_done, 1)
            pe.wait_ge(fT_kept, t + 1)
            pe.wait_ge(fsum_ready, t + 1)
            mm(PS[:, 0, 0:rows], ones, fsum[:, 0:rows], start=True, stop=True).then_inc(ssq_done, 1)
            if t == 0:
                pe.wait_ge(sc_read, 4)
                key_scores(2)

    @blk.vector
    def _(dve):
        own = Order(dve, dve_own)
        v = nc.vector

        def norm(n, c0=0, c1=NT, bank=6):
            dve.wait_ge(ssq_done, n + 1)
            v.tensor_scalar(rstd[:, c0:c1], PS[:, bank, 0:c1 - c0], 1.0 / D, EPS, ALU.mult,
                            ALU.add).then_inc(var_ready, 1)
            dve.wait_ge(std_ready, n + 1)
            own(v.reciprocal(rstd[:, c0:c1], rstd[:, c0:c1]))

        def rows9(a, n=NQ):
            return a[:, :, 1:NROW].unsqueeze(3).broadcast_to([P, KC, NB, n])

        def by_batch(a):
            return a.rearrange("p k (b i) -> p k b i", i=NQ)

        def add_gated(src, G, c0=0, c1=NT):
            c = min(c1, NP_TOK)
            if c > c0:
                for k in range(KC):
                    last = v.scalar_tensor_tensor(xT[:, k, c0:c], src[:, k, c0:c], G[:, k, 0:1], xT[:, k, c0:c],
                                                  ALU.mult, ALU.add)
            if c1 == NT:
                new = src[:, :, NP_TOK:NT]
                own(v.tensor_tensor(by_batch(new), by_batch(new), rows9(G), ALU.mult))
                last = v.tensor_tensor(xT[:, :, NP_TOK:NT], xT[:, :, NP_TOK:NT], new, ALU.add)
            return last

        def over_tokens(c0=0, c1=NT):
            return rstd[:, c0:c1].unsqueeze(1).broadcast_to([P, KC, c1 - c0])

        def keep_ada(count, n, bank=7):
            dve.wait_ge(adaT_done, count)
            return v.tensor_tensor(
                adaT[:, bass.ds(n * KC, KC), :].rearrange("p (j c) n -> p c j n", c=4),
                PS[:, bank, :].rearrange("p (c j n) -> p c j n", c=4, j=4)[:, :, :, 0:NROW],
                b_ada[:, bass.ds(n * KC, KC)].rearrange("p (j c) -> p c j", c=4).unsqueeze(3)
                .broadcast_to([P, 4, 4, NROW]), ALU.add).then_inc(ada_kept, 1)

        def gain(n):
            return gains[:, n, :].unsqueeze(2).broadcast_to([P, KC, NROW])

        def stage_c(phase, k0, n):
            ph = PLAN[phase]
            with dve.Fori(0, ph.rounds) as i:
                dve.wait_ge(used[7], i + ph.used0)
                v.tensor_copy(cstage[:, 0:n, :], cT[:, bass.ds(i * n + k0, n), :]).then_inc(cstage_ready, 1)

        v.memset(PS[:, 7, :], 0.0).then_inc(ada_kept, 1)
        dve.sem_inc(k_kept, 1)
        own(v.memset(lfs[:, 0], 0.0))
        dve.wait_ge(pages_in, 32)
        own(v.tensor_copy(mxs[:, 0:64], pg_i[:, :]))
        dve.wait_ge(cst_ready, 16)
        own(v.tensor_scalar(mxs[:, 0:64], mxs[:, 0:64], float(P), cst[:, C_PART:C_PART + 1], ALU.mult, ALU.add))
        v.tensor_copy(pg_i[:, :], mxs[:, 0:64]).then_inc(pgidx_ready, 1)
        dve.wait_ge(prm_ready, 16)
        keep_ada(1, 0)
        norm(0)
        own(v.tensor_tensor(hT[:, :, :], xT[:, :, :], over_tokens(), ALU.mult))

        dve.wait_ge(lfpT_done, 1)
        own(v.tensor_copy(lfp.rearrange("p g h -> p h g"), PS[:, 5, :].rearrange("p (h g) -> p h g", h=HEADS)))
        pages = lfp.rearrange("p (b g) h -> p b g h", b=NB)
        later = lfsuf.rearrange("p (b g) h -> p b g h", b=NB)
        own(v.memset(later[:, :, PAGES - 1, :], 0.0))
        for g in range(PAGES - 2, -1, -1):
            ins = v.tensor_tensor(later[:, :, g, :], later[:, :, g + 1, :], pages[:, :, g + 1, :], ALU.add)
            if g:
                own(ins)
            else:
                ins.then_inc(lfp_kept, 1)
        dve.wait_ge(suf_done, 1)
        for b in range(NB):
            last = v.tensor_copy(
                bias[:, b // 4, :, 32 * (b % 4):32 * (b % 4) + 32].rearrange("p n (h q) -> p n h q", q=NQ),
                PS[:, 5, 64 * b:64 * b + 64].rearrange("p (n h) -> p n h", h=HEADS).unsqueeze(3)
                .broadcast_to([P, PAGES, HEADS, NQ]))
        last.then_inc(suf_kept, 1)
        dve.wait_ge(biasT_done, 1)
        v.tensor_copy(Pnat.rearrange("p g (a b) -> p (g a) b", a=2), PS[:, 0:4, :]).then_inc(bias_kept, 1)

        keep_ada(2, 1)
        dve.wait_ge(ada_kept, 3)
        own(v.scalar_tensor_tensor(A1, A1, 1.0, gain(0), ALU.add, ALU.mult))
        dve.sem_inc(a1_ready, 1)
        for k in range(8):
            v.tensor_scalar(hT[:, k, 0:NP_TOK], hT[:, k, 0:NP_TOK], A1[:, k, 0:1], SH1[:, k, 0:1],
                            ALU.mult, ALU.add)
        sample = by_batch(hT[:, :, NP_TOK:NT])
        own(v.tensor_tensor(sample, sample, rows9(A1), ALU.mult))
        v.tensor_tensor(sample, sample, rows9(SH1), ALU.add).then_inc(h_ready, 1)

        dve.wait_ge(lf_done, 1)
        v.tensor_tensor(lfs[:, 0, 0:2, :], PS[:, 5, 0:16].rearrange("p (t h) -> p t h", t=2),
                        bf.unsqueeze(1).broadcast_to([P, 2, HEADS]), ALU.add)
        own(v.tensor_tensor(lfs[0:32, 0, 2, :], PS[0:32, 5, 16:24], bf[0:32], ALU.add))
        v.scalar_tensor_tensor(lfs[:, 1], lfs[:, 0], -1.0, lfs[:, 0], ALU.mult, ALU.min).then_inc(lfabs_ready, 1)
        dve.wait_ge(lfexp_ready, 1)
        own(v.tensor_scalar(lfs[:, 2], lfs[:, 1], 1.0, None, ALU.add))
        own(v.tensor_scalar(lfs[:, 4], lfs[:, 2], -1.0, None, ALU.add))
        own(v.tensor_tensor(lfs[:, 4], lfs[:, 1], lfs[:, 4], ALU.subtract))
        v.tensor_scalar(lfs[:, 5], lfs[:, 0], 0.0, None, ALU.min).then_inc(lfu_ready, 1)
        own(v.reciprocal(lfs[:, 1], lfs[:, 2]))
        own(v.tensor_tensor(lfs[:, 4], lfs[:, 4], lfs[:, 1], ALU.mult))
        dve.wait_ge(lfln_ready, 1)
        own(v.tensor_tensor(lfs[:, 4], lfs[:, 4], lfs[:, 3], ALU.add))
        v.tensor_tensor(lfs[:, 5], lfs[:, 5], lfs[:, 4], ALU.subtract).then_inc(lf_ready, 1)

        dve.wait_ge(lf_ready, 1)
        v.tensor_copy(lfrows.rearrange("p (b h q) -> p b h q", b=4, q=NQ),
                      lfs[0:NS_TOK, 5, 2, :].unsqueeze(1).unsqueeze(3).broadcast_to([NS_TOK, 4, HEADS, NQ]))
        v.memset(work[:, 0:2048], 0.0)
        stage_c("p", 0, 4)
        for b in range(4):
            dve.wait_ge(emptied[b], 1 + 2)
        dve.wait_ge(hist_ready, 16)
        (pa, sa) = extA
        v.memset(pa[:, :, 0:HIST], 0.0)
        v.tensor_copy(pa[:, :, HIST:], pT[:, :, 0:NP_TOK])
        v.tensor_copy(sa[:, :, :, 0:HIST], hist)
        own(v.tensor_copy(sa[:, :, :, HIST:], pT[:, :, NP_TOK:NT].rearrange("p c (b i) -> p c b i", i=NQ)))
        v.tensor_copy(pool_st[:, 0:8 * HIST].rearrange("p (c t) -> p c t", c=8), pa[:, :, NP_TOK:NP_TOK + HIST])
        own(v.tensor_copy(pool_st[:, 8 * HIST:].rearrange("p (c b t) -> p c b t", c=8, b=NB), sa[:, :, :, NQ:]))
        dve.sem_inc(pstage_ready, 1)
        bufs = [extA, extB]
        for g, w in enumerate(WINDOWS):
            (p0, s0), (p1, s1) = bufs[g % 2], bufs[(g + 1) % 2]
            lo, sh = 2 * g, w // 2
            v.tensor_tensor(p1[:, lo:, w - 1:], p0[:, lo:, w - 1:], p0[:, lo:, w - 1 - sh:HIST + NP_TOK - sh], ALU.add)
            own(v.tensor_tensor(s1[:, lo:, :, w - 1:], s0[:, lo:, :, w - 1:],
                                s0[:, lo:, :, w - 1 - sh:HIST + NQ - sh], ALU.add))
        for g, w in enumerate(WINDOWS):
            pw, sw = bufs[(g + 1) % 2]
            c = slice(2 * g, 2 * g + 2)
            first = pw[:, c, HIST:HIST + 16]
            own(v.tensor_tensor(first, first, cst[:, C_RC + 16 * g:C_RC + 16 * g + 16].unsqueeze(1)
                                .broadcast_to([P, 2, 16]), ALU.mult))
            v.tensor_tensor(pT[:, c, 0:16], first, pT[:, c, 0:16], ALU.subtract)
            v.scalar_tensor_tensor(pT[:, c, 16:NP_TOK], pw[:, c, HIST + 16:], 1.0 / w, pT[:, c, 16:NP_TOK],
                                   ALU.mult, ALU.subtract)
            for k in range(2):
                new = pT[:, 2 * g + k, NP_TOK:NT].rearrange("p (b i) -> p b i", i=NQ)
                last = v.scalar_tensor_tensor(new, sw[:, 2 * g + k, :, HIST:], 1.0 / w, new, ALU.mult, ALU.subtract)
        last.then_inc(pooled_ready, 1)

        for b in range(4):
            dve.wait_ge(emptied[b], 1 + 4)
        own(v.tensor_scalar(uT[:, 0:8, :], uT[:, 0:8, :], float(HD) ** -0.5, None, ALU.mult))
        for h in range(HEADS):
            last = v.tensor_copy(qz[:, h, :, NQ * h:NQ * h + NQ],
                                 uT[:, h, NP_TOK:NT].rearrange("p (b i) -> p b i", i=NQ))
        last.then_inc(qz_ready, 1)
        keep_ada(3, 2)

        for g in range(2):
            ph = PLAN[f"kv{g}"]
            with dve.Fori(0, ph.rounds) as i:
                dve.wait_ge(used[7], i + ph.used0)
                v.tensor_copy(cstage[:, 0:2, :], cT[:, bass.ds(i * 2 + 8 * g, 2), :]).then_inc(cstage_ready, 1)
                dve.wait_ge(used[5], i + (ph.used0 + 1))
                at = work[:, bass.ds(i * 256 + (3384 + 1024 * g), 256)].rearrange("p (a b) -> p a b", a=2)
                v.tensor_tensor(at, PS[:, 4:6, 0:P], at, ALU.add).then_inc(k_kept, 1)
            if g == 0:
                dve.wait_ge(new_done, 1)
                v.tensor_tensor(Snew[:, :, :], PS[:, 3, 448:512].rearrange("p (g j) -> p g j", g=2), masknew,
                                ALU.add).then_inc(newmax_ready, 1)
                dve.wait_ge(newmax_ready, 1)
            dve.wait_ge(k_kept, 1 + 4 * (g + 1))
            v.tensor_reduce(mxs[:, 70:71], Pnat[:, g, :], AX_X, ALU.max)
            own(v.tensor_reduce(mxs[:, 71:72], Snew[:, g, :], AX_X, ALU.max))
            own(v.tensor_tensor(mxs[:, 70:71], mxs[:, 70:71], mxs[:, 71:72], ALU.max))
            v.tensor_scalar(mxs[:, 64 + g:65 + g], mxs[:, 70:71], -1.0, None, ALU.mult).then_inc(negmax_ready, 1)
            dve.wait_ge(negmax_ready, g + 1)
        keep_ada(4, 4)
        for t, b0 in ((0, 0), (2, 2)):
            rows = TILE_ROWS[t]
            dve.wait_ge(vnT_done, t + 1)
            v.tensor_copy(vnat[0:rows, t, :].rearrange("p (a b) -> p a b", a=2),
                          PS[0:rows, b0:b0 + 2, :]).then_inc(vn_kept, 1)

        def before_exp(u):
            dve.wait_ge(s_done, u + 1)
            own(v.tensor_reduce(mxs[:, 32 + u:33 + u], PS[:, u % 2, 0:P * (1 + u % 2)], AX_X, ALU.max))
            v.tensor_scalar(mxs[:, u:u + 1], mxs[:, 32 + u:33 + u], -1.0, None, ALU.mult).then_inc(smax_ready, 1)

        def after_exp(u):
            buf = S_sb[u % 4][:, 0:P * (1 + u % 2)]
            dve.wait_ge(p_exp, u + 1)
            own(v.reciprocal(mxs[:, 48 + u:49 + u], mxs[:, 16 + u:17 + u]))
            v.tensor_scalar(buf, buf, mxs[:, 48 + u:49 + u], None, ALU.mult).then_inc(p_ready, 1)

        before_exp(0)
        before_exp(1)
        for u in range(UNITS):
            after_exp(u)
            if u + 2 < UNITS:
                before_exp(u + 2)
            if u == 1:
                dve.wait_ge(exp_ready, 4)
                own(v.tensor_tensor(mxs[:, 72:74], mxs[:, 66:68], mxs[:, 68:70], ALU.add))
                v.reciprocal(mxs[:, 72:74], mxs[:, 72:74]).then_inc(den_ready, 1)
        dve.wait_ge(ada_kept, 5)
        own(v.tensor_tensor(G1, G1, gain(1), ALU.mult))
        own(v.scalar_tensor_tensor(A2, A2, 1.0, gain(2), ALU.add, ALU.mult))

        dve.wait_ge(oT_done, 1)
        for h in range(HEADS):
            bank, c0 = h // 2, 256 * (h % 2)
            last = v.tensor_copy(
                mixT[:, h, NP_TOK:NT].rearrange("p (b i) -> p b i", i=NQ),
                PS[:, bank, c0:c0 + 256].rearrange("p (b m) -> p b m", b=NB)[:, :, NQ * h:NQ * h + NQ])
        last.then_inc(oT_kept, 1)
        own(v.memset(sqsum, 0.0))
        ph = PLAN["out"]
        with dve.Fori(0, ph.rounds) as i:
            own.enter(i, 4)
            dve.wait_ge(used[7], i + ph.used0)
            v.tensor_copy(cstage[:, :, :], cT[:, bass.ds(i * 4, 4), :]).then_inc(cstage_ready, 1)
            for n in range(4):
                dve.wait_ge(emptied[n], i + (OUT_FILLS[n] + 2))
                own(v.tensor_tensor(sqsum, sqsum, uF[:, bass.ds(i * (4 * NT) + (KC + n) * NT, NT)], ALU.add))
            own.leave(ph.rounds)
        dve.sem_inc(sqsum_ready, 1)

        norm(1)
        m3 = uT[:, 0:KC, :]
        new, x_new, h_new = m3[:, :, NP_TOK:NT], xT[:, :, NP_TOK:NT], hT[:, :, NP_TOK:NT]
        own(v.tensor_tensor(new, new, over_tokens(NP_TOK, NT), ALU.mult))
        own(v.tensor_tensor(by_batch(new), by_batch(new), rows9(G1), ALU.mult))
        v.tensor_tensor(x_new, x_new, new, ALU.add)
        for g in range(4):
            ks = slice(4 * g, 4 * g + 4)
            for k in range(4 * g, 4 * g + 4):
                last = v.scalar_tensor_tensor(m3[:, k, 0:NP_TOK], m3[:, k, 0:NP_TOK], G1[:, k, 0:1],
                                              rstd[:, 0:NP_TOK], ALU.mult, ALU.mult)
            own(last)
            v.tensor_tensor(xT[:, ks, 0:NP_TOK], xT[:, ks, 0:NP_TOK], m3[:, ks, 0:NP_TOK], ALU.add).then_inc(x1_ready, 1)
            if g == 0:
                keep_ada(5, 3)
        norm(2)
        own(v.tensor_tensor(h_new, x_new, over_tokens(NP_TOK, NT), ALU.mult))
        own(v.tensor_tensor(by_batch(h_new), by_batch(h_new), rows9(A2), ALU.mult))
        dve.wait_ge(ada_kept, 6)
        v.tensor_tensor(by_batch(h_new), by_batch(h_new), rows9(SH2), ALU.add)
        for k in range(KC):
            last = v.scalar_tensor_tensor(hT[:, k, 0:NP_TOK], xT[:, k, 0:NP_TOK], A2[:, k, 0:1],
                                          rstd[:, 0:NP_TOK], ALU.mult, ALU.mult)
            if k % 4 == 3:
                last.then_inc(h2mul_ready, 1)

        def choose(t, h0=0, h1=HEADS):
            hs, nh, ks = slice(h0, h1), h1 - h0, range(2 * h0, 2 * h1)
            count = t + 3 if t else 1 + h0 // 2
            dve.wait_ge(sc_done, count)
            sc = PS[:, 4:8, :].rearrange("p a (k n) -> p (a k) n", n=SK)
            cut = scr.rearrange("p (k n) -> p k n", n=SK)
            for k in ks:
                last = v.max(v16[:, k, 0:8], sc[:, k, :])
            own(last)
            for k in ks:
                v.max_index(i16[:, k, 0:8], v16[:, k, 0:8], sc[:, k, :])
                last = v.match_replace(cut[:, k, :], v16[:, k, 0:8], sc[:, k, :], LOWEST)
            own(last)
            dve.sem_inc(sc_read, 1)
            yield
            for k in ks:
                last = v.max(v16[:, k, 8:16], cut[:, k, :])
            own(last)
            for k in ks:
                last = v.max_index(i16[:, k, 8:16], v16[:, k, 8:16], cut[:, k, :])
            own(last)
            yield
            v.tensor_copy(i16f[:, 2 * h0:2 * h1, :], i16[:, 2 * h0:2 * h1, :])
            cand = scr.rearrange("p (h a b) -> p h a b", h=HEADS, a=TOPK)
            vals = v16.rearrange("p (h c) n -> p h c n", c=2)
            own(v.tensor_tensor(cand[:, hs], vals[:, hs, 0, :].unsqueeze(3).broadcast_to([P, nh, TOPK, TOPK]),
                                vals[:, hs, 1, :].unsqueeze(2).broadcast_to([P, nh, TOPK, TOPK]), ALU.add))
            yield
            cnd = scr.rearrange("p (h n) -> p h n", h=HEADS)
            for h in range(h0, h1):
                last = v.max(top[:, h, 0:8], cnd[:, h, :])
            own(last)
            for h in range(h0, h1):
                last = v.max_index(sel[:, h, 0:8], top[:, h, 0:8], cnd[:, h, :])
            own(last)
            for h in range(h0, h1):
                last = v.match_replace(cnd[:, h, :], top[:, h, 0:8], cnd[:, h, :], LOWEST)
            own(last)
            yield
            for h in range(h0, h1):
                last = v.max(top[:, h, 8:16], cnd[:, h, :])
            own(last)
            for h in range(h0, h1):
                last = v.max_index(sel[:, h, 8:16], top[:, h, 8:16], cnd[:, h, :])
            own(last)
            yield
            v.tensor_scalar(sela[:, hs], sel[:, hs], 4, None, ALU.logical_shift_right)
            own(v.tensor_scalar(selb[:, hs], sel[:, hs], 15, None, ALU.bitwise_and))
            v.tensor_copy(saf[:, hs], sela[:, hs])
            own(v.tensor_copy(sbf[:, hs], selb[:, hs]))
            ms = slice(TOPK * h0, TOPK * h1)
            iota = cst[:, C_IOTA:C_IOTA + TOPK].unsqueeze(1).broadcast_to([P, TOPK * nh, TOPK])
            hit = scr.rearrange("p (m j) -> p m j", j=TOPK)[:, ms]
            hit4 = scr.rearrange("p (h m j) -> p h m j", h=HEADS, j=TOPK)[:, hs]
            keys = i16f.rearrange("p (h c) n -> p h c n", c=2)
            for c, (which, dst) in enumerate(((saf, e1), (sbf, e2))):
                own(v.tensor_tensor(hit, which.rearrange("p h n -> p (h n)")[:, ms].unsqueeze(2)
                                    .broadcast_to([P, TOPK * nh, TOPK]), iota, ALU.is_equal))
                own(v.tensor_tensor(hit4, hit4, keys[:, hs, c, :].unsqueeze(2)
                                    .broadcast_to([P, nh, TOPK, TOPK]), ALU.mult))
                own(v.tensor_reduce(dst.rearrange("p h n -> p (h n)")[:, ms], hit, AX_X, ALU.add))
                if c == 0:
                    yield
            own(v.scalar_tensor_tensor(eidx[:, ms], e1.rearrange("p h n -> p (h n)")[:, ms], float(SK),
                                       e2.rearrange("p h n -> p (h n)")[:, ms], ALU.mult, ALU.add))
            if t < 2:
                v.tensor_copy(uidx[:, t, ms], eidx[:, ms]).then_inc(uidx_ready, 1)
            else:
                for q in range(4):
                    rows = slice(32 * q, 32 * q + 32)
                    last = v.tensor_copy(uidx[rows, 0, 0:32], eidx[rows, 32 * q:32 * q + 32])
                last.then_inc(uidx_ready, 1)
            if h1 < HEADS:
                return
            own(v.tensor_tensor(gate, top, top[:, :, 0:1].broadcast_to([P, HEADS, TOPK]), ALU.subtract))
            dve.sem_inc(gsub_ready, 1)
            yield

        def gates(t):
            dve.wait_ge(gexp_ready, t + 1)
            own(v.tensor_reduce(gsum, gate, AX_X, ALU.add))
            own(v.reciprocal(grec, gsum))
            own(v.tensor_tensor(gate, gate, grec.unsqueeze(2).broadcast_to([P, HEADS, TOPK]), ALU.mult))
            if t == 2:
                flat = gate.rearrange("p h n -> p (h n)")
                for q in range(4):
                    rows = slice(32 * q, 32 * q + 32)
                    last = v.tensor_copy(gate2[rows, :], flat[rows, 32 * q:32 * q + 32])
                own(last)

        def finish(t):
            c0, c1 = TILE_COLS[t]
            dve.wait_ge(fT_kept, t + 1)
            own(v.tensor_reduce(fsum[:, 0:c1 - c0], fsq[:, 0:KC * (c1 - c0)].rearrange("p (k m) -> p m k", k=KC),
                                AX_X, ALU.add))
            dve.sem_inc(fsum_ready, 1)
            yield
            norm(3 + t, c0, c1, bank=0)
            own(v.tensor_tensor(fT[:, :, c0:c1], fT[:, :, c0:c1], over_tokens(c0, c1), ALU.mult))
            yield
            add_gated(fT, G2, c0, c1).then_inc(y_ready, 1)
            yield

        def expert_products(t, phase, col0, i0, i1):
            ph = PLAN[phase]
            slots = [r for r in range(SLOTS) if ph.kinds[r] == "U"]
            with dve.Fori(i0, i1) as i:
                for n, r in enumerate(slots):
                    arrived(dve, ph, r, i)
                    v.scalar_tensor_tensor(
                        ring[:, r, :], ring[:, r, :], 1.0, h2n[:, t, :], ALU.mult, ALU.mult,
                        accum_out=act[:, bass.ds(i * len(slots) + (col0 + n), 1)]).then_inc(used[r], 1)

        def expert_sums(t, i0, i1):
            ph = PLAN[f"x{t}"]
            with dve.Fori(i0, i1) as i:
                for r in range(SLOTS):
                    arrived(dve, ph, r, i)
                    dve.wait_ge(used[(r - 1) % SLOTS], i + (ph.used0 + (1 if r else 0)))
                    v.scalar_tensor_tensor(h2n[:, t, :], ring[:, r, :], wgt[:, bass.ds(i * SLOTS + r, 1)],
                                           h2n[:, t, :], ALU.mult, ALU.add).then_inc(used[r], 1)

        def spread(step, rounds, parts):
            n = len(parts) + 1
            at = 0
            for m in range(n):
                to = rounds * (m + 1) // n
                if to > at:
                    step(at, to)
                at = to
                if m < n - 1:
                    next(parts[m])

        for _ in choose(0, 0, 2):
            pass
        keep_ada(6, 5)
        dve.wait_ge(ada_kept, 7)
        own(v.tensor_tensor(G2, G2, gain(3), ALU.mult))
        for t in range(3):
            if t == 0:
                dve.wait_ge(h2n_kept, 1)
                expert_products(0, "pq1", 0, 0, 1)
                for _ in choose(0, 2, 4):
                    pass
                expert_products(0, "pq1", 0, 1, PLAN["pq1"].rounds)
                spread(lambda i0, i1: expert_products(0, "u0a", 24, i0, i1), PLAN["u0a"].rounds, [choose(0, 4, 8)] * 7)
                last_phase = PLAN["u0b"]
                expert_products(0, "u0b", 64, 0, last_phase.rounds)
            else:
                last_phase = PLAN[f"u{t}"]
                spread(lambda i0, i1: expert_products(t, f"u{t}", 0, i0, i1), last_phase.rounds, [finish(t - 1)] * 3)
            dve.wait_ge(used[7], last_phase.used0 + last_phase.rounds)
            dve.sem_inc(act_ready, 1)
            gates(t)
            own(v.memset(h2n[:, t, :], 0.0))
            dve.wait_ge(gelu_ready, t + 1)
            n = P if t < 2 else NS_TOK
            own(v.tensor_tensor(wgt[:, 0:n], gate.rearrange("p h n -> p (h n)") if t < 2 else gate2, gel[:, 0:n],
                                ALU.mult))
            spread(lambda i0, i1: expert_sums(t, i0, i1), PLAN[f"x{t}"].rounds, [choose(t + 1)] * 7 if t < 2 else [])
            dve.wait_ge(used[7], PLAN[f"x{t}"].used0 + PLAN[f"x{t}"].rounds)
            dve.sem_inc(f_ready, 1)
        for _ in finish(2):
            pass

    block.__exit__(None, None, None)


def constants():
    c = np.zeros((P, C_END), np.float32)
    i = np.arange(P)
    c[:, C_ID:C_ID + P] = np.eye(P)
    c[:, C_ONE:C_ONE + P] = 1.0
    c[:, C_NTRI:C_NTRI + P] = -(i[:, None] <= i[None, :]).astype(np.float32)
    c[:, C_NONE:C_NONE + P] = -1.0
    c[:, C_MASK + P:C_MASK + 2 * P] = np.where(i[None, :] > i[:, None], NEG, 0.0)
    c[:, C_SUF:C_SUF + P] = i[:, None] > i[None, :]
    j = np.arange(NS_TOK)
    same = (j[:, None] // NQ) == (j[None, :] // NQ)
    c[0:NS_TOK, C_NT32:C_NT32 + NS_TOK] = -(same & (j[:, None] <= j[None, :])).astype(np.float32)
    row_b, row_q = i // (HEADS * NQ), i % NQ
    for g in range(2):
        seen = (j[None, :] // NQ == 4 * g + row_b[:, None]) & (j[None, :] % NQ <= row_q[:, None])
        c[:, C_MNEW + NS_TOK * g:C_MNEW + NS_TOK * (g + 1)] = np.where(seen, 0.0, NEG)
    c[:, C_FOLD:C_FOLD + NS_TOK] = (i[:, None] % NS_TOK) == j[None, :]
    c[:, C_IOTA:C_IOTA + TOPK] = np.arange(TOPK)
    for g, w in enumerate(WINDOWS):
        c[:, C_RC + 16 * g:C_RC + 16 * g + 16] = 1.0 / np.minimum(np.arange(16) + 1, w)
    c[:, C_PART] = i
    return c


def kernel(x_prompt, x_sample, c_prompt, c_sample, cache_k, cache_v, cache_logf, state_pool, page_table,
           w_ada, b_ada, g_pre_mix, g_post_mix, g_pre_ffn, g_post_ffn, w_in, b_f, w_pool, pool_scale,
           w_out, w_peer_q, peer_subkeys, peer_u, peer_v):
    from concourse import bacc
    from concourse.bass_utils import run_bass_kernel_spmd

    def arr(a):
        return np.ascontiguousarray(np.asarray(a))

    def cols(a):
        return arr(a).reshape(-1, P, a.shape[1]).transpose(1, 0, 2)

    def tiles(w):
        w = arr(w)
        return arr(w.reshape(KC, P, -1, P).transpose(2, 1, 0, 3).reshape(-1, P, D))

    x = np.concatenate([arr(x_prompt)[0], arr(x_sample).reshape(NS_TOK, D)])
    c = np.concatenate([arr(c_prompt), arr(c_sample)])
    w_i = arr(w_in)[0]
    att_w = HEADS * HD
    per_feature = [arr(b_ada)[0].reshape(6 * KC, P).T] + [
        arr(g)[0].reshape(KC, P).T for g in (g_pre_mix, g_post_mix, g_pre_ffn, g_post_ffn)]
    prm = np.concatenate(
        [cols(c.T).reshape(P, -1)] + per_feature + [
            arr(pool_scale)[0].reshape(8, P).T,
            np.broadcast_to(arr(b_f)[0][None, :], (P, HEADS)),
            cols(w_i[:, 3 * att_w:3 * att_w + HEADS]).reshape(P, -1)], axis=1)
    w_main = np.concatenate([w_i[:, :3 * att_w], w_i[:, 3 * att_w + HEADS:]], axis=1)
    pages = arr(page_table).astype(np.int32).reshape(-1)
    arrays = {
        "x_t": arr(cols(x.T)),
        "cst_in": constants(),
        "prm_in": arr(prm),
        "w_ada": arr(arr(w_ada)[0].reshape(KC, P, 6, D).transpose(2, 0, 1, 3).reshape(6 * KC, P, D)),
        "w_in": tiles(w_main),
        "w_out": tiles(arr(w_out)[0]),
        "w_pq": tiles(arr(w_peer_q)[0]),
        "cache_k": arr(arr(cache_k)[0].transpose(0, 3, 2, 1).reshape(POOL_PAGES * P, HEADS * P)),
        "cache_v": arr(cache_v)[0].reshape(POOL_PAGES * P, HEADS * HD),
        "cache_f": arr(arr(cache_logf)[0].transpose(0, 2, 1).reshape(POOL_PAGES, HEADS * P)),
        "pages_bc": arr(np.broadcast_to(pages.reshape(2, 4, PAGES).transpose(0, 2, 1).reshape(1, -1), (P, 64))),
        "pages_col": arr(pages[:, None]),
        "hist_in": arr(arr(state_pool)[0].reshape(NB, HIST, 8, P).transpose(3, 2, 0, 1)),
        "sk_in": arr(arr(peer_subkeys)[0].reshape(KC, SK, P).transpose(2, 0, 1)),
        "wpool_in": arr(arr(w_pool)[0].reshape(4, 2, P, 256).transpose(2, 0, 1, 3)),
        "peer_u": arr(peer_u)[0],
        "peer_v": arr(peer_v)[0],
    }
    outs = {"y_out": (P, KC, NT), "kv_out": (P, 16, NT), "lf_out": (NT, HEADS),
            "pool_out": (P, 8 * HIST * (1 + NB))}
    nc = bacc.Bacc("TRN2", target_bir_lowering=False, num_devices=1)
    args = {n: nc.dram_tensor(n, a.shape, mybir.dt.from_np(a.dtype), kind="ExternalInput").ap()
            for n, a in arrays.items()}
    args.update({n: nc.dram_tensor(n, s, F32, kind="ExternalOutput").ap() for n, s in outs.items()})
    build(nc, **args)
    r = run_bass_kernel_spmd(nc, [arrays], core_ids=[0]).results[0]
    y = r["y_out"].transpose(2, 1, 0).reshape(NT, D)
    kv = r["kv_out"].transpose(2, 1, 0)
    k, v = kv[:, 0:HEADS], kv[:, HEADS:]
    pool = r["pool_out"]
    pool_p = pool[:, :8 * HIST].reshape(P, 8, HIST).transpose(2, 1, 0).reshape(1, 1, HIST, 1024)
    pool_s = pool[:, 8 * HIST:].reshape(P, 8, NB, HIST).transpose(2, 3, 1, 0).reshape(1, NB, HIST, 1024)
    lf = r["lf_out"]
    return (y[:NP_TOK].reshape(1, NP_TOK, D), y[NP_TOK:].reshape(NB, NQ, D),
            k[:NP_TOK].reshape(1, 1, NP_TOK, HEADS, HD), v[:NP_TOK].reshape(1, 1, NP_TOK, HEADS, HD),
            lf[:NP_TOK].reshape(1, 1, NP_TOK, HEADS), pool_p,
            k[NP_TOK:].reshape(1, NB, NQ, HEADS, HD), v[NP_TOK:].reshape(1, NB, NQ, HEADS, HD),
            lf[NP_TOK:].reshape(1, NB, NQ, HEADS), pool_s)
```
